# Optimizing a Trainium2 kernel written in Bass

```python
import jax, jax.numpy as jnp
from jax import lax
import numpy as np

D_MODEL = 1024
BATCH = 1
SEQ = 512
DEPTH = 1

MEM_LEN = 256
MLA_HEADS = 8
MLA_NOPE_DIM = 64
MLA_ROPE_DIM = 32
MLA_V_DIM = 64
MLA_Q_LORA = 384
MLA_KV_LORA = 256
FOX_HEADS = 8
FOX_HEAD_DIM = 64
MEM_HEADS = 4
MEM_HEAD_DIM = 128
N_BRANCHES = 3
D_FF = 2816
BLOCK_Q = 128
ROPE_THETA = 10000.0
LN_EPS = 1e-5
RMS_EPS = 1e-6
DEEPNORM_ALPHA = (2.0 * DEPTH) ** 0.25
DEEPNORM_BETA = (8.0 * DEPTH) ** -0.25
MLA_W = MLA_HEADS * MLA_V_DIM
FOX_W = FOX_HEADS * FOX_HEAD_DIM
MEM_W = MEM_HEADS * MEM_HEAD_DIM
IN_COLS = MLA_Q_LORA + MLA_KV_LORA + MLA_ROPE_DIM + 3 * FOX_W + FOX_HEADS + MEM_W + N_BRANCHES * D_MODEL

kernel_name = "hybrid_mla_fox_memxattn_macaron_deepnorm"

def layer_norm(x, g, b):
    xf = x.astype(jnp.float32)
    mu = jnp.mean(xf, axis=-1, keepdims=True)
    var = jnp.mean(jnp.square(xf - mu), axis=-1, keepdims=True)
    y = (xf - mu) * lax.rsqrt(var + LN_EPS)
    return (y * g.astype(jnp.float32) + b.astype(jnp.float32)).astype(x.dtype)

def rms_norm(x, g):
    xf = x.astype(jnp.float32)
    y = xf * lax.rsqrt(jnp.mean(jnp.square(xf), axis=-1, keepdims=True) + RMS_EPS)
    return (y * g.astype(jnp.float32)).astype(x.dtype)

def apply_rope(x, positions):
    half = x.shape[-1] // 2
    inv_freq = ROPE_THETA ** (-jnp.arange(half, dtype=jnp.float32) / half)
    ang = positions.astype(jnp.float32)[..., None] * inv_freq
    cos = jnp.cos(ang)[:, :, None, :].astype(x.dtype)
    sin = jnp.sin(ang)[:, :, None, :].astype(x.dtype)
    x1, x2 = x[..., :half], x[..., half:]
    return jnp.concatenate([x1 * cos - x2 * sin, x2 * cos + x1 * sin], axis=-1)

def swiglu_ffn(x, w_in, w_down):
    a, b = jnp.split(x @ w_in, 2, axis=-1)
    return (jax.nn.silu(a) * b) @ w_down

def causal_block_attention(q, k, v, scale, fcum=None):
    b, h, s, dk = q.shape
    dv = v.shape[-1]
    nb = s // BLOCK_Q
    q_blocks = q.reshape(b, h, nb, BLOCK_Q, dk).transpose(2, 0, 1, 3, 4)
    key_pos = jnp.arange(s)
    xs = (jnp.arange(nb), q_blocks)
    if fcum is not None:
        xs = xs + (fcum.reshape(b, h, nb, BLOCK_Q).transpose(2, 0, 1, 3),)

    def attend_block(blk):
        i, q_i = blk[0], blk[1]
        logits = jnp.einsum('bhqd,bhkd->bhqk', q_i, k, preferred_element_type=jnp.float32) * scale
        if fcum is not None:
            logits = logits + (blk[2][..., :, None] - fcum[..., None, :])
        q_pos = i * BLOCK_Q + jnp.arange(BLOCK_Q)
        causal = key_pos[None, :] <= q_pos[:, None]
        logits = jnp.where(causal, logits, -jnp.inf)
        p = jax.nn.softmax(logits, axis=-1)
        return jnp.einsum('bhqk,bhkd->bhqd', p.astype(v.dtype), v)

    out = lax.map(attend_block, xs)
    return out.transpose(1, 2, 0, 3, 4).reshape(b, h, s, dv)

def hybrid_mixer(h, mem, positions, w_in, b_gate, mla_q_norm, mla_w_uq, mla_kv_norm, mla_w_ukv,
                 fox_b_f, mem_w_kv, w_br_mla, w_br_fox, w_br_mem, w_out):
    B, S, _ = h.shape
    sizes = (MLA_Q_LORA, MLA_KV_LORA, MLA_ROPE_DIM, FOX_W, FOX_W, FOX_W, FOX_HEADS, MEM_W)
    splits = np.cumsum(sizes).tolist()
    proj = h @ w_in
    c_q, c_kv, k_pe, fq, fk, fv, f_logit, mq, gates = jnp.split(proj, splits, axis=-1)

    q = (rms_norm(c_q, mla_q_norm) @ mla_w_uq).reshape(B, S, MLA_HEADS, MLA_NOPE_DIM + MLA_ROPE_DIM)
    q = jnp.concatenate([q[..., :MLA_NOPE_DIM], apply_rope(q[..., MLA_NOPE_DIM:], positions)], axis=-1)
    kv = (rms_norm(c_kv, mla_kv_norm) @ mla_w_ukv).reshape(B, S, MLA_HEADS, MLA_NOPE_DIM + MLA_V_DIM)
    k_nope, v_mla = kv[..., :MLA_NOPE_DIM], kv[..., MLA_NOPE_DIM:]
    k_rope = apply_rope(k_pe[:, :, None, :], positions)
    k = jnp.concatenate([k_nope, jnp.broadcast_to(k_rope, (B, S, MLA_HEADS, MLA_ROPE_DIM))], axis=-1)
    o_mla = causal_block_attention(q.transpose(0, 2, 1, 3), k.transpose(0, 2, 1, 3),
                                   v_mla.transpose(0, 2, 1, 3),
                                   (MLA_NOPE_DIM + MLA_ROPE_DIM) ** -0.5)
    o_mla = o_mla.transpose(0, 2, 1, 3).reshape(B, S, MLA_W)

    log_f = jax.nn.log_sigmoid((f_logit + fox_b_f).astype(jnp.float32))
    fcum = jnp.cumsum(log_f, axis=1).transpose(0, 2, 1)
    to_heads = lambda t: t.reshape(B, S, FOX_HEADS, FOX_HEAD_DIM).transpose(0, 2, 1, 3)
    o_fox = causal_block_attention(to_heads(fq), to_heads(fk), to_heads(fv),
                                   FOX_HEAD_DIM ** -0.5, fcum)
    o_fox = o_fox.transpose(0, 2, 1, 3).reshape(B, S, FOX_W)

    mk, mv = jnp.split(mem @ mem_w_kv, 2, axis=-1)
    mk = mk.reshape(B, MEM_LEN, MEM_HEADS, MEM_HEAD_DIM)
    mv = mv.reshape(B, MEM_LEN, MEM_HEADS, MEM_HEAD_DIM)
    mqh = mq.reshape(B, S, MEM_HEADS, MEM_HEAD_DIM)
    m_logits = jnp.einsum('bshd,bmhd->bhsm', mqh, mk, preferred_element_type=jnp.float32) * MEM_HEAD_DIM ** -0.5
    m_p = jax.nn.softmax(m_logits, axis=-1).astype(mv.dtype)
    o_mem = jnp.einsum('bhsm,bmhd->bshd', m_p, mv).reshape(B, S, MEM_W)

    g = jax.nn.sigmoid(gates + b_gate).reshape(B, S, N_BRANCHES, D_MODEL)
    merged = (g[:, :, 0] * (o_mla @ w_br_mla)
              + g[:, :, 1] * (o_fox @ w_br_fox)
              + g[:, :, 2] * (o_mem @ w_br_mem))
    return merged @ w_out

def setup_inputs(seed: int = 0) -> dict:
    key = jax.random.key(seed)
    ks = jax.random.split(key, 32)
    L = DEPTH

    def nrm(k, shape, scale):
        return jax.random.normal(k, shape, jnp.float32) * scale

    x = nrm(ks[0], (BATCH, SEQ, D_MODEL), 1.0)
    mem = nrm(ks[1], (BATCH, MEM_LEN, D_MODEL), 1.0)
    start = jax.random.randint(ks[2], (BATCH, 1), 0, 1024, dtype=jnp.int32)
    positions = (start + jnp.arange(SEQ, dtype=jnp.int32)[None, :]).astype(jnp.int32)
    return {
        "x": x,
        "mem": mem,
        "positions": positions,
        "ln1_g": 1.0 + nrm(ks[3], (L, D_MODEL), 0.02),
        "ln1_b": nrm(ks[4], (L, D_MODEL), 0.02),
        "ffn1_w_in": nrm(ks[5], (L, D_MODEL, 2 * D_FF), D_MODEL ** -0.5),
        "ffn1_w_down": nrm(ks[6], (L, D_FF, D_MODEL), D_FF ** -0.5 * DEEPNORM_BETA),
        "w_in": nrm(ks[7], (L, D_MODEL, IN_COLS), D_MODEL ** -0.5),
        "b_gate": nrm(ks[8], (L, N_BRANCHES * D_MODEL), 0.01),
        "mla_q_norm": 1.0 + nrm(ks[9], (L, MLA_Q_LORA), 0.02),
        "mla_w_uq": nrm(ks[10], (L, MLA_Q_LORA, MLA_HEADS * (MLA_NOPE_DIM + MLA_ROPE_DIM)), MLA_Q_LORA ** -0.5),
        "mla_kv_norm": 1.0 + nrm(ks[11], (L, MLA_KV_LORA), 0.02),
        "mla_w_ukv": nrm(ks[12], (L, MLA_KV_LORA, MLA_HEADS * (MLA_NOPE_DIM + MLA_V_DIM)), MLA_KV_LORA ** -0.5),
        "fox_b_f": 2.0 + nrm(ks[13], (L, FOX_HEADS), 0.5),
        "mem_w_kv": nrm(ks[14], (L, D_MODEL, 2 * MEM_W), D_MODEL ** -0.5),
        "w_br_mla": nrm(ks[15], (L, MLA_W, D_MODEL), MLA_W ** -0.5),
        "w_br_fox": nrm(ks[16], (L, FOX_W, D_MODEL), FOX_W ** -0.5),
        "w_br_mem": nrm(ks[17], (L, MEM_W, D_MODEL), MEM_W ** -0.5),
        "w_out": nrm(ks[18], (L, D_MODEL, D_MODEL), D_MODEL ** -0.5 * DEEPNORM_BETA),
        "ln2_g": 1.0 + nrm(ks[19], (L, D_MODEL), 0.02),
        "ln2_b": nrm(ks[20], (L, D_MODEL), 0.02),
        "ffn2_w_in": nrm(ks[21], (L, D_MODEL, 2 * D_FF), D_MODEL ** -0.5),
        "ffn2_w_down": nrm(ks[22], (L, D_FF, D_MODEL), D_FF ** -0.5 * DEEPNORM_BETA),
        "ln3_g": 1.0 + nrm(ks[23], (L, D_MODEL), 0.02),
        "ln3_b": nrm(ks[24], (L, D_MODEL), 0.02),
    }

def reference(x, mem, positions, ln1_g, ln1_b, ffn1_w_in, ffn1_w_down, w_in, b_gate,
              mla_q_norm, mla_w_uq, mla_kv_norm, mla_w_ukv, fox_b_f, mem_w_kv,
              w_br_mla, w_br_fox, w_br_mem, w_out, ln2_g, ln2_b,
              ffn2_w_in, ffn2_w_down, ln3_g, ln3_b):
    for l in range(DEPTH):
        x = layer_norm(DEEPNORM_ALPHA * x + 0.5 * swiglu_ffn(x, ffn1_w_in[l], ffn1_w_down[l]),
                       ln1_g[l], ln1_b[l])
        mix = hybrid_mixer(x, mem, positions, w_in[l], b_gate[l], mla_q_norm[l], mla_w_uq[l],
                           mla_kv_norm[l], mla_w_ukv[l], fox_b_f[l], mem_w_kv[l],
                           w_br_mla[l], w_br_fox[l], w_br_mem[l], w_out[l])
        x = layer_norm(DEEPNORM_ALPHA * x + mix, ln2_g[l], ln2_b[l])
        x = layer_norm(DEEPNORM_ALPHA * x + 0.5 * swiglu_ffn(x, ffn2_w_in[l], ffn2_w_down[l]),
                       ln3_g[l], ln3_b[l])
    return x


_drawn_inputs = setup_inputs


def setup_inputs(seed=0):
    import zlib

    import numpy as np

    out = dict(_drawn_inputs(seed))
    spreads = {}
    factors = {'ln1_g': 2.942,
     'b_gate': 34.779,
     'mla_q_norm': 8.0,
     'mla_kv_norm': 8.0,
     'fox_b_f': 3.046,
     'ln2_g': 2.806,
     'ln2_b': 2.919,
     'ln3_g': 8.443,
     'ln3_b': 8.278}
    for name, (base, spread) in spreads.items():
        noise = np.random.default_rng([zlib.crc32(name.encode()), seed]).standard_normal(out[name].shape)
        drawn = base * np.exp(spread * noise) if base else spread * noise
        out[name] = __import__('jax').numpy.asarray(drawn.astype(out[name].dtype))
    for name, factor in factors.items():
        out[name] = (out[name] * factor).astype(out[name].dtype)
    return out
```

```python
from contextlib import ExitStack

import numpy as np

import concourse.bass as bass
from concourse import mybir

F32 = mybir.dt.float32
F32R = mybir.dt.float32r
I32 = mybir.dt.int32
ALU = mybir.AluOpType
ACT = mybir.ActivationFunctionType
AX = mybir.AxisListType

P = 128
S, D, M = 512, 1024, 256
KD = D // P
NT = S // P
FF = 2816
NF = FF // P
HEADS, MEM_HEADS = 8, 4
NOPE, ROPE, DV = 64, 32, 64
QK_MLA = NOPE + ROPE
QL, KVL = 384, 256
KQ, KKV = QL // P, KVL // P
FOX_W = 512
ALPHA = 2.0 ** 0.25
LN_EPS, RMS_EPS = 1e-5, 1e-6
NEG = -1e30

C_CQ = 0
C_KPE = QL + KVL
C_FQ = C_KPE + ROPE
C_FK = C_FQ + FOX_W
C_FV = C_FK + FOX_W
C_FLOG = C_FV + FOX_W
C_MQ = C_FLOG + HEADS
C_GATE = C_MQ + 512

RING = 4
B_UP1 = 0
B_DN1 = B_UP1 + 2 * NF
B_MK = B_DN1 + NF
B_MV = B_MK + 4
B_C = B_MV + 4
B_KF = B_C + KQ + KKV
B_MQ = B_KF + 1
B_FQK = B_MQ + 4
B_UQ = B_FQK + 8
B_FV = B_UQ + KQ
B_UKV = B_FV + 4
B_MG = B_UKV + KKV
B_OUT = B_MG + 3 * 16
B_UP2 = B_OUT + KD
B_DN2 = B_UP2 + 2 * NF
B_END = B_DN2 + NF

E_MK, E_MV, E_C, E_KF, E_MQ, E_FQK, E_UQ, E_K, E_V, E_FV, E_ALL = 0, 4, 6, 11, 13, 17, 25, 33, 41, 45, 49

J_MEM, J_MLA, J_FOX, J_END = 0, 4, 12, 20
PT_OFF = {False: (0, 512), True: (0, 512, 896, 1152)}


def pt_first(j):
    return 2 * j if isinstance(j, int) and j <= J_MLA else j * 4 - 2 * J_MLA


def shape_constants():
    c = np.zeros((P, 8), np.float32)
    half = ROPE // 2
    inv = (10000.0 ** (-np.arange(half, dtype=np.float64) / half)).astype(np.float32)
    c[64:64 + half, 0] = inv
    c[64 + half:96, 0] = inv
    c[64:64 + half, 1] = -1.0
    c[64 + half:96, 1] = 1.0
    c[:, 2] = LN_EPS
    c[:, 3] = RMS_EPS
    c[:, 4] = np.pi / 2
    return c


def layer_program(nc, x, mem, positions, ln1_g, ln1_b, ffn1_w_in, ffn1_w_down, w_in, b_gate,
                  mla_q_norm, mla_w_uq, mla_kv_norm, mla_w_ukv, fox_b_f, mem_w_kv, w_br_mla, w_br_fox,
                  w_br_mem, w_out, ln2_g, ln2_b, ffn2_w_in, ffn2_w_down, ln3_g, ln3_b, consts, out):
    with ExitStack() as ctx:
        base = (nc.sbuf_base + 31) // 32 * 32
        ctx.enter_context(nc.sbuf_tensor("arena", [P, (nc.sbuf_usable_end - base - 64) // 4], F32))
        limit = nc.sbuf_usable_end

        def at(name, shape, dt, offset):
            size = 4
            for s in shape[1:]:
                size *= s
            assert base + offset + size <= limit, (name, base + offset + size, limit)
            return nc.alloc_sbuf_tensor_at(name, shape, dt, offset=base + offset)

        K1 = 1024
        whi = at("whi", [P, RING, 1024], F32R, 0)
        wlo = at("wlo", [P, RING, 1024], F32R, 16 * K1)
        raw = at("raw", [P, RING, 1024], F32, 32 * K1)
        xhi = at("xhi", [P, KD, S], F32R, 48 * K1)
        xlo = at("xlo", [P, KD, S], F32R, 64 * K1)
        X = at("X", [P, NT, D], F32, 80 * K1)
        merged = at("merged", [P, KD, S], F32, 80 * K1)
        A = 96 * K1
        h = at("h", [P, NF, S], F32, A)
        hhi = at("hhi", [P, RING, S], F32R, A + 44 * K1)
        hlo = at("hlo", [P, RING, S], F32R, A + 52 * K1)
        Q = at("Q", [P, HEADS, S], F32, A)
        craw = at("craw", [P, KQ + KKV, S], F32, A)
        csq = at("csq", [P, 3, S], F32, A + 10 * K1)
        Kt = at("Kt", [P, HEADS, S], F32, A + 16 * K1)
        mk = at("mk", [P, MEM_HEADS, M], F32, A + 16 * K1)
        cqhi = at("cqhi", [P, KQ, S], F32R, A + 20 * K1)
        cqlo = at("cqlo", [P, KQ, S], F32R, A + 26 * K1)
        V = at("V", [P, NT, 512], F32, A + 32 * K1)
        mv = at("mv", [P, 2, 512], F32, A + 32 * K1)
        rms = at("rms", [P, 2, S], F32, A + 36 * K1)
        FQK = at("FQK", [P, 8, S], F32, A + 40 * K1)
        FV = at("FV", [P, NT, 512], F32, A + 56 * K1)
        ckhi = at("ckhi", [P, KKV, S], F32R, A + 56 * K1)
        cklo = at("cklo", [P, KKV, S], F32R, A + 60 * K1)
        ohi = at("ohi", [P, 4, S], F32R, A + 64 * K1)
        olo = at("olo", [P, 4, S], F32R, A + 72 * K1)
        MQ = at("MQ", [P, MEM_HEADS, S], F32, A + 72 * K1)
        mThi = at("mThi", [P, KD, M], F32R, A + 64 * K1)
        mTlo = at("mTlo", [P, KD, M], F32R, A + 72 * K1)
        PB = A + 80 * K1
        prob = at("prob", [P, 1280], F32, PB)
        stmp = at("stmp", [P, 2, S], F32, PB)
        rtmp = at("rtmp", [P, S], F32, PB)
        T = PB + 5 * K1
        pthi = at("pthi", [P, 1280], F32R, T)
        ptlo = at("ptlo", [P, 1280], F32R, T + 5 * K1)
        res = at("res", [P, 2, D], F32, T)
        tabs = at("tabs", [P, 5, S], F32, T)
        G = T + 10 * K1
        qh = at("qh", [P, S], F32R, G)
        ql = at("ql", [P, S], F32R, G + 2 * K1)
        kh = at("kh", [P, S], F32R, G + 4 * K1)
        kl = at("kl", [P, S], F32R, G + 6 * K1)
        vh = at("vh", [P, 256], F32R, G + 8 * K1)
        vl = at("vl", [P, 256], F32R, G + 9 * K1)
        lng = at("lng", [P, D], F32, G)
        lnb = at("lnb", [P, D], F32, G + 4 * K1)
        Z = G + 10 * K1
        ident = at("ident", [P, P], F32, Z)
        identR = at("identR", [P, P], F32R, Z + 512)
        maskR = at("maskR", [P, P], F32R, Z + 1024)
        ones = at("ones", [P, P], F32, PB + 4 * K1)
        kf = at("kf", [P, S], F32, Z + 1536)
        sig = at("sig", [P, S], F32, Z + 1536)
        tmp = at("tmp", [P, S], F32, Z + 3584)
        pos = at("pos", [P, S], I32, Z + 3584)
        maskF = at("maskF", [P, P], F32, A)
        SM = Z + 5632
        cst = at("cst", [P, 8], F32, SM)
        bg = at("bg", [P, 24], F32, SM + 32)
        gq = at("gq", [P, KQ + KKV], F32, SM + 128)
        bf = at("bf", [P, 1], F32, SM + 160)
        stats = at("stats", [P, 2, 6], F32, SM + 192)
        mvar = at("mvar", [P, 2], F32, SM + 256)
        rstd = at("rstd", [P, 2], F32, SM + 288)
        nmax = at("nmax", [P, 4], F32, SM + 320)
        rsum = at("rsum", [P, 4], F32, SM + 352)
        rinv = at("rinv", [P, 4], F32, SM + 384)

        ps = ctx.enter_context(nc.psum_tensor("ps", [P, 8, 512], F32))
        spill = nc.dram_tensor("spill_x1", (S, D), F32, kind="Internal").ap()

        def sem(name):
            return ctx.enter_context(nc.semaphore(name))

        w_raw = [sem(f"w_raw{i}") for i in range(RING)]
        w_hi, w_lo = sem("w_hi"), sem("w_lo")
        w_used = sem("w_used")
        c_in, k_in = sem("c_in"), sem("k_in")
        x_in = [sem(f"x_in{t}") for t in range(NT)]
        m_in = sem("m_in")
        g_in = sem("g_in")
        sp_out = sem("sp_out")
        f_rows = sem("f_rows")
        y_out = sem("y_out")
        pool_c = sem("pool_c")
        act_c = sem("act_c")
        t_done = sem("t_done")
        t_hi, t_lo = sem("t_hi"), sem("t_lo")
        sl_done, h_done = sem("sl_done"), sem("h_done")
        hs_hi, hs_lo = sem("hs_hi"), sem("hs_lo")
        y_done = sem("y_done")
        lnc = sem("lnc")
        ln_sd = sem("ln_sd")
        ev = sem("ev")
        pj = sem("pj")
        sq_done, ss_done = sem("sq_done"), sem("ss_done")
        rm_sd, rm_r = sem("rm_sd"), sem("rm_r")
        cn, cn_hi, cn_lo = sem("cn"), sem("cn_hi"), sem("cn_lo")
        tb_v, tb_s = sem("tb_v"), sem("tb_s")
        fg_v, fg_s = sem("fg_v"), sem("fg_s")
        rp = sem("rp")
        kr = sem("kr")
        st_hi, st_lo = sem("st_hi"), sem("st_lo")
        sv_hi, sv_lo = sem("sv_hi"), sem("sv_lo")
        s_done = sem("s_done")
        mx_done, ex_done = sem("mx_done"), sem("ex_done")
        rc_done, pn_done = sem("rc_done"), sem("pn_done")
        pt_done = sem("pt_done")
        ph_done, pl_done = sem("ph_done"), sem("pl_done")
        pv_done, o_done = sem("pv_done"), sem("o_done")
        os_hi, os_lo = sem("os_hi"), sem("os_lo")
        sg_done, mt_done, mg_done = sem("sg_done"), sem("mt_done"), sem("mg_done")
        ms_hi, ms_lo = sem("ms_hi"), sem("ms_lo")

        def wait(eng, s, v):
            if not isinstance(v, int) or v > 0:
                eng.wait_ge(s, v)

        def apart(eng, *held):
            if any(not isinstance(v, int) for v in held):
                eng.wait_ge(c_in, 16)

        def row(t, i):
            if isinstance(i, int):
                return t[:, i, :]
            return t[:, bass.ds(i, 1), :].rearrange("p a n -> p (a n)")

        def rows(t, lo, hi, i):
            if isinstance(i, int):
                return t[lo:hi, i, :]
            return t[lo:hi, bass.ds(i, 1), :].rearrange("p a n -> p (a n)")

        def wcols(n):
            if n == B_KF:
                return lambda t: t[:, n % RING, :].rearrange("p (k m) -> p k m", m=P)[:, :, 64:104]
            if B_UQ <= n < B_UQ + KQ:
                return lambda t: t[:, n % RING, 0:768]
            if B_MG <= n < B_OUT and (n - B_MG) % 2:
                return lambda t: t[:, n % RING, 0:512]
            return lambda t: t[:, n % RING, :]

        def block(base_n, i=0, per=RING):
            if isinstance(i, int):
                n = base_n + per * i
                return n, n, n // RING
            return i * per + base_n, base_n, i * (per // RING) + base_n // RING

        blk = ctx.enter_context(nc.Block())

        @blk.sync
        def _(sp):
            def load(b, src):
                n, like, lap = b
                apart(sp, n)
                wait(sp, w_lo, n - RING + 1)
                dst = wcols(like)(raw)
                if len(src.shape) == 3 and len(dst.shape) == 2:
                    dst = dst.rearrange("p (k m) -> p k m", k=src.shape[1])
                sp.dma_start(dst, src).then_inc(w_raw[like % RING], 16)

            def kcols(w, col, width=P):
                wv = w.rearrange("(k p) n -> p k n", p=P)
                return wv[:, :, bass.ds(col, width)] if not isinstance(col, int) else wv[:, :, col:col + width]

            def up(b0, w):
                def body(i):
                    for j in range(4):
                        f_off = (j // 2) * P + (j % 2) * FF
                        load(block(b0 + j, i), kcols(w, i * (2 * P) + f_off))
                return body

            def down_rows(w, r):
                if isinstance(r, int):
                    return w[r:r + P, :]
                return w[bass.ds(r, P), :]

            def down(b0, w):
                def body(i):
                    for j in range(4):
                        load(block(b0 + j, i), down_rows(w, i * (4 * P) + j * P))
                return body

            def ln_params(g, b):
                sp.dma_start(lng[:], g.partition_broadcast(P)).then_inc(g_in, 16)
                sp.dma_start(lnb[:], b.partition_broadcast(P)).then_inc(g_in, 16)

            xv = x.rearrange("(t p) d -> t p d", p=P)
            sp.dma_start(cst[:], consts).then_inc(c_in, 16)
            for t in range(NT):
                sp.dma_start(X[:, t, :], xv[t]).then_inc(x_in[t], 16)
            first = up(B_UP1, ffn1_w_in)
            first(0)
            memv = mem.rearrange("(t p) d -> p t d", p=P)
            sp.dma_start(res[:, :, :], memv).then_inc(m_in, 16)
            with nc.allow_non_contiguous_dma(reason="small per-feature parameters"):
                sp.dma_start(bg[:], b_gate.rearrange("(c p) -> p c", p=P)).then_inc(k_in, 16)
                sp.dma_start(gq[:, 0:KQ], mla_q_norm.rearrange("(c p) -> p c", p=P)).then_inc(k_in, 16)
                sp.dma_start(gq[:, KQ:KQ + KKV], mla_kv_norm.rearrange("(c p) -> p c", p=P)).then_inc(k_in, 16)
                sp.dma_start(bf[0:HEADS, :], fox_b_f.rearrange("(p a) -> p a", a=1)).then_inc(k_in, 16)
            sp.dma_start(pos[64:96, :], positions.partition_broadcast(ROPE)).then_inc(k_in, 16)
            ln_params(ln1_g, ln1_b)
            with sp.Fori(1, NF // 2) as i:
                first(i)
            dn1 = down(B_DN1, ffn1_w_down)
            with sp.Fori(0, NF // 4) as i:
                dn1(i)
            for f in range(NF // 4 * 4, NF):
                load(block(B_DN1 + f), down_rows(ffn1_w_down, f * P))
            for j in range(4):
                load(block(B_MK + j), kcols(mem_w_kv, j * P))
            mkv = mem_w_kv.rearrange("(k p) n -> p k n", p=P)
            for j in range(4):
                load(block(B_MV + j), mkv[:, 2 * j:2 * j + 2, 512:1024])
            for t in range(NT):
                wait(sp, lnc, 6 * (t + 1))
                sp.dma_start(spill[t * P:(t + 1) * P, :], X[:, t, :]).then_inc(sp_out, 16)
                if t < 3:
                    load(block(B_C + t), kcols(w_in, C_CQ + t * P))
            for j in range(3, KQ + KKV):
                load(block(B_C + j), kcols(w_in, C_CQ + j * P))
            n, like, lap = block(B_KF)
            wait(sp, w_lo, n - RING + 1)
            kfv = raw[:, n % RING, :].rearrange("p (k m) -> p k m", m=P)
            sp.dma_start(kfv[:, :, 64:96], kcols(w_in, C_KPE, ROPE)).then_inc(w_raw[n % RING], 16)
            with nc.allow_non_contiguous_dma(reason="eight columns"):
                sp.dma_start(kfv[:, :, 96:104], kcols(w_in, C_FLOG, HEADS)).then_inc(k_in, 16)
            for j in range(4):
                load(block(B_MQ + j), kcols(w_in, C_MQ + j * P))
            for j in range(8):
                load(block(B_FQK + j), kcols(w_in, C_FQ + j * P))
            for k in range(KQ):
                load(block(B_UQ + k), mla_w_uq[k * P:(k + 1) * P, :])
            winv = w_in.rearrange("(k p) n -> p k n", p=P)
            for j in range(4):
                load(block(B_FV + j), winv[:, 2 * j:2 * j + 2, C_FV:C_FV + 512])
            for k in range(KKV):
                load(block(B_UKV + k), mla_w_ukv[k * P:(k + 1) * P, :])
            wait(sp, fg_v, 8)
            for part, (r0, s0) in enumerate(((64, 1), (65, 2), (98, 3), (99, 4))):
                sp.dma_start(Kt[r0:r0 + 1, :, :], tabs[0:HEADS, s0, :]).then_inc(f_rows, 16)
            for b, (w_br, gate) in enumerate(((w_br_mem, 2), (w_br_mla, 0), (w_br_fox, 1))):
                for d in range(KD):
                    load(block(B_MG + 16 * b + 2 * d), kcols(w_in, C_GATE + gate * D + d * P))
                    load(block(B_MG + 16 * b + 2 * d + 1), kcols(w_br, d * P))
            for k in range(4):
                load(block(B_OUT + k), w_out[k * P:(k + 1) * P, :])
            wait(sp, ms_lo, KD)
            wait(sp, sp_out, 16 * NT)
            for t in range(NT):
                sp.dma_start(X[:, t, :], spill[t * P:(t + 1) * P, :]).then_inc(x_in[t], 16)
            ln_params(ln2_g, ln2_b)
            for k in range(4, KD):
                load(block(B_OUT + k), w_out[k * P:(k + 1) * P, :])
            second = up(B_UP2, ffn2_w_in)
            for i in range(2):
                second(i)
            wait(sp, lnc, 6 * 2 * NT)
            ln_params(ln3_g, ln3_b)
            with sp.Fori(2, NF // 2) as i:
                second(i)
            dn2 = down(B_DN2, ffn2_w_down)
            with sp.Fori(0, NF // 4) as i:
                dn2(i)
            for f in range(NF // 4 * 4, NF):
                load(block(B_DN2 + f), down_rows(ffn2_w_down, f * P))
            for t in range(NT):
                wait(sp, lnc, 6 * (2 * NT + t + 1))
                sp.dma_start(out[t * P:(t + 1) * P, :], X[:, t, :]).then_inc(y_out, 16)
            sp.wait_ge(y_out, 16 * NT)

        @blk.gpsimd
        def _(pool):
            nc.gpsimd.memset(ident[:], 0.0).then_inc(pool_c, 1)
            nc.gpsimd.memset(maskF[:], 0.0).then_inc(pool_c, 1)
            nc.gpsimd.memset(ones[:], 1.0).then_inc(pool_c, 1)
            pool.wait_ge(pool_c, 3)
            nc.gpsimd.affine_select(out=ident[:], in_=ident[:], compare_op=ALU.not_equal, fill=1.0, base=0,
                                    pattern=[[-1, P]], channel_multiplier=1).then_inc(pool_c, 1)
            nc.gpsimd.affine_select(out=maskF[:], in_=maskF[:], compare_op=ALU.is_ge, fill=NEG, base=0,
                                    pattern=[[-1, P]], channel_multiplier=1).then_inc(pool_c, 1)

            def low(b):
                n, like, lap = b
                v = wcols(like)
                pool.wait_ge(w_hi, n + 1)
                nc.gpsimd.tensor_tensor(v(wlo), v(raw), v(whi).bitcast(F32), ALU.subtract).then_inc(w_lo, 1)

            for n in range(RING):
                low(block(n))
            with pool.Fori(1, B_MV // RING + 1) as i:
                for j in range(RING):
                    low(block(j, i))
            for n in range((B_MV // RING + 1) * RING, B_MG + 3):
                low(block(n))
            with pool.Fori(0, 11) as i:
                for j in range(RING):
                    low(block(B_MG + 3 + j, i))
            for n in range(B_MG + 47, B_OUT + 3):
                low(block(n))
            with pool.Fori(0, (B_END - B_OUT - 3) // RING) as i:
                for j in range(RING):
                    low(block(B_OUT + 3 + j, i))
            for n in range(B_OUT + 3 + (B_END - B_OUT - 3) // RING * RING, B_END):
                low(block(n))

        @blk.scalar
        def _(act):
            def high(b):
                n, like, lap = b
                v = wcols(like)
                act.wait_ge(w_raw[like % RING], lap * 16 + 16)
                if like == B_KF:
                    act.wait_ge(k_in, 16 * 6)
                wait(act, w_used, n - RING + 1)
                nc.scalar.activation(v(whi), v(raw), ACT.Copy).then_inc(w_hi, 1)

            def turned_hi(g, t):
                act.wait_ge(t_done, g + 1)
                nc.scalar.activation(xhi[:, :, t * P:(t + 1) * P],
                                     ps[:, 2 * t:2 * t + 2, :].rearrange("p a (k m) -> p (a k) m", m=P),
                                     ACT.Copy).then_inc(t_hi, 1)

            def sd(q):
                act.wait_ge(lnc, 6 * q + 3)
                nc.scalar.activation(rstd[:, q % 2:q % 2 + 1], mvar[:, 1:2], ACT.Sqrt,
                                     bias=cst[:, 2:3]).then_inc(ln_sd, 1)

            def up(b0, h0):
                def body(i):
                    for p in range(2):
                        na, la, _ = block(b0 + 2 * p, i)
                        f = i * 2 + p
                        act.wait_ge(w_used, na + 1)
                        wait(act, h_done, f + h0 - 1)
                        nc.scalar.activation(stmp[:, p, :], ps[:, 2 * p, :], ACT.Silu).then_inc(sl_done, 1)
                        high(block(b0 + 2 * p + 4, i))
                        high(block(b0 + 2 * p + 5, i))
                return body

            def hidden_hi(f, slot, h0, after=None):
                apart(act, f)
                act.wait_ge(h_done, f + h0 + 1)
                if after is not None:
                    act.wait_ge(w_used, after)
                nc.scalar.activation(hhi[:, slot, :], row(h, f), ACT.Copy).then_inc(hs_hi, 1)

            def ffn(b0, b1, h0, start):
                body = up(b0, h0)
                with act.Fori(start, NF // 2 - 1) as i:
                    body(i)
                for f in range(RING):
                    hidden_hi(f, f, h0)
                body(NF // 2 - 1)
                with act.Fori(0, 4) as i:
                    for j in range(RING):
                        n, _, _ = block(b1 + j, i)
                        hidden_hi(i * RING + (j + RING), j, h0, after=n + 1)
                        high(block(b1 + j + RING, i))
                for f in range(16, 18):
                    hidden_hi(f + RING, f % RING, h0, after=b1 + f + 1)
                    high(block(b1 + f + RING))

            def evac(dst, src, done_sem, done, **kw):
                act.wait_ge(done_sem, done)
                nc.scalar.activation(dst, src, ACT.Identity if kw else ACT.Copy, **kw).then_inc(ev, 1)

            act.wait_ge(pool_c, 5)
            nc.scalar.activation(identR[:], ident[:], ACT.Copy).then_inc(act_c, 1)
            nc.scalar.activation(maskR[:], maskF[:], ACT.Copy).then_inc(act_c, 1)
            act.wait_ge(c_in, 16)
            for t in range(NT):
                turned_hi(t, t)
            for n in range(RING):
                high(block(n))
            up(B_UP1, 0)(0)
            for kb in range(2):
                act.wait_ge(t_done, NT + kb + 1)
                nc.scalar.activation(mThi[:, :, kb * P:(kb + 1) * P],
                                     ps[:, 4 + 2 * kb:6 + 2 * kb, :].rearrange("p a (k m) -> p (a k) m", m=P),
                                     ACT.Copy).then_inc(t_hi, 1)
            ffn(B_UP1, B_DN1, 0, 1)
            TG1 = NT + 2
            sd(0); sd(1); turned_hi(TG1, 0); sd(2); turned_hi(TG1 + 1, 1)
            for j in range(4):
                high(block(B_MK + j))
            sd(3); turned_hi(TG1 + 2, 2)
            for j in range(4):
                evac(mk[:, j, :], ps[:, j, 0:M], w_used, B_MK + j + 1)
                high(block(B_MK + j + 4))
                if j == 1:
                    turned_hi(TG1 + 3, 3)
            for j in range(4):
                high(block(B_MV + j + 4))
            for kb in range(2):
                evac(mv[:, kb, :], ps[:, 4 + kb, :], w_used, B_MV + 4)
            for j in range(KQ + KKV):
                evac(craw[:, j, :], ps[:, (0, 1, 2, 3, 6)[j], :], w_used, B_C + j + 1)
                high(block(B_C + j + 4))
            evac(kf[64:96, :], ps[0:ROPE, 7, :], w_used, B_KF + 1)
            evac(kf[0:HEADS, :], ps[32:32 + HEADS, 7, :], w_used, B_KF + 1, bias=bf[0:HEADS, :])
            high(block(B_KF + 4))
            for j in range(4):
                evac(MQ[:, j, :], ps[:, (4, 5, 0, 1)[j], :], w_used, B_MQ + j + 1)
                high(block(B_MQ + j + 4))

            def stage(kind, j, hd, p):
                apart(act, j)
                wait(act, s_done, j * 4)
                if isinstance(j, int) and j == J_FOX:
                    act.wait_ge(f_rows, 16 * 4)
                if kind == "mem":
                    nc.scalar.activation(qh[:], MQ[:, hd, :], ACT.Copy, scale=128.0 ** -0.5)
                    nc.scalar.activation(kh[:, 0:M], mk[:, hd, :], ACT.Copy).then_inc(st_hi, 1)
                elif kind == "mla":
                    nc.scalar.activation(qh[0:QK_MLA, :], rows(Q, 0, QK_MLA, hd), ACT.Copy,
                                         scale=float(QK_MLA) ** -0.5)
                    nc.scalar.activation(kh[0:NOPE, :], rows(Kt, 0, NOPE, hd), ACT.Copy).then_inc(st_hi, 1)
                else:
                    c = (hd - p) // 2 if isinstance(hd, int) else hd
                    src = lambda off: rows(FQK, 64 * p, 64 * p + 64, c + off)
                    slot = 2 * c + p if isinstance(c, int) else c * 2 + p
                    nc.scalar.activation(qh[0:64, :], src(0), ACT.Copy, scale=0.125)
                    nc.scalar.activation(kh[0:64, :], src(4), ACT.Copy)
                    nc.scalar.activation(qh[64:68, :], rows(Kt, 64, 68, slot), ACT.Copy)
                    nc.scalar.activation(kh[64:68, :], rows(Kt, 96, 100, slot), ACT.Copy).then_inc(st_hi, 1)

            def v_source(kind, hd, p):
                if kind == "mem":
                    return mv[:, :, hd * P:(hd + 1) * P], 2
                t = V if kind == "mla" else FV
                if isinstance(hd, int):
                    return t[:, :, hd * DV:(hd + 1) * DV], 4
                return t[:, :, bass.ds(hd * DV, DV)], 4

            def head(kind, j, hd, pair, p, nxt, a, b):
                src, nb = v_source(kind, hd, p)
                apart(act, j)
                wait(act, pv_done, j)
                nc.scalar.activation(vh[:].rearrange("p (k m) -> p k m", k=nb), src, ACT.Copy).then_inc(sv_hi, 1)
                for qt in range(NT):
                    nk = M if kind == "mem" else P * (qt + 1)
                    off = M * qt if kind == "mem" else P * qt * (qt + 1) // 2
                    act.wait_ge(mx_done, j * 4 + qt + 1)
                    if qt == 0:
                        wait(act, pt_done, pt_first(j))
                    nc.scalar.activation(prob[:, off:off + nk], ps[:, qt % 2, 0:nk], ACT.Exp,
                                         bias=nmax[:, qt:qt + 1], accum_out=rsum[:, qt:qt + 1]).then_inc(ex_done, 1)
                if nxt is not None:
                    stage(*nxt)
                kbs = 2 if kind == "mem" else 4
                for kb in range(kbs):
                    w = S if kind == "mem" else S - P * kb
                    off = PT_OFF[kind != "mem"][kb]
                    act.wait_ge(pt_done, pt_first(j) + kb + 1)
                    nc.scalar.activation(pthi[:, off:off + w], ps[:, 2 + kb % 2, 0:w], ACT.Copy).then_inc(ph_done, 1)
                a()
                apart(act, j)
                act.wait_ge(pv_done, j + 1)
                if kind == "mem":
                    nc.scalar.activation(MQ[:, hd, :], ps[:, 4 + p, :], ACT.Copy).then_inc(o_done, 1)
                else:
                    t = Q if kind == "mla" else FQK
                    nc.scalar.activation(rows(t, 64 * p, 64 * p + 64, pair), ps[0:64, 4 + p, :],
                                         ACT.Copy).then_inc(o_done, 1)
                b()

            act.wait_ge(ev, E_MQ + 4)
            stage("mem", 0, 0, 0)
            for hd in range(MEM_HEADS):
                n = B_FQK + 2 * hd

                def fill_a(n=n, hd=hd):
                    evac(FQK[:, 2 * hd, :], ps[:, 6, :], w_used, n + 1)
                    high(block(n + 4))

                def fill_b(n=n, hd=hd):
                    evac(FQK[:, 2 * hd + 1, :], ps[:, 7, :], w_used, n + 2)
                    high(block(n + 5))
                    if hd >= 2:
                        for c in (range(KQ) if hd == 2 else range(KQ, KQ + KKV)):
                            act.wait_ge(cn, c + 1)
                            dst = cqhi[:, c, :] if c < KQ else ckhi[:, c - KQ, :]
                            nc.scalar.activation(dst, craw[:, c, :], ACT.Copy).then_inc(cn_hi, 1)
                if hd == 0:
                    for c, width in enumerate((QL, KVL)):
                        act.wait_ge(ss_done, c + 1)
                        nc.scalar.activation(rms[:, c, :], ps[:, 2 + c, :], ACT.Sqrt, scale=1.0 / width,
                                             bias=cst[:, 3:4]).then_inc(rm_sd, 1)
                nxt = ("mem", hd + 1, hd + 1, (hd + 1) % 2) if hd + 1 < MEM_HEADS else None
                head("mem", hd, hd, None, hd % 2, nxt, fill_a, fill_b)

            act.wait_ge(o_done, MEM_HEADS)
            nc.scalar.activation(ohi[:], MQ[:], ACT.Copy).then_inc(os_hi, 1)
            act.wait_ge(tb_v, 8)
            nc.scalar.activation(tabs[64:96, 2, :], tabs[64:96, 0, :], ACT.Sin,
                                 scale=cst[64:96, 1:2]).then_inc(tb_s, 1)
            nc.scalar.activation(tabs[64:96, 1, :], tabs[64:96, 0, :], ACT.Abs).then_inc(tb_s, 1)
            act.wait_ge(tb_s, 2)
            nc.scalar.activation(tabs[64:96, 3, :], tabs[64:96, 1, :], ACT.Sin, scale=-1.0,
                                 bias=cst[64:96, 4:5]).then_inc(tb_s, 1)
            for hd in range(HEADS):
                evac(Q[0:QK_MLA, hd, :], ps[0:QK_MLA, hd, :], *((pj, hd + 1) if hd < 7 else (w_used, B_UQ + KQ)))
            for n in (B_FV + 1, B_FV + 2, B_FV + 3):
                high(block(n))
            nc.scalar.activation(tabs[0:HEADS, 0, :], kf[0:HEADS, :], ACT.Abs).then_inc(fg_s, 1)
            act.wait_ge(fg_s, 1)
            nc.scalar.activation(tabs[0:HEADS, 1, :], tabs[0:HEADS, 0, :], ACT.Exp, scale=-1.0).then_inc(fg_s, 1)
            act.wait_ge(fg_s, 2)
            nc.scalar.activation(tabs[0:HEADS, 2, :], tabs[0:HEADS, 1, :], ACT.Ln, bias=1.0).then_inc(fg_s, 1)
            for j in range(4):
                high(block(B_FV + j + 4))
            for hd in range(HEADS):
                evac(Kt[0:NOPE, hd, :], ps[0:NOPE, hd % 4, :], pj, HEADS + hd)
            for t in range(NT):
                evac(V[:, t, :], ps[:, t, :], *((pj, 2 * HEADS + t) if t < 3 else (w_used, B_UKV + KKV)))
            for t in range(NT):
                evac(FV[:, t, :], ps[:, 4 + t, :], w_used, B_FV + 4)
            for n in (B_MG + 2, B_MG + 3):
                high(block(n))
            act.wait_ge(rp, 12)
            nc.scalar.activation(kh[64:96, :], kf[64:96, :], ACT.Copy).then_inc(kr, 1)

            def gate(br, n, d, g):
                apart(act, g)
                act.wait_ge(w_used, n + 1)
                wait(act, mg_done, g)
                bank = 6
                bcol = (2, 0, 1)[br] * 8
                b_ap = bg[:, bcol + d:bcol + d + 1] if isinstance(d, int) else bg[:, bass.ds(d + bcol, 1)]
                nc.scalar.activation(sig[:], ps[:, bank, :], ACT.Sigmoid, bias=b_ap).then_inc(sg_done, 1)

            def branch_heads(kind, br, j0, first_next):
                def body(i, last=False):
                    for p in range(2):
                        hd = i * 2 + p
                        j = i * 2 + (j0 + p)
                        n, like, _ = block(B_MG + 16 * br + 2 * p, i)

                        def fill_a():
                            gate(br, n, hd, i * 2 + (8 * br + p))
                            high(block(B_MG + 16 * br + 2 * p + 4, i))

                        def fill_b():
                            high(block(B_MG + 16 * br + 2 * p + 5, i))
                        if last and p == 1:
                            nxt = first_next
                        elif kind == "mla":
                            nxt = (kind, j + 1, hd + 1, 1 - p)
                        else:
                            nxt = (kind, j + 1, (i + p) if not isinstance(i, int) else hd + 1, 1 - p)
                        head(kind, j, hd, i, p, nxt, fill_a, fill_b)
                if br == 0:
                    body(0)
                with act.Fori(1 if br == 0 else 0, 3) as i:
                    body(i)
                body(3, True)

            def split_branch(src, br):
                act.wait_ge(o_done, J_MLA + HEADS * br)
                act.wait_ge(w_used, B_MG + 16 * br)
                nc.scalar.activation(ohi[:], src, ACT.Copy).then_inc(os_hi, 1)

            act.wait_ge(ev, E_ALL)
            stage("mla", J_MLA, 0, 0)
            act.wait_ge(kr, 2)
            branch_heads("mla", 0, J_MLA, ("fox", J_FOX, 0, 0))
            split_branch(Q[:, 0:4, :], 1)
            branch_heads("fox", 1, J_FOX, None)
            split_branch(FQK[:, 0:4, :], 2)

            def merge(i):
                for p in range(2):
                    n, _, _ = block(B_MG + 32 + 2 * p, i)
                    gate(2, n, i * 2 + p, i * 2 + (16 + p))
                    high(block(B_MG + 32 + 2 * p + 4, i))
                    high(block(B_MG + 32 + 2 * p + 5, i))
            with act.Fori(0, 3) as i:
                merge(i)
            merge(3)
            for k in range(KD):
                act.wait_ge(w_used, B_OUT)
                act.wait_ge(mg_done, 16 + k + 1)
                nc.scalar.activation(xhi[:, k, :], merged[:, k, :], ACT.Copy).then_inc(ms_hi, 1)
            for k in range(4):
                high(block(B_OUT + k + 4))
            TG2 = TG1 + NT
            sd(4); sd(5); turned_hi(TG2, 0); sd(6); turned_hi(TG2 + 1, 1)
            for n in range(RING):
                high(block(B_UP2 + n))
            sd(7); turned_hi(TG2 + 2, 2); turned_hi(TG2 + 3, 3)
            body = up(B_UP2, NF)
            with act.Fori(0, NF // 2 - 1) as i:
                body(i)
            for f in range(RING):
                hidden_hi(f, f, NF)
            body(NF // 2 - 1)
            with act.Fori(0, 4) as i:
                for j in range(RING):
                    n, _, _ = block(B_DN2 + j, i)
                    hidden_hi(i * RING + (j + RING), j, NF, after=n + 1)
                    high(block(B_DN2 + j + RING, i))
            for f in range(16, 18):
                hidden_hi(f + RING, f % RING, NF, after=B_DN2 + f + 1)
                high(block(B_DN2 + f + RING))
            for q in range(2 * NT, 3 * NT):
                sd(q)

        @blk.vector
        def _(dve):
            def turned_lo(g, t):
                dve.wait_ge(t_hi, g + 1)
                nc.vector.tensor_tensor(xlo[:, :, t * P:(t + 1) * P],
                                        ps[:, 2 * t:2 * t + 2, :].rearrange("p a (k m) -> p (a k) m", m=P),
                                        xhi[:, :, t * P:(t + 1) * P].bitcast(F32), ALU.subtract).then_inc(t_lo, 1)

            def norm(q):
                t = q % NT
                r = res[:, q % 2, :]
                yv = ps[:, 2 * t:2 * t + 2, :].rearrange("p a n -> p (a n)")
                if t < NT - 1:
                    dve.wait_ge(y_done, (NT - 1) * (q // NT) + t + 1)
                else:
                    dve.wait_ge(w_used, (B_MK, B_UP2, B_END)[q // NT])
                dve.wait_ge(x_in[t], 32 if q >= NT else 16)
                dve.wait_ge(g_in, 32 * (q // NT + 1))
                wait(dve, lnc, 6 * q)
                nc.vector.scalar_tensor_tensor(r, X[:, t, :], ALPHA, yv, ALU.mult, ALU.add).then_inc(lnc, 1)
                dve.wait_ge(lnc, 6 * q + 1)
                nc.vector.bn_stats(stats[:, 0, :], r[:, 0:512])
                nc.vector.bn_stats(stats[:, 1, :], r[:, 512:1024]).then_inc(lnc, 1)
                dve.wait_ge(lnc, 6 * q + 2)
                nc.vector.bn_aggr(mvar[:], stats[:].rearrange("p a b -> p (a b)")).then_inc(lnc, 1)
                dve.wait_ge(ln_sd, q + 1)
                nc.vector.reciprocal(rstd[:, q % 2:q % 2 + 1], rstd[:, q % 2:q % 2 + 1]).then_inc(lnc, 1)
                nc.vector.scalar_tensor_tensor(r, r, mvar[:, 0:1], lng[:], ALU.subtract, ALU.mult).then_inc(lnc, 1)
                dve.wait_ge(lnc, 6 * q + 5)
                nc.vector.scalar_tensor_tensor(X[:, t, :], r, rstd[:, q % 2:q % 2 + 1], lnb[:], ALU.mult,
                                               ALU.add).then_inc(lnc, 1)

            def up(b0, h0):
                def body(i):
                    for p in range(2):
                        nb, _, _ = block(b0 + 2 * p + 1, i)
                        f = i * 2 + p
                        dve.wait_ge(sl_done, f + h0 + 1)
                        dve.wait_ge(w_used, nb + 1)
                        nc.vector.scalar_tensor_tensor(row(h, f), stmp[:, p, :], 0.5, ps[:, 2 * p + 1, :],
                                                       ALU.mult, ALU.mult).then_inc(h_done, 1)
                return body

            def hidden_lo(f, slot, h0):
                dve.wait_ge(hs_hi, f + h0 + 1)
                nc.vector.tensor_tensor(hlo[:, slot, :], row(h, f), hhi[:, slot, :].bitcast(F32),
                                        ALU.subtract).then_inc(hs_lo, 1)

            def ffn(b0, b1, h0, start):
                body = up(b0, h0)
                with dve.Fori(start, NF // 2 - 1) as i:
                    body(i)
                for f in range(RING):
                    hidden_lo(f, f, h0)
                body(NF // 2 - 1)
                with dve.Fori(0, 4) as i:
                    for j in range(RING):
                        hidden_lo(i * RING + (j + RING), j, h0)
                for f in range(20, NF):
                    hidden_lo(f, f % RING, h0)

            for t in range(NT):
                turned_lo(t, t)
            up(B_UP1, 0)(0)
            for kb in range(2):
                dve.wait_ge(t_hi, NT + kb + 1)
                nc.vector.tensor_tensor(mTlo[:, :, kb * P:(kb + 1) * P],
                                        ps[:, 4 + 2 * kb:6 + 2 * kb, :].rearrange("p a (k m) -> p (a k) m", m=P),
                                        mThi[:, :, kb * P:(kb + 1) * P].bitcast(F32), ALU.subtract).then_inc(t_lo, 1)
            ffn(B_UP1, B_DN1, 0, 1)
            TG1 = NT + 2
            norm(0); norm(1); turned_lo(TG1, 0)
            norm(2); turned_lo(TG1 + 1, 1)
            norm(3); turned_lo(TG1 + 2, 2); turned_lo(TG1 + 3, 3)
            dve.wait_ge(h_done, NF)
            for c in range(KQ + KKV):
                dve.wait_ge(ev, E_C + c + 1)
                if c >= 3:
                    dve.wait_ge(ss_done, 1)
                nc.vector.tensor_tensor(csq[:, c % 3, :], craw[:, c, :], craw[:, c, :], ALU.mult).then_inc(sq_done, 1)

            def stage(kind, j, hd, p):
                dve.wait_ge(st_hi, j + 1)
                if kind == "mem" and hd == 0:
                    dve.wait_ge(ev, E_MQ + 4)
                def low(dst, src, hi, scale=None):
                    if scale is None:
                        return nc.vector.tensor_tensor(dst, src, hi.bitcast(F32), ALU.subtract)
                    return nc.vector.scalar_tensor_tensor(dst, src, scale, hi.bitcast(F32), ALU.mult, ALU.subtract)
                if kind == "mem":
                    low(ql[:], MQ[:, hd, :], qh[:], 128.0 ** -0.5)
                    low(kl[:, 0:M], mk[:, hd, :], kh[:, 0:M]).then_inc(st_lo, 1)
                elif kind == "mla":
                    low(ql[0:QK_MLA, :], rows(Q, 0, QK_MLA, hd), qh[0:QK_MLA, :], float(QK_MLA) ** -0.5)
                    low(kl[0:NOPE, :], rows(Kt, 0, NOPE, hd), kh[0:NOPE, :]).then_inc(st_lo, 1)
                else:
                    c = (hd - p) // 2 if isinstance(hd, int) else hd
                    src = lambda off: rows(FQK, 64 * p, 64 * p + 64, c + off)
                    low(ql[0:64, :], src(0), qh[0:64, :], 0.125)
                    low(kl[0:64, :], src(4), kh[0:64, :]).then_inc(st_lo, 1)

            def v_source(kind, hd):
                if kind == "mem":
                    return mv[:, :, hd * P:(hd + 1) * P], 2
                t = V if kind == "mla" else FV
                if isinstance(hd, int):
                    return t[:, :, hd * DV:(hd + 1) * DV], 4
                return t[:, :, bass.ds(hd * DV, DV)], 4

            def head(kind, j, hd, p, nxt, fill):
                src, nb = v_source(kind, hd)
                dve.wait_ge(sv_hi, j + 1)
                nc.vector.tensor_tensor(vl[:].rearrange("p (k m) -> p k m", k=nb), src,
                                        vh[:].bitcast(F32).rearrange("p (k m) -> p k m", k=nb),
                                        ALU.subtract).then_inc(sv_lo, 1)

                def row_max(qt):
                    nk = M if kind == "mem" else P * (qt + 1)
                    dve.wait_ge(s_done, j * 4 + qt + 1)
                    nc.vector.tensor_reduce(nmax[:, qt:qt + 1], ps[:, qt % 2, 0:nk], AX.X, ALU.max,
                                            negate=True).then_inc(mx_done, 1)

                def normalise(qt):
                    nk = M if kind == "mem" else P * (qt + 1)
                    off = M * qt if kind == "mem" else P * qt * (qt + 1) // 2
                    dve.wait_ge(ex_done, j * 4 + qt + 1)
                    nc.vector.reciprocal(rinv[:, qt:qt + 1], rsum[:, qt:qt + 1]).then_inc(rc_done, 1)
                    dve.wait_ge(rc_done, j * 4 + qt + 1)
                    nc.vector.tensor_scalar(prob[:, off:off + nk], prob[:, off:off + nk], rinv[:, qt:qt + 1], None,
                                            ALU.mult).then_inc(pn_done, 1)
                row_max(0)
                row_max(1)
                normalise(0)
                row_max(2)
                normalise(1)
                row_max(3)
                normalise(2)
                normalise(3)
                if nxt is not None:
                    stage(*nxt)
                for kb in range(2 if kind == "mem" else 4):
                    w = S if kind == "mem" else S - P * kb
                    off = PT_OFF[kind != "mem"][kb]
                    dve.wait_ge(ph_done, pt_first(j) + kb + 1)
                    nc.vector.tensor_tensor(ptlo[:, off:off + w], ps[:, 2 + kb % 2, 0:w],
                                            pthi[:, off:off + w].bitcast(F32), ALU.subtract).then_inc(pl_done, 1)
                fill()

            stage("mem", 0, 0, 0)
            for hd in range(MEM_HEADS):
                def fill(hd=hd):
                    if hd < 2:
                        dve.wait_ge(rm_sd, hd + 1)
                        nc.vector.reciprocal(rms[:, hd, :], rms[:, hd, :]).then_inc(rm_r, 1)
                    if hd >= 2:
                        cs = range(KQ) if hd == 2 else range(KQ, KQ + KKV)
                        dve.wait_ge(rm_r, hd - 1)
                        for c in cs:
                            nc.vector.scalar_tensor_tensor(craw[:, c, :], craw[:, c, :], gq[:, c:c + 1],
                                                           rms[:, 0 if c < KQ else 1, :], ALU.mult,
                                                           ALU.mult).then_inc(cn, 1)
                        for c in cs:
                            hi, lo = (cqhi[:, c, :], cqlo[:, c, :]) if c < KQ else (ckhi[:, c - KQ, :], cklo[:, c - KQ, :])
                            dve.wait_ge(cn_hi, c + 1)
                            nc.vector.tensor_tensor(lo, craw[:, c, :], hi.bitcast(F32), ALU.subtract).then_inc(cn_lo, 1)
                nxt = ("mem", hd + 1, hd + 1, (hd + 1) % 2) if hd + 1 < MEM_HEADS else None
                head("mem", hd, hd, hd % 2, nxt, fill)
            dve.wait_ge(os_hi, 1)
            nc.vector.tensor_tensor(olo[:], MQ[:], ohi[:].bitcast(F32), ALU.subtract).then_inc(os_lo, 1)

            R = slice(64, 96)
            two_pi = 2.0 * np.pi
            parts, rest = [], two_pi
            for bits in (5, 13, 21):
                c = float(np.round(rest * 2.0 ** bits) / 2.0 ** bits)
                parts.append(c)
                rest -= c
            parts.append(float(np.float32(rest)))
            magic = float(1.5 * 2 ** 23)
            dve.wait_ge(pv_done, MEM_HEADS)
            nc.vector.tensor_scalar(tabs[R, 0, :], pos[R, :], cst[R, 0:1], None, ALU.mult).then_inc(tb_v, 1)
            dve.wait_ge(tb_v, 1)
            nc.vector.tensor_scalar(tabs[R, 1, :], tabs[R, 0, :], 1.0 / two_pi, magic, ALU.mult, ALU.add).then_inc(tb_v, 1)
            dve.wait_ge(tb_v, 2)
            nc.vector.tensor_scalar(tabs[R, 1, :], tabs[R, 1, :], magic, None, ALU.subtract).then_inc(tb_v, 1)
            for n, c in enumerate(parts):
                dve.wait_ge(tb_v, 3 + n)
                nc.vector.scalar_tensor_tensor(tabs[R, 0, :], tabs[R, 1, :], -c, tabs[R, 0, :], ALU.mult,
                                               ALU.add).then_inc(tb_v, 1)
            dve.wait_ge(tb_v, 7)
            nc.vector.tensor_scalar(tabs[R, 0, :], tabs[R, 0, :], 3.1415925, -3.1415925, ALU.min, ALU.max).then_inc(tb_v, 1)
            dve.wait_ge(tb_s, 3)
            swap = [(k + ROPE // 2) % ROPE for k in range(ROPE)]

            def rotate(v, t, sin, cos, before):
                wait(dve, rp, before)
                nc.vector.stream_shuffle(t, v, swap).then_inc(rp, 1)
                dve.wait_ge(rp, before + 1)
                nc.vector.tensor_tensor(t, t, sin, ALU.mult).then_inc(rp, 1)
                nc.vector.tensor_tensor(v, v, cos, ALU.mult).then_inc(rp, 1)
                dve.wait_ge(rp, before + 3)
                nc.vector.tensor_tensor(v, v, t, ALU.add).then_inc(rp, 1)

            rotate(kf[R, :], rtmp[R, :], tabs[R, 2, :], tabs[R, 3, :], 0)
            dve.wait_ge(w_used, B_UQ + KQ)
            for half in range(2):
                hs = slice(4 * half, 4 * half + 4)
                dve.wait_ge(ev, E_UQ + 4 * half + 4)
                rotate(Q[R, hs, :], Kt[R, hs, :], tabs[R, 2:3, :].to_broadcast([ROPE, 4, S]),
                       tabs[R, 3:4, :].to_broadcast([ROPE, 4, S]), 4 + 4 * half)
            H8 = slice(0, HEADS)
            nc.vector.memset(tabs[H8, 4, :], 0.0).then_inc(fg_v, 1)
            dve.wait_ge(fg_s, 3)
            nc.vector.scalar_tensor_tensor(tabs[H8, 3, :], kf[H8, :], 0.0, tabs[H8, 2, :], ALU.min,
                                           ALU.subtract).then_inc(fg_v, 1)
            dve.wait_ge(fg_v, 2)
            nc.vector.tensor_tensor_scan(tabs[H8, 0, :], tabs[H8, 4, :], tabs[H8, 3, :], 0.0, ALU.add,
                                         ALU.add).then_inc(fg_v, 1)
            dve.wait_ge(fg_v, 3)
            nc.vector.tensor_copy(tabs[H8, 1, :].bitcast(F32R), tabs[H8, 0, :]).then_inc(fg_v, 1)
            dve.wait_ge(fg_v, 4)
            nc.vector.tensor_tensor(tabs[H8, 2, :], tabs[H8, 0, :], tabs[H8, 1, :], ALU.subtract).then_inc(fg_v, 1)
            nc.vector.tensor_scalar(tabs[H8, 3, :], tabs[H8, 1, :], -1.0, None, ALU.mult)
            dve.wait_ge(fg_v, 5)
            nc.vector.tensor_scalar(tabs[H8, 4, :], tabs[H8, 2, :], -1.0, None, ALU.mult).then_inc(fg_v, 1)
            dve.wait_ge(rp, 12)
            nc.vector.memset(Kt[64:68, :, :], 1.0).then_inc(fg_v, 1)
            nc.vector.memset(Kt[96:100, :, :], 1.0).then_inc(fg_v, 1)
            dve.wait_ge(kr, 1)
            nc.vector.tensor_tensor(kl[64:96, :], kf[64:96, :], kh[64:96, :].bitcast(F32), ALU.subtract).then_inc(kr, 1)
            dve.wait_ge(sp_out, 16 * NT)

            def merge(br, n, d, g, ybank):
                dve.wait_ge(sg_done, g + 1)
                dve.wait_ge(w_used, n + 1)
                if br == 0:
                    nc.vector.tensor_tensor(row(merged, d), sig[:], ps[:, ybank, :], ALU.mult).then_inc(mg_done, 1)
                else:
                    nc.vector.tensor_tensor(tmp[:], sig[:], ps[:, ybank, :], ALU.mult).then_inc(mt_done, 1)
                    dve.wait_ge(mt_done, g - 8 + 1)
                    nc.vector.tensor_tensor(row(merged, d), row(merged, d), tmp[:], ALU.add).then_inc(mg_done, 1)

            def branch_heads(kind, br, j0, first_next):
                def body(i, last=False):
                    for p in range(2):
                        hd = i * 2 + p
                        j = i * 2 + (j0 + p)
                        n, _, _ = block(B_MG + 16 * br + 2 * p + 1, i)
                        if last and p == 1:
                            nxt = first_next
                        elif kind == "mla":
                            nxt = (kind, j + 1, hd + 1, 1 - p)
                        else:
                            nxt = (kind, j + 1, (i + p) if not isinstance(i, int) else hd + 1, 1 - p)
                        head(kind, j, hd, p, nxt, lambda: merge(br, n, hd, i * 2 + (8 * br + p), 7))
                with dve.Fori(0, 3) as i:
                    body(i)
                body(3, True)

            def split_branch(src, br):
                dve.wait_ge(os_hi, br + 1)
                nc.vector.tensor_tensor(olo[:], src, ohi[:].bitcast(F32), ALU.subtract).then_inc(os_lo, 1)

            stage("mla", J_MLA, 0, 0)
            branch_heads("mla", 0, J_MLA, ("fox", J_FOX, 0, 0))
            split_branch(Q[:, 0:4, :], 1)
            branch_heads("fox", 1, J_FOX, None)
            split_branch(FQK[:, 0:4, :], 2)
            with dve.Fori(0, 4) as i:
                for p in range(2):
                    n, _, _ = block(B_MG + 32 + 2 * p + 1, i)
                    merge(2, n, i * 2 + p, i * 2 + (16 + p), (7, 5)[p])
            for k in range(KD):
                dve.wait_ge(ms_hi, k + 1)
                nc.vector.tensor_tensor(xlo[:, k, :], merged[:, k, :], xhi[:, k, :].bitcast(F32),
                                        ALU.subtract).then_inc(ms_lo, 1)
            TG2 = TG1 + NT
            norm(4); norm(5); turned_lo(TG2, 0)
            norm(6); turned_lo(TG2 + 1, 1)
            norm(7); turned_lo(TG2 + 2, 2); turned_lo(TG2 + 3, 3)
            ffn(B_UP2, B_DN2, NF, 0)
            for t in range(NT):
                norm(2 * NT + t)

        @blk.tensor
        def _(pe):
            mm = nc.tensor.matmul

            def wv(t, like, m=P):
                return t[:, like % RING, :].rearrange("p (k m) -> p k m", m=m)

            def three(k):
                return ((0, 0), (0, 1), (1, 0))[k]

            def product(m, like, out_ap, rh, rl, last, cols=slice(0, P)):
                k, (a, b) = m // 3, three(m % 3)
                return mm(out_ap, wv((whi, wlo)[a], like)[:, k, cols], (rh, rl)[b](k), start=m == 0, stop=m == last)

            def feature_block(b, bank, cols=slice(0, P), rh=None, rl=None, width=S):
                n, like, _ = b
                pe.wait_ge(w_lo, n + 1)
                rh = rh or (lambda k: xhi[:, k, :])
                rl = rl or (lambda k: xlo[:, k, :])
                rows_out = cols.stop - cols.start
                for m in range(3 * KD):
                    ins = product(m, like, ps[0:rows_out, bank, 0:width], rh, rl, 3 * KD - 1, cols)
                ins.then_inc(w_used, 1)

            def turn(g, src, bank, ready=None):
                for k in range(KD):
                    ins = nc.tensor.transpose(ps[:, bank + k // 4, (k % 4) * P:(k % 4 + 1) * P],
                                              src[:, k * P:(k + 1) * P], ident[:])
                ins.then_inc(t_done, 1)

            def token_block(like, t, sh, sl, start, stop):
                for a, b in ((sh, whi), (sh, wlo), (sl, whi)):
                    for half in range(2):
                        ins = mm(ps[:, 2 * t + half, :], a(t), b[:, like % RING, half * 512:(half + 1) * 512],
                                 start=start and a is sh and b is whi, stop=stop and a is sl)
                return ins

            def up(b0, h0):
                def body(i):
                    for p in range(2):
                        f = i * 2 + p
                        wait(pe, h_done, f + h0 - 1)
                        feature_block(block(b0 + 2 * p, i), 2 * p)
                        feature_block(block(b0 + 2 * p + 1, i), 2 * p + 1)
                return body

            def hidden(slot):
                return (lambda t: hhi[:, slot, t * P:(t + 1) * P]), (lambda t: hlo[:, slot, t * P:(t + 1) * P])

            def turn_tile(L, t):
                pe.wait_ge(lnc, 6 * (L * NT + t + 1))
                turn(NT + 2 + L * NT + t, X[:, t, :], 2 * t)

            def finish(b0, sources, L):
                for t in range(NT):
                    for c, (sh, sl, ready, count) in enumerate(sources):
                        if t == 0:
                            pe.wait_ge(ready, count)
                            pe.wait_ge(w_lo, b0 + c + 1)
                        ins = token_block(b0 + c, t, sh, sl, False, c == RING - 1)
                        if t == NT - 1:
                            ins.then_inc(w_used, 1)
                    if t < NT - 1:
                        ins.then_inc(y_done, 1)
                    if t >= 1 and L < 2:
                        turn_tile(L, t - 1)

            def down(b1, h0, L):
                def one(b, f, slot, first):
                    n, like, _ = b
                    pe.wait_ge(hs_lo, f + h0 + 1)
                    pe.wait_ge(w_lo, n + 1)
                    sh, sl = hidden(slot)
                    order = (2, 3, 0, 1) if first else range(NT)
                    for t in order:
                        if first and t == 0:
                            pe.wait_ge(h_done, h0 + NF)
                        ins = token_block(like, t, sh, sl, first, False)
                    ins.then_inc(w_used, 1)
                for f in range(RING):
                    one(block(b1 + f), f, f, f == 0)
                with pe.Fori(1, 4) as i:
                    for j in range(RING):
                        one(block(b1 + j, i), i * RING + j, j, False)
                for f in (16, 17):
                    one(block(b1 + f), f, f % RING, False)
                finish(b1 + 18, [(*hidden(f % RING), hs_lo, f + h0 + 1) for f in range(18, NF)], L)

            pe.wait_ge(pool_c, 5)
            for t in range(NT):
                pe.wait_ge(x_in[t], 16)
                turn(t, X[:, t, :], 2 * t)
            pe.wait_ge(t_lo, NT)
            up(B_UP1, 0)(0)
            pe.wait_ge(m_in, 16)
            for kb in range(2):
                turn(NT + kb, res[:, kb, :], 4 + 2 * kb)
            with pe.Fori(1, NF // 2) as i:
                up(B_UP1, 0)(i)
            pe.wait_ge(t_lo, NT + 2)
            TG1 = NT + 2
            down(B_DN1, 0, 0)
            for j in range(4):
                if j % 2 == 0:
                    pe.wait_ge(t_lo, TG1 + j // 2 + 1)
                feature_block(block(B_MK + j), j, rh=lambda k: mThi[:, k, :], rl=lambda k: mTlo[:, k, :], width=M)
                if j == 1:
                    turn_tile(0, 3)
            pe.wait_ge(t_lo, TG1 + 3)
            for j in range(4):
                n, like, _ = block(B_MV + j)
                pe.wait_ge(w_lo, n + 1)
                for k in range(2):
                    for kb in range(2):
                        for a, b in ((0, 0), (0, 1), (1, 0)):
                            ins = mm(ps[:, 4 + kb, :], (mThi, mTlo)[a][:, 2 * j + k, kb * P:(kb + 1) * P],
                                     wv((whi, wlo)[b], like, 512)[:, k, :], start=j == 0 and k == 0 and a + b == 0,
                                     stop=j == 3 and k == 1 and a == 1)
                ins.then_inc(w_used, 1)
            pe.wait_ge(t_lo, TG1 + 4)
            for j in range(KQ + KKV):
                pe.wait_ge(ev, j + 1 if j < 4 else E_MK + 4)
                feature_block(block(B_C + j), (0, 1, 2, 3, 6)[j])
            feature_block(block(B_KF), 7, cols=slice(64, 104))
            for j in range(4):
                pe.wait_ge(ev, (E_MV + 1, E_MV + 2, E_C + 1, E_C + 2)[j])
                feature_block(block(B_MQ + j), (4, 5, 0, 1)[j])
            pe.wait_ge(ev, E_C + 4)
            pe.wait_ge(pool_c, 5)
            for c, ks in enumerate((range(0, KQ), range(KQ, KQ + KKV))):
                for k in ks:
                    pe.wait_ge(sq_done, k + 1)
                    ins = mm(ps[:, 2 + c, :], ones[:], csq[:, k % 3, :], start=k == ks[0], stop=k == ks[-1])
                ins.then_inc(ss_done, 1)

            def head(kind, j, p, fill, cuts):
                kq = {"mem": P, "mla": QK_MLA, "fox": 68}[kind]
                kq_lo = {"mem": P, "mla": QK_MLA, "fox": 64}[kind]
                causal = kind != "mem"
                step = [0]

                def filler():
                    fill(cuts[step[0]], cuts[step[0] + 1])
                    step[0] += 1

                def logits(qt):
                    nk = P * (qt + 1) if causal else M
                    wait(pe, ex_done, j * 4 + (qt - 1))
                    o = ps[:, qt % 2, 0:nk]
                    q_cols = slice(qt * P, (qt + 1) * P)
                    mm(o, qh[0:kq, q_cols], kh[0:kq, 0:nk], start=True, stop=False)
                    mm(o, qh[0:kq_lo, q_cols], kl[0:kq_lo, 0:nk], start=False, stop=False)
                    ins = mm(o, ql[0:kq_lo, q_cols], kh[0:kq_lo, 0:nk], start=False, stop=not causal)
                    if causal:
                        ins = mm(ps[:, qt % 2, nk - P:nk], identR[:], maskR[:], start=False, stop=True)
                    ins.then_inc(s_done, 1)

                def turn_probs(kb):
                    if isinstance(j, int) and j == 0:
                        pe.wait_ge(rm_sd, 2)
                    wait(pe, pl_done, pt_first(j) + kb - 1)
                    first = kb if causal else 0
                    for qt in range(first, NT):
                        pe.wait_ge(pn_done, j * 4 + qt + 1)
                        off = P * qt * (qt + 1) // 2 if causal else M * qt
                        ins = nc.tensor.transpose(ps[:, 2 + kb % 2, (qt - first) * P:(qt - first + 1) * P],
                                                  prob[:, off + kb * P:off + (kb + 1) * P], ident[:])
                    ins.then_inc(pt_done, 1)

                def values(kb):
                    w = S - P * kb if causal else S
                    off = PT_OFF[causal][kb]
                    dv = DV if causal else P
                    nb = 4 if causal else 2
                    pe.wait_ge(pl_done, pt_first(j) + kb + 1)
                    if kb == 0:
                        pe.wait_ge(sv_lo, j + 1)
                        wait(pe, o_done, j - 1)
                    o = ps[0:dv, 4 + p, S - w:S]
                    for a, b in ((0, 0), (0, 1), (1, 0)):
                        ins = mm(o, (vh, vl)[a][:].rearrange("p (k m) -> p k m", k=nb)[:, kb, :],
                                 (pthi, ptlo)[b][:, off:off + w], start=kb == 0 and a + b == 0,
                                 stop=kb == nb - 1 and a == 1)
                    return ins

                pe.wait_ge(st_lo, j + 1)
                logits(0)
                logits(1)
                filler()
                logits(2)
                filler()
                logits(3)
                filler()
                filler()
                if causal:
                    turn_probs(0)
                    turn_probs(1)
                    filler()
                    turn_probs(2)
                    turn_probs(3)
                    filler()
                    values(0)
                    values(1)
                    filler()
                    values(2)
                    values(3).then_inc(pv_done, 1)
                else:
                    turn_probs(0)
                    filler()
                    turn_probs(1)
                    filler()
                    values(0)
                    filler()
                    values(1).then_inc(pv_done, 1)
                filler()

            pe.wait_ge(ev, E_MQ + 4)
            for hd in range(MEM_HEADS):
                def fill(lo, hi, hd=hd):
                    for m in range(lo, hi):
                        k, m1 = m // 24, m % 24
                        n = B_FQK + 2 * hd + k
                        if m1 == 0:
                            pe.wait_ge(w_lo, n + 1)
                            wait(pe, ev, (E_KF + 2) if hd == 0 else E_FQK + 2 * (hd - 1) + k + 1)
                        ins = product(m1, n, ps[:, 6 + k, :], lambda k: xhi[:, k, :], lambda k: xlo[:, k, :], 23)
                        if m1 == 23:
                            ins.then_inc(w_used, 1)
                head("mem", hd, hd % 2, fill, [6 * k for k in range(9)])
            pe.wait_ge(ev, E_FQK + 8)
            pe.wait_ge(pl_done, 2 * MEM_HEADS)
            pe.wait_ge(o_done, MEM_HEADS)
            pe.wait_ge(ex_done, 4 * MEM_HEADS)
            pe.wait_ge(cn_lo, KQ)
            for k in range(KQ):
                pe.wait_ge(w_lo, B_UQ + k + 1)
            for hd in range(HEADS):
                for k in range(KQ):
                    for a, b in ((0, 0), (0, 1), (1, 0)):
                        ins = mm(ps[0:QK_MLA, hd, :],
                                 (whi, wlo)[a][:, (B_UQ + k) % RING, hd * QK_MLA:(hd + 1) * QK_MLA],
                                 (cqhi, cqlo)[b][:, k, :], start=k == 0 and a + b == 0, stop=k == KQ - 1 and a == 1)
                        if hd == HEADS - 1 and a == 1 and k < KQ - 1:
                            ins.then_inc(w_used, 1)
                if hd < HEADS - 1:
                    ins.then_inc(pj, 1)
            ins.then_inc(w_used, 1)
            for j in range(4):
                n, like, _ = block(B_FV + j)
                pe.wait_ge(w_lo, n + 1)
                if j == 0:
                    pe.wait_ge(ev, E_UQ + HEADS)
                for t in range(NT):
                    for k in range(2):
                        for a, b in ((0, 0), (0, 1), (1, 0)):
                            ins = mm(ps[:, 4 + t, :], (xhi, xlo)[a][:, 2 * j + k, t * P:(t + 1) * P],
                                     wv((whi, wlo)[b], like, 512)[:, k, :], start=j == 0 and k == 0 and a + b == 0,
                                     stop=j == 3 and k == 1 and a == 1)
                ins.then_inc(w_used, 1)
            pe.wait_ge(cn_lo, KQ + KKV)
            for k in range(KKV):
                pe.wait_ge(w_lo, B_UKV + k + 1)
            for hd in range(HEADS):
                wait(pe, ev, E_UQ + 8 if hd < 4 else E_K + hd - 3)
                for k in range(KKV):
                    for a, b in ((0, 0), (0, 1), (1, 0)):
                        ins = mm(ps[0:NOPE, hd % 4, :],
                                 wv((whi, wlo)[a], B_UKV + k)[:, hd, 0:NOPE],
                                 (ckhi, cklo)[b][:, k, :], start=k == 0 and a + b == 0, stop=k == KKV - 1 and a == 1)
                ins.then_inc(pj, 1)
            for t in range(NT):
                pe.wait_ge(ev, E_K + 5 + t)
                for k in range(KKV):
                    for a, b in ((0, 0), (0, 1), (1, 0)):
                        ins = mm(ps[:, t, :], (ckhi, cklo)[a][:, k, t * P:(t + 1) * P],
                                 wv((whi, wlo)[b], B_UKV + k)[:, :, NOPE:P],
                                 start=k == 0 and a + b == 0, stop=k == KKV - 1 and a == 1)
                        if t == NT - 1 and k == 0 and a == 1:
                            ins.then_inc(w_used, 1)
                if t < NT - 1:
                    ins.then_inc(pj, 1)
            ins.then_inc(w_used, 1)

            def gate_and_branch(br, i, p, gbank, ybank, g):
                ng, lg, _ = block(B_MG + 16 * br + 2 * p, i)
                ny, ly, _ = block(B_MG + 16 * br + 2 * p + 1, i)

                def fill(lo, hi):
                    for m in range(lo, hi):
                        if m == 0:
                            pe.wait_ge(w_lo, ng + 1)
                            wait(pe, sg_done, g)
                        if m == 24:
                            pe.wait_ge(w_lo, ny + 1)
                            pe.wait_ge(os_lo, br + 1)
                            wait(pe, mg_done, g)
                        if m < 24:
                            ins = product(m, lg, ps[:, gbank, :], lambda k: xhi[:, k, :], lambda k: xlo[:, k, :], 23)
                        else:
                            ins = product(m - 24, ly, ps[:, ybank, :], lambda k: ohi[:, k, :],
                                          lambda k: olo[:, k, :], 11)
                        if m in (23, 35):
                            ins.then_inc(w_used, 1)
                return fill

            pe.wait_ge(ev, E_ALL)
            pe.wait_ge(kr, 2)
            cuts = [0, 5, 10, 14, 19, 23, 28, 32, 36]
            for kind, br, j0 in (("mla", 0, J_MLA), ("fox", 1, J_FOX)):
                def two_heads(i):
                    for p in range(2):
                        head(kind, i * 2 + (j0 + p), p,
                             gate_and_branch(br, i, p, 6, 7, i * 2 + (8 * br + p)), cuts)
                if br == 0:
                    two_heads(0)
                with pe.Fori(1 if br == 0 else 0, 4) as i:
                    two_heads(i)
            pe.wait_ge(o_done, J_END)
            with pe.Fori(0, 4) as i:
                for p in range(2):
                    gate_and_branch(2, i, p, 6, (7, 5)[p], i * 2 + (16 + p))(0, 36)
            pe.wait_ge(mg_done, 24)
            pe.wait_ge(sg_done, 24)
            def chunk(k):
                return (lambda t: xhi[:, k, t * P:(t + 1) * P]), (lambda t: xlo[:, k, t * P:(t + 1) * P])
            for k in range(4):
                pe.wait_ge(ms_lo, k + 1)
                pe.wait_ge(w_lo, B_OUT + k + 1)
                for t in range(NT):
                    ins = token_block(B_OUT + k, t, *chunk(k), k == 0, False)
                ins.then_inc(w_used, 1)
            TG2 = TG1 + NT
            finish(B_OUT + 4, [(*chunk(k), ms_lo, k + 1) for k in range(4, KD)], 1)
            turn_tile(1, 3)
            pe.wait_ge(t_lo, TG2 + 4)
            with pe.Fori(0, NF // 2) as i:
                up(B_UP2, NF)(i)
            down(B_DN2, NF, 2)


_INS = ["x", "mem", "positions", "ln1_g", "ln1_b", "ffn1_w_in", "ffn1_w_down", "w_in", "b_gate", "mla_q_norm",
        "mla_w_uq", "mla_kv_norm", "mla_w_ukv", "fox_b_f", "mem_w_kv", "w_br_mla", "w_br_fox", "w_br_mem", "w_out",
        "ln2_g", "ln2_b", "ffn2_w_in", "ffn2_w_down", "ln3_g", "ln3_b"]


def kernel(**inputs):
    import numpy as _np
    import concourse.bacc as _bacc
    from concourse import mybir as _mybir
    from concourse.bass_utils import run_bass_kernel_spmd as _run

    nc = _bacc.Bacc("TRN2", target_bir_lowering=False, num_devices=1)
    arrays, args = {}, []
    for name in _INS:
        a = _np.ascontiguousarray(inputs[name])
        a = a.reshape(a.shape[1:])
        arrays[f"in_{name}_dram"] = a
        args.append(nc.dram_tensor(f"in_{name}_dram", a.shape, _mybir.dt.from_np(a.dtype), kind="ExternalInput").ap())
    arrays["in_consts_dram"] = shape_constants()
    args.append(nc.dram_tensor("in_consts_dram", (P, 8), _mybir.dt.float32, kind="ExternalInput").ap())
    args.append(nc.dram_tensor("out_0_dram", (S, D), _mybir.dt.float32, kind="ExternalOutput").ap())
    layer_program(nc, *args)
    r = _run(nc, [arrays], core_ids=[0])
    return r.results[0]["out_0_dram"].reshape(1, S, D)
```

```python
from contextlib import ExitStack

import numpy as np

import concourse.bass as bass
from concourse import mybir

F32 = mybir.dt.float32
F32R = mybir.dt.float32r
I32 = mybir.dt.int32
ALU = mybir.AluOpType
ACT = mybir.ActivationFunctionType
AX = mybir.AxisListType

P = 128
S, D, M = 512, 1024, 256
KD = D // P
NT = S // P
FF = 2816
NF = FF // P
HEADS, MEM_HEADS = 8, 4
NOPE, ROPE, DV = 64, 32, 64
QK_MLA = NOPE + ROPE
QL, KVL = 384, 256
KQ, KKV = QL // P, KVL // P
FOX_W = 512
ALPHA = 2.0 ** 0.25
LN_EPS, RMS_EPS = 1e-5, 1e-6
NEG = -1e30

C_CQ = 0
C_KPE = QL + KVL
C_FQ = C_KPE + ROPE
C_FK = C_FQ + FOX_W
C_FV = C_FK + FOX_W
C_FLOG = C_FV + FOX_W
C_MQ = C_FLOG + HEADS
C_GATE = C_MQ + 512

RING = 4
B_UP1 = 0
B_DN1 = B_UP1 + 2 * NF
B_MK = B_DN1 + NF
B_MV = B_MK + 4
B_C = B_MV + 4
B_KF = B_C + KQ + KKV
B_MQ = B_KF + 1
B_FQK = B_MQ + 4
B_UQ = B_FQK + 8
B_FV = B_UQ + KQ
B_UKV = B_FV + 2
B_FV2 = B_UKV + KKV
B_MG = B_FV2 + 2
B_OUT = B_MG + 3 * 16
B_UP2 = B_OUT + KD
B_DN2 = B_UP2 + 2 * NF
B_END = B_DN2 + NF

E_MK, E_MV, E_C, E_KF, E_MQ, E_FQK, E_UQ, E_K, E_V, E_FV, E_ALL = 0, 4, 6, 11, 13, 17, 25, 33, 41, 45, 49

J_MEM, J_MLA, J_FOX, J_END = 0, 4, 12, 20
PT_OFF = {False: (0, 512), True: (0, 512, 0, 512)}


def pt_first(j):
    return 2 * j if isinstance(j, int) and j <= J_MLA else j * 4 - 2 * J_MLA


def shape_constants():
    c = np.zeros((P, 8), np.float32)
    half = ROPE // 2
    inv = (10000.0 ** (-np.arange(half, dtype=np.float64) / half)).astype(np.float32)
    c[64:64 + half, 0] = inv
    c[64 + half:96, 0] = inv
    c[64:64 + half, 1] = -1.0
    c[64 + half:96, 1] = 1.0
    c[:, 2] = LN_EPS
    c[:, 3] = RMS_EPS
    c[:, 4] = np.pi / 2
    return c


def layer_program(nc, x, mem, positions, ln1_g, ln1_b, ffn1_w_in, ffn1_w_down, w_in, b_gate,
                  mla_q_norm, mla_w_uq, mla_kv_norm, mla_w_ukv, fox_b_f, mem_w_kv, w_br_mla, w_br_fox,
                  w_br_mem, w_out, ln2_g, ln2_b, ffn2_w_in, ffn2_w_down, ln3_g, ln3_b, consts, out):
    with ExitStack() as ctx:
        base = (nc.sbuf_base + 31) // 32 * 32
        ctx.enter_context(nc.sbuf_tensor("arena", [P, (nc.sbuf_usable_end - base - 64) // 4], F32))
        limit = nc.sbuf_usable_end

        def at(name, shape, dt, offset):
            size = 4
            for s in shape[1:]:
                size *= s
            assert base + offset + size <= limit, (name, base + offset + size, limit)
            return nc.alloc_sbuf_tensor_at(name, shape, dt, offset=base + offset)

        K1 = 1024
        whi = at("whi", [P, RING, 1024], F32R, 0)
        wlo = at("wlo", [P, RING, 1024], F32R, 16 * K1)
        raw = at("raw", [P, RING, 1024], F32, 32 * K1)
        xhi = at("xhi", [P, KD, S], F32R, 48 * K1)
        xlo = at("xlo", [P, KD, S], F32R, 64 * K1)
        X = at("X", [P, NT, D], F32, 80 * K1)
        merged = at("merged", [P, KD, S], F32, 80 * K1)
        A = 96 * K1
        h = at("h", [P, NF, S], F32, A)
        hhi = at("hhi", [P, RING, S], F32R, A + 44 * K1)
        hlo = at("hlo", [P, RING, S], F32R, A + 52 * K1)
        Q = at("Q", [P, HEADS, S], F32, A)
        craw = at("craw", [P, KQ + KKV, S], F32, A)
        csq = at("csq", [P, KQ + KKV, S], F32, A + 40 * K1)
        Kt = at("Kt", [P, HEADS, S], F32, A + 16 * K1)
        mk = at("mk", [P, MEM_HEADS, M], F32, A + 16 * K1)
        cqhi = at("cqhi", [P, KQ, S], F32R, A + 20 * K1)
        cqlo = at("cqlo", [P, KQ, S], F32R, A + 26 * K1)
        V = at("V", [P, NT, 512], F32, A + 32 * K1)
        mv = at("mv", [P, 2, 512], F32, A + 32 * K1)
        rms = at("rms", [P, 2, S], F32, A + 36 * K1)
        FQK = at("FQK", [P, 8, S], F32, A + 40 * K1)
        mhi = at("mhi", [P, KD, S], F32R, A)
        mlo = at("mlo", [P, KD, S], F32R, A + 16 * K1)
        FV = at("FV", [P, NT, 512], F32, A + 56 * K1)
        ckhi = at("ckhi", [P, KKV, S], F32R, A + 56 * K1)
        cklo = at("cklo", [P, KKV, S], F32R, A + 60 * K1)
        ohi = at("ohi", [P, 4, S], F32R, A + 64 * K1)
        olo = at("olo", [P, 4, S], F32R, A + 72 * K1)
        MQ = at("MQ", [P, MEM_HEADS, S], F32, A + 72 * K1)
        mThi = at("mThi", [P, KD, M], F32R, A + 64 * K1)
        mTlo = at("mTlo", [P, KD, M], F32R, A + 72 * K1)
        PB = A + 80 * K1
        stmp = at("stmp", [P, 2, S], F32, PB)
        T = PB + 5 * K1
        pthi = at("pthi", [P, 1024], F32R, T)
        ptlo = at("ptlo", [P, 1024], F32R, T + 4 * K1)
        res = at("res", [P, 2, D], F32, T)
        tabs = at("tabs", [P, 5, S], F32, 80 * K1)
        rtmp = at("rtmp", [P, S], F32, 90 * K1)
        G = T + 8 * K1
        qh = at("qh", [P, S], F32R, G)
        ql = at("ql", [P, S], F32R, G + 2 * K1)
        kh = at("kh", [P, S], F32R, G + 4 * K1)
        kl = at("kl", [P, S], F32R, G + 6 * K1)
        vh = at("vh", [P, 256], F32R, G + 8 * K1)
        vl = at("vl", [P, 256], F32R, G + 9 * K1)
        lng = at("lng", [P, D], F32, G)
        lnb = at("lnb", [P, D], F32, G + 4 * K1)
        Z = G + 10 * K1
        identR = at("identR", [P, P], F32R, Z)
        maskR = at("maskR", [P, P], F32R, Z + 512)
        kf = at("kf", [P, S], F32, Z + 1024)
        sig = at("sig", [P, S], F32, Z + 1024)
        ones = at("ones", [P, P], F32, PB + 4 * K1)
        pos = at("pos", [P, S], I32, G + 8 * K1)
        maskF = at("maskF", [P, P], F32, A)
        ident = at("ident", [P, P], F32, Z + 3072)
        SM = Z + 3584
        cst = at("cst", [P, 8], F32, SM)
        bg = at("bg", [P, 24], F32, SM + 32)
        rms_gain = at("rms_gain_and_forget_bias", [P, 8], F32, SM + 128)
        gq, bf = rms_gain[:, 0:KQ + KKV], rms_gain[:, 5:6]
        moments = at("moments", [P, 16], F32, SM + 160)
        stats = moments[:, 0:12].rearrange("p (a b) -> p a b", b=6)
        mvar, rstd = moments[:, 12:14], moments[:, 14:16]
        nmax = at("nmax", [P, 8], F32, SM + 224)
        rsum = at("rsum", [P, 8], F32, SM + 256)
        rinv = at("rinv", [P, 8], F32, SM + 288)
        prob = [at("prob_even", [P, 1280], F32, PB), at("prob_odd", [P, 1280], F32, SM + 320)]

        ps = ctx.enter_context(nc.psum_tensor("ps", [P, 8, 512], F32))
        spill = nc.dram_tensor("spill_x1", (S, D), F32, kind="Internal").ap()

        def sem(name):
            return ctx.enter_context(nc.semaphore(name))

        w_raw = [sem(f"w_raw{i}") for i in range(RING)]
        w_hi, w_lo = sem("w_hi"), sem("w_lo")
        w_used = sem("w_used")
        c_in, k_in = sem("c_in"), sem("k_in")
        kf_in = sem("kf_in")
        x_in = [sem(f"x_in{t}") for t in range(NT)]
        m_in = sem("m_in")
        g_in = sem("g_in")
        sp_out = sem("sp_out")
        f_rows = sem("f_rows")
        y_out = sem("y_out")
        pool_c = sem("pool_c")
        act_c = sem("act_c")
        t_done = sem("t_done")
        t_hi, t_lo = sem("t_hi"), sem("t_lo")
        sl_done, h_done = sem("sl_done"), sem("h_done")
        hs_hi, hs_lo = sem("hs_hi"), sem("hs_lo")
        y_done = sem("y_done")
        lnc = sem("lnc")
        ln_sd = sem("ln_sd")
        ev = sem("ev")
        pj = sem("pj")
        sq_done, ss_done = sem("sq_done"), sem("ss_done")
        rm_sd, rm_r = sem("rm_sd"), sem("rm_r")
        cn, cn_hi, cn_lo = sem("cn"), sem("cn_hi"), sem("cn_lo")
        tb_v, tb_s = sem("tb_v"), sem("tb_s")
        fg_v, fg_s = sem("fg_v"), sem("fg_s")
        rp = sem("rp")
        kr = sem("kr")
        st_hi, st_lo = sem("st_hi"), sem("st_lo")
        sv_hi, sv_lo = sem("sv_hi"), sem("sv_lo")
        s_done = sem("s_done")
        mx_done, ex_done = sem("mx_done"), sem("ex_done")
        rc_done, pn_done = sem("rc_done"), sem("pn_done")
        pt_done = sem("pt_done")
        ph_done, pl_done = sem("ph_done"), sem("pl_done")
        pv_done, o_done = sem("pv_done"), sem("o_done")
        os_hi, os_lo = sem("os_hi"), sem("os_lo")
        sg_done, mt_done, mg_done = sem("sg_done"), sem("mt_done"), sem("mg_done")
        ms_hi, ms_lo = sem("ms_hi"), sem("ms_lo")

        def wait(eng, s, v):
            if not isinstance(v, int) or v > 0:
                eng.wait_ge(s, v)

        def apart(eng, *held):
            if any(not isinstance(v, int) for v in held):
                eng.wait_ge(c_in, 16)

        def row(t, i):
            if isinstance(i, int):
                return t[:, i, :]
            return t[:, bass.ds(i, 1), :].rearrange("p a n -> p (a n)")

        def rows(t, lo, hi, i):
            if isinstance(i, int):
                return t[lo:hi, i, :]
            return t[lo:hi, bass.ds(i, 1), :].rearrange("p a n -> p (a n)")

        def wcols(n):
            if n == B_KF:
                return lambda t: t[:, n % RING, :].rearrange("p (k m) -> p k m", m=P)[:, :, 64:104]
            if B_UQ <= n < B_UQ + KQ:
                return lambda t: t[:, n % RING, 0:768]
            if B_MG <= n < B_OUT and (n - B_MG) % 2:
                return lambda t: t[:, n % RING, 0:512]
            return lambda t: t[:, n % RING, :]

        def block(base_n, i=0, per=RING):
            if isinstance(i, int):
                n = base_n + per * i
                return n, n, n // RING
            return i * per + base_n, base_n, i * (per // RING) + base_n // RING

        blk = ctx.enter_context(nc.Block())

        @blk.sync
        def _(sp):
            def load(b, src):
                n, like, lap = b
                apart(sp, n)
                wait(sp, w_lo, n - RING + 1)
                dst = wcols(like)(raw)
                if len(src.shape) == 3 and len(dst.shape) == 2:
                    dst = dst.rearrange("p (k m) -> p k m", k=src.shape[1])
                sp.dma_start(dst, src).then_inc(w_raw[like % RING], 16)

            def kcols(w, col, width=P):
                wv = w.rearrange("(k p) n -> p k n", p=P)
                return wv[:, :, bass.ds(col, width)] if not isinstance(col, int) else wv[:, :, col:col + width]

            def up(b0, w):
                def body(i):
                    for j in range(4):
                        f_off = (j // 2) * P + (j % 2) * FF
                        load(block(b0 + j, i), kcols(w, i * (2 * P) + f_off))
                return body

            def down_rows(w, r):
                if isinstance(r, int):
                    return w[r:r + P, :]
                return w[bass.ds(r, P), :]

            def down(b0, w):
                def body(i):
                    for j in range(4):
                        load(block(b0 + j, i), down_rows(w, i * (4 * P) + j * P))
                return body

            def ln_params(g, b):
                sp.dma_start(lng[:], g.partition_broadcast(P)).then_inc(g_in, 16)
                sp.dma_start(lnb[:], b.partition_broadcast(P)).then_inc(g_in, 16)

            xv = x.rearrange("(t p) d -> t p d", p=P)
            sp.dma_start(cst[:], consts).then_inc(c_in, 16)
            first = up(B_UP1, ffn1_w_in)
            for t in range(2):
                sp.dma_start(X[:, t, :], xv[t]).then_inc(x_in[t], 16)
            load(block(B_UP1), kcols(ffn1_w_in, 0))
            for t in range(2, NT):
                sp.dma_start(X[:, t, :], xv[t]).then_inc(x_in[t], 16)
            for j in range(1, 4):
                load(block(B_UP1 + j), kcols(ffn1_w_in, (j // 2) * P + (j % 2) * FF))
            memv = mem.rearrange("(t p) d -> p t d", p=P)
            sp.dma_start(res[:, :, :], memv).then_inc(m_in, 16)
            with nc.allow_non_contiguous_dma(reason="small per-feature parameters"):
                sp.dma_start(bg[:], b_gate.rearrange("(c p) -> p c", p=P)).then_inc(k_in, 16)
                sp.dma_start(gq[:, 0:KQ], mla_q_norm.rearrange("(c p) -> p c", p=P)).then_inc(k_in, 16)
                sp.dma_start(gq[:, KQ:KQ + KKV], mla_kv_norm.rearrange("(c p) -> p c", p=P)).then_inc(k_in, 16)
                sp.dma_start(bf[0:HEADS, :], fox_b_f.rearrange("(p a) -> p a", a=1)).then_inc(k_in, 16)
            sp.dma_start(pos[64:96, :], positions.partition_broadcast(ROPE)).then_inc(k_in, 16)
            ln_params(ln1_g, ln1_b)
            with sp.Fori(1, NF // 2) as i:
                first(i)
            dn1 = down(B_DN1, ffn1_w_down)
            with sp.Fori(0, NF // 4) as i:
                dn1(i)
            for f in range(NF // 4 * 4, NF):
                load(block(B_DN1 + f), down_rows(ffn1_w_down, f * P))
            for j in range(4):
                load(block(B_MK + j), kcols(mem_w_kv, j * P))
            mkv = mem_w_kv.rearrange("(k p) n -> p k n", p=P)
            for j in range(4):
                load(block(B_MV + j), mkv[:, 2 * j:2 * j + 2, 512:1024])
            for t in range(NT):
                wait(sp, lnc, 6 * (t + 1))
                sp.dma_start(spill[t * P:(t + 1) * P, :], X[:, t, :]).then_inc(sp_out, 16)
                if t < 3:
                    load(block(B_C + t), kcols(w_in, C_CQ + t * P))
            for j in range(3, KQ + KKV):
                load(block(B_C + j), kcols(w_in, C_CQ + j * P))
            n, like, lap = block(B_KF)
            wait(sp, w_lo, n - RING + 1)
            kfv = raw[:, n % RING, :].rearrange("p (k m) -> p k m", m=P)
            sp.dma_start(kfv[:, :, 64:96], kcols(w_in, C_KPE, ROPE)).then_inc(w_raw[n % RING], 16)
            with nc.allow_non_contiguous_dma(reason="eight columns"):
                sp.dma_start(kfv[:, :, 96:104], kcols(w_in, C_FLOG, HEADS)).then_inc(kf_in, 16)
            for j in range(4):
                load(block(B_MQ + j), kcols(w_in, C_MQ + j * P))
            for j in range(8):
                load(block(B_FQK + j), kcols(w_in, C_FQ + j * P))
            for k in range(KQ):
                load(block(B_UQ + k), mla_w_uq[k * P:(k + 1) * P, :])
            winv = w_in.rearrange("(k p) n -> p k n", p=P)
            for j in range(2):
                load(block(B_FV + j), winv[:, 2 * j:2 * j + 2, C_FV:C_FV + 512])
            for k in range(KKV):
                load(block(B_UKV + k), mla_w_ukv[k * P:(k + 1) * P, :])
            for j in range(2, 4):
                load(block(B_FV2 + j - 2), winv[:, 2 * j:2 * j + 2, C_FV:C_FV + 512])
            wait(sp, fg_v, 7)
            wait(sp, rp, 12)
            for r0, s0 in ((64, 1), (65, 2), (66, 0), (67, 0), (96, 0), (97, 0), (98, 3), (99, 4)):
                sp.dma_start(Kt[r0:r0 + 1, :, :], tabs[0:HEADS, s0, :]).then_inc(f_rows, 16)
            for b, (w_br, gate) in enumerate(((w_br_mem, 2), (w_br_mla, 0), (w_br_fox, 1))):
                for d in range(KD):
                    load(block(B_MG + 16 * b + 2 * d), kcols(w_in, C_GATE + gate * D + d * P))
                    load(block(B_MG + 16 * b + 2 * d + 1), kcols(w_br, d * P))
            for k in range(4):
                load(block(B_OUT + k), w_out[k * P:(k + 1) * P, :])
            wait(sp, ms_lo, KD)
            wait(sp, sp_out, 16 * NT)
            for t in range(NT):
                sp.dma_start(X[:, t, :], spill[t * P:(t + 1) * P, :]).then_inc(x_in[t], 16)
            ln_params(ln2_g, ln2_b)
            for k in range(4, KD):
                load(block(B_OUT + k), w_out[k * P:(k + 1) * P, :])
            second = up(B_UP2, ffn2_w_in)
            for i in range(2):
                second(i)
            wait(sp, lnc, 6 * 2 * NT)
            ln_params(ln3_g, ln3_b)
            with sp.Fori(2, NF // 2) as i:
                second(i)
            dn2 = down(B_DN2, ffn2_w_down)
            with sp.Fori(0, NF // 4) as i:
                dn2(i)
            for f in range(NF // 4 * 4, NF):
                load(block(B_DN2 + f), down_rows(ffn2_w_down, f * P))
            for t in range(NT):
                wait(sp, lnc, 6 * (2 * NT + t + 1))
                sp.dma_start(out[t * P:(t + 1) * P, :], X[:, t, :]).then_inc(y_out, 16)
            sp.wait_ge(y_out, 16 * NT)

        @blk.gpsimd
        def _(pool):
            nc.gpsimd.memset(ident[:], 0.0).then_inc(pool_c, 1)
            nc.gpsimd.memset(maskF[:], 0.0).then_inc(pool_c, 1)
            nc.gpsimd.memset(ones[:], 1.0).then_inc(pool_c, 1)
            pool.wait_ge(pool_c, 3)
            nc.gpsimd.affine_select(out=ident[:], in_=ident[:], compare_op=ALU.not_equal, fill=1.0, base=0,
                                    pattern=[[-1, P]], channel_multiplier=1).then_inc(pool_c, 1)
            nc.gpsimd.affine_select(out=maskF[:], in_=maskF[:], compare_op=ALU.is_ge, fill=NEG, base=0,
                                    pattern=[[-1, P]], channel_multiplier=1).then_inc(pool_c, 1)

            def low(b):
                n, like, lap = b
                v = wcols(like)
                pool.wait_ge(w_hi, n + 1)
                nc.gpsimd.tensor_tensor(v(wlo), v(raw), v(whi).bitcast(F32), ALU.subtract).then_inc(w_lo, 1)

            for n in range(RING):
                low(block(n))
            with pool.Fori(1, B_MV // RING + 1) as i:
                for j in range(RING):
                    low(block(j, i))
            for n in range((B_MV // RING + 1) * RING, B_MG + 3):
                low(block(n))
            with pool.Fori(0, 11) as i:
                for j in range(RING):
                    low(block(B_MG + 3 + j, i))
            for n in range(B_MG + 47, B_OUT + 3):
                low(block(n))
            with pool.Fori(0, (B_END - B_OUT - 3) // RING) as i:
                for j in range(RING):
                    low(block(B_OUT + 3 + j, i))
            for n in range(B_OUT + 3 + (B_END - B_OUT - 3) // RING * RING, B_END):
                low(block(n))

        @blk.scalar
        def _(act):
            def high(b):
                n, like, lap = b
                v = wcols(like)
                act.wait_ge(w_raw[like % RING], lap * 16 + 16)
                if like == B_KF:
                    act.wait_ge(kf_in, 16)
                wait(act, w_used, n - RING + 1)
                nc.scalar.activation(v(whi), v(raw), ACT.Copy).then_inc(w_hi, 1)

            def turned_hi(g, t):
                act.wait_ge(t_done, g + 1)
                nc.scalar.activation(xhi[:, :, t * P:(t + 1) * P],
                                     ps[:, 2 * t:2 * t + 2, :].rearrange("p a (k m) -> p (a k) m", m=P),
                                     ACT.Copy).then_inc(t_hi, 1)

            def sd(q):
                act.wait_ge(lnc, 6 * q + 3)
                nc.scalar.activation(rstd[:, q % 2:q % 2 + 1], mvar[:, 1:2], ACT.Sqrt,
                                     bias=cst[:, 2:3]).then_inc(ln_sd, 1)

            def up(b0, h0):
                def body(i):
                    for p in range(2):
                        na, la, _ = block(b0 + 2 * p, i)
                        f = i * 2 + p
                        act.wait_ge(w_used, na + 1)
                        wait(act, h_done, f + h0 - 1)
                        nc.scalar.activation(stmp[:, p, :], ps[:, 2 * p, :], ACT.Silu).then_inc(sl_done, 1)
                        high(block(b0 + 2 * p + 4, i))
                        high(block(b0 + 2 * p + 5, i))
                return body

            def hidden_hi(f, slot, h0, after=None):
                apart(act, f)
                act.wait_ge(h_done, f + h0 + 1)
                if after is not None:
                    act.wait_ge(w_used, after)
                nc.scalar.activation(hhi[:, slot, :], row(h, f), ACT.Copy).then_inc(hs_hi, 1)

            def ffn(b0, b1, h0, start):
                body = up(b0, h0)
                with act.Fori(start, NF // 2 - 1) as i:
                    body(i)
                for f in range(RING):
                    hidden_hi(f, f, h0)
                body(NF // 2 - 1)
                with act.Fori(0, 4) as i:
                    for j in range(RING):
                        n, _, _ = block(b1 + j, i)
                        hidden_hi(i * RING + (j + RING), j, h0, after=n + 1)
                        high(block(b1 + j + RING, i))
                for f in range(16, 18):
                    hidden_hi(f + RING, f % RING, h0, after=b1 + f + 1)
                    high(block(b1 + f + RING))

            def evac(dst, src, done_sem, done, **kw):
                act.wait_ge(done_sem, done)
                nc.scalar.activation(dst, src, ACT.Identity if kw else ACT.Copy, **kw).then_inc(ev, 1)

            act.wait_ge(pool_c, 5)
            nc.scalar.activation(identR[:], ident[:], ACT.Copy).then_inc(act_c, 1)
            nc.scalar.activation(maskR[:], maskF[:], ACT.Copy).then_inc(act_c, 1)
            act.wait_ge(c_in, 16)
            turned_hi(0, 0); turned_hi(1, 1)
            high(block(0))
            turned_hi(2, 2); turned_hi(3, 3)
            for n in range(1, RING):
                high(block(n))
            up(B_UP1, 0)(0)
            for kb in range(2):
                act.wait_ge(t_done, NT + kb + 1)
                nc.scalar.activation(mThi[:, :, kb * P:(kb + 1) * P],
                                     ps[:, 4 + 2 * kb:6 + 2 * kb, :].rearrange("p a (k m) -> p (a k) m", m=P),
                                     ACT.Copy).then_inc(t_hi, 1)
            ffn(B_UP1, B_DN1, 0, 1)
            TG1 = NT + 2
            def two_tiles(L, g, b0):
                sd(NT * L); sd(NT * L + 1)
                turned_hi(g, 0)
                high(block(b0))
                turned_hi(g + 1, 1)
                for n in range(b0 + 1, b0 + 4):
                    high(block(n))
                sd(NT * L + 2)

            two_tiles(0, TG1, B_MK)
            for j in range(4):
                evac(mk[:, j, :], ps[:, j, 0:M], w_used, B_MK + j + 1)
                high(block(B_MK + j + 4))
                if j == 1:
                    turned_hi(TG1 + 2, 2)
                    sd(3)
            for j in range(4):
                high(block(B_MV + j + 4))
                if j == 1:
                    turned_hi(TG1 + 3, 3)
            for kb in range(2):
                evac(mv[:, kb, :], ps[:, kb, :], w_used, B_MV + 4)
            act.wait_ge(k_in, 16 * 5)
            nc.scalar.activation(bg[:], bg[:], ACT.Copy, scale=0.5)
            for j in range(KQ + KKV):
                evac(craw[:, j, :], ps[:, j + 2, :], w_used, B_C + j + 1)
                high(block(B_C + j + 4))
                if j == 3:
                    act.wait_ge(tb_v, 8)
                    nc.scalar.activation(tabs[64:96, 2, :], tabs[64:96, 0, :], ACT.Sin,
                                         scale=cst[64:96, 1:2]).then_inc(tb_s, 1)
                    nc.scalar.activation(tabs[64:96, 1, :], tabs[64:96, 0, :], ACT.Abs).then_inc(tb_s, 1)
                    act.wait_ge(tb_s, 2)
                    nc.scalar.activation(tabs[64:96, 3, :], tabs[64:96, 1, :], ACT.Sin, scale=-1.0,
                                         bias=cst[64:96, 4:5]).then_inc(tb_s, 1)
            evac(kf[64:96, :], ps[0:ROPE, 7, :], w_used, B_KF + 1)
            evac(kf[0:HEADS, :], ps[32:32 + HEADS, 7, :], w_used, B_KF + 1, bias=bf[0:HEADS, :])
            high(block(B_KF + 4))
            act.wait_ge(ev, E_KF + 2)
            nc.scalar.activation(tabs[0:HEADS, 0, :], kf[0:HEADS, :], ACT.Abs).then_inc(fg_s, 1)
            act.wait_ge(fg_s, 1)
            nc.scalar.activation(tabs[0:HEADS, 1, :], tabs[0:HEADS, 0, :], ACT.Exp, scale=-1.0).then_inc(fg_s, 1)
            act.wait_ge(fg_s, 2)
            nc.scalar.activation(tabs[0:HEADS, 2, :], tabs[0:HEADS, 1, :], ACT.Ln, bias=1.0).then_inc(fg_s, 1)

            def memory_query(j):
                evac(MQ[:, j, :], ps[:, 4 + j, :], w_used, B_MQ + j + 1)
                high(block(B_MQ + j + 4))

            def stage(kind, j, hd, c, p):
                apart(act, j)
                wait(act, s_done, j * 4)
                if isinstance(j, int) and j == J_FOX:
                    act.wait_ge(f_rows, 16 * 8)
                if kind == "mem":
                    act.wait_ge(ev, E_MQ + hd + 1)
                    nc.scalar.activation(qh[:], MQ[:, hd, :], ACT.Copy, scale=128.0 ** -0.5)
                    nc.scalar.activation(kh[:, 0:M], mk[:, hd, :], ACT.Copy).then_inc(st_hi, 1)
                elif kind == "mla":
                    nc.scalar.activation(qh[0:QK_MLA, :], rows(Q, 0, QK_MLA, hd), ACT.Copy,
                                         scale=float(QK_MLA) ** -0.5)
                    nc.scalar.activation(kh[0:NOPE, :], rows(Kt, 0, NOPE, hd), ACT.Copy).then_inc(st_hi, 1)
                else:
                    nc.scalar.activation(qh[0:64, :], rows(FQK, 64 * p, 64 * p + 64, c), ACT.Copy, scale=0.125)
                    nc.scalar.activation(kh[0:64, :], rows(FQK, 64 * p, 64 * p + 64, c + 4), ACT.Copy)
                    nc.scalar.activation(qh[64:68, :], rows(Kt, 64, 68, hd), ACT.Copy)
                    nc.scalar.activation(kh[64:68, :], rows(Kt, 96, 100, hd), ACT.Copy).then_inc(st_hi, 1)

            def v_source(kind, hd, p):
                if kind == "mem":
                    return mv[:, :, hd * P:(hd + 1) * P], 2
                t = V if kind == "mla" else FV
                if isinstance(hd, int):
                    return t[:, :, hd * DV:(hd + 1) * DV], 4
                return t[:, :, bass.ds(hd * DV, DV)], 4

            def exponentials(kind, j, p, qt):
                nk = M if kind == "mem" else P * (qt + 1)
                off = M * qt if kind == "mem" else P * qt * (qt + 1) // 2
                act.wait_ge(mx_done, j * 4 + qt + 1)
                nc.scalar.activation(prob[p][:, off:off + nk], ps[:, qt % 2, 0:nk], ACT.Exp,
                                     bias=nmax[:, 4 * p + qt:4 * p + qt + 1],
                                     accum_out=rsum[:, 4 * p + qt:4 * p + qt + 1]).then_inc(ex_done, 1)

            def head(kind, J, hd, pair, p, more, nxt, a, b, between=None):
                j = J(0)
                src, nb = v_source(kind, hd, p)
                apart(act, j)
                wait(act, pv_done, j)
                nc.scalar.activation(vh[:].rearrange("p (k m) -> p k m", k=nb), src, ACT.Copy).then_inc(sv_hi, 1)
                kbs = 2 if kind == "mem" else 4
                for kb in range(NT):
                    if kb < kbs:
                        w = S if kind == "mem" else S - P * kb
                        off = PT_OFF[kind != "mem"][kb]
                        act.wait_ge(pt_done, pt_first(j) + kb + 1)
                        nc.scalar.activation(pthi[:, off:off + w], ps[:, 2 + kb % 2, 0:w],
                                             ACT.Copy).then_inc(ph_done, 1)
                    if more:
                        exponentials(kind, J(1), 1 - p, kb)
                    if between is not None:
                        between(kb)
                if nxt is not None:
                    stage(*nxt)
                a()
                apart(act, j)
                act.wait_ge(pv_done, j + 1)
                if kind == "mem":
                    nc.scalar.activation(MQ[:, hd, :], ps[:, 4 + p, :], ACT.Copy).then_inc(o_done, 1)
                else:
                    t = Q if kind == "mla" else FQK
                    nc.scalar.activation(rows(t, 64 * p, 64 * p + 64, pair), ps[0:64, 4 + p, :],
                                         ACT.Copy).then_inc(o_done, 1)
                b()

            memory_query(0)
            stage("mem", 0, 0, 0, 0)
            for c, width in enumerate((QL, KVL)):
                act.wait_ge(ss_done, c + 1)
                nc.scalar.activation(rms[:, c, :], ps[:, 2 + c, :], ACT.Sqrt, scale=1.0 / width,
                                     bias=cst[:, 3:4]).then_inc(rm_sd, 1)
            memory_query(1)
            for qt in range(2):
                exponentials("mem", 0, 0, qt)
            memory_query(2)
            for qt in range(2, NT):
                exponentials("mem", 0, 0, qt)
            stage("mem", 1, 1, 0, 1)
            memory_query(3)
            for hd in range(MEM_HEADS):
                n = B_FQK + 2 * hd

                def fill_a():
                    evac(FQK[:, 2 * hd, :], ps[:, 6, :], w_used, n + 1)
                    high(block(n + 4))

                def fill_b():
                    evac(FQK[:, 2 * hd + 1, :], ps[:, 7, :], w_used, n + 2)
                    high(block(n + 5))
                    if hd in (1, 2):
                        for c in (range(KQ) if hd == 1 else range(KQ, KQ + KKV)):
                            act.wait_ge(cn, c + 1)
                            dst = cqhi[:, c, :] if c < KQ else ckhi[:, c - KQ, :]
                            nc.scalar.activation(dst, craw[:, c, :], ACT.Copy).then_inc(cn_hi, 1)
                nxt = ("mem", hd + 2, hd + 2, 0, hd % 2) if hd + 2 < MEM_HEADS else None
                head("mem", lambda d: hd + d, hd, None, hd % 2, hd + 1 < MEM_HEADS, nxt, fill_a, fill_b)

            def split_hi(src, br, c):
                act.wait_ge(o_done, (MEM_HEADS, J_FOX, J_END)[br])
                if br:
                    act.wait_ge(w_used, B_MG + 16 * br)
                nc.scalar.activation(ohi[:, c, :], src[:, c, :], ACT.Copy).then_inc(os_hi, 1)

            for hd in range(HEADS):
                evac(Q[0:QK_MLA, hd, :], ps[0:QK_MLA, hd % 4, :],
                     *((pj, hd + 1) if hd < 7 else (w_used, B_UQ + KQ)))
            for n in range(B_UQ, B_UQ + KQ):
                high(block(n + 4))
            nc.scalar.activation(kh[64:96, :], kf[64:96, :], ACT.Copy).then_inc(kr, 1)
            for n in (B_FV, B_FV + 1):
                high(block(n + 4))
            for c in range(4):
                split_hi(MQ, 0, c)
            for hd in range(HEADS):
                evac(Kt[0:NOPE, hd, :], ps[0:NOPE, hd % 4, :], pj, HEADS + hd)
            for t in range(NT):
                evac(V[:, t, :], ps[:, t, :], *((pj, 2 * HEADS + t) if t < 3 else (w_used, B_UKV + KKV)))
            act.wait_ge(rp, 12)
            act.wait_ge(ev, E_V + NT)
            stage("mla", J_MLA, 0, 0, 0)
            for n in (B_UKV, B_UKV + 1, B_FV2):
                high(block(n + 4))
            for qt in range(NT):
                exponentials("mla", J_MLA, 0, qt)
            stage("mla", J_MLA + 1, 1, 0, 1)
            for t in (2, 0, 3, 1):
                evac(FV[:, t, :], ps[:, 4 + t, :], w_used, B_FV2 + 2)
            high(block(B_FV2 + 5))
            act.wait_ge(kr, 2)

            def gate(br, n, d, g):
                apart(act, g)
                act.wait_ge(w_used, n + 1)
                wait(act, mg_done, g)
                bank = 6
                bcol = (2, 0, 1)[br] * 8
                b_ap = bg[:, bcol + d:bcol + d + 1] if isinstance(d, int) else bg[:, bass.ds(d + bcol, 1)]
                nc.scalar.activation(sig[:], ps[:, bank, :], ACT.Tanh, scale=0.5, bias=b_ap).then_inc(sg_done, 1)

            def split_mla(kb):
                for c in ((0,), (1,), (2, 3), ())[kb]:
                    split_hi(Q, 1, c)

            def branch_heads(kind, br, j0):
                def body(i, last=False):
                    for p in range(2):
                        hd = i * 2 + p
                        n, like, _ = block(B_MG + 16 * br + 2 * p, i)

                        def fill_a():
                            gate(br, n, hd, i * 2 + (8 * br + p))
                            high(block(B_MG + 16 * br + 2 * p + 4, i))

                        def fill_b():
                            high(block(B_MG + 16 * br + 2 * p + 5, i))
                        if not last:
                            nxt = (kind, i * 2 + (j0 + p + 2), i * 2 + (p + 2), i + 1, p)
                        else:
                            nxt = ("fox", J_FOX + p, p, 0, p) if kind == "mla" else None
                        first = isinstance(i, int) and i == 0 and p == 0
                        head(kind, lambda d: i * 2 + (j0 + p + d), hd, i, p, kind == "mla" or not (last and p == 1),
                             nxt, fill_a, fill_b, split_mla if first and br == 1 else None)
                body(0)
                with act.Fori(1, 3) as i:
                    body(i)
                body(3, True)

            act.wait_ge(ev, E_ALL)

            branch_heads("mla", 0, J_MLA)
            branch_heads("fox", 1, J_FOX)
            for c in range(4):
                split_hi(FQK, 2, c)

            def merge(i):
                for p in range(2):
                    n, _, _ = block(B_MG + 32 + 2 * p, i)
                    d, g = i * 2 + p, i * 2 + (16 + p)
                    gate(2, n, d, g)
                    high(block(B_MG + 32 + 2 * p + 4, i))
                    high(block(B_MG + 32 + 2 * p + 5, i))
                    apart(act, d)
                    act.wait_ge(mg_done, g + 1)
                    nc.scalar.activation(row(mhi, d), row(merged, d), ACT.Copy, scale=0.5).then_inc(ms_hi, 1)
            with act.Fori(0, 3) as i:
                merge(i)
            merge(3)
            for k in range(4):
                high(block(B_OUT + k + 4))
            TG2 = TG1 + NT
            two_tiles(1, TG2, B_UP2)
            turned_hi(TG2 + 2, 2)
            sd(7)
            turned_hi(TG2 + 3, 3)
            body = up(B_UP2, NF)
            with act.Fori(0, NF // 2 - 1) as i:
                body(i)
            for f in range(RING):
                hidden_hi(f, f, NF)
            body(NF // 2 - 1)
            with act.Fori(0, 4) as i:
                for j in range(RING):
                    n, _, _ = block(B_DN2 + j, i)
                    hidden_hi(i * RING + (j + RING), j, NF, after=n + 1)
                    high(block(B_DN2 + j + RING, i))
            for f in range(16, 18):
                hidden_hi(f + RING, f % RING, NF, after=B_DN2 + f + 1)
                high(block(B_DN2 + f + RING))
            for q in range(2 * NT, 3 * NT):
                sd(q)

        @blk.vector
        def _(dve):
            def turned_lo(g, t):
                dve.wait_ge(t_hi, g + 1)
                nc.vector.tensor_tensor(xlo[:, :, t * P:(t + 1) * P],
                                        ps[:, 2 * t:2 * t + 2, :].rearrange("p a (k m) -> p (a k) m", m=P),
                                        xhi[:, :, t * P:(t + 1) * P].bitcast(F32), ALU.subtract).then_inc(t_lo, 1)

            def norm(q):
                t = q % NT
                r = res[:, q % 2, :]
                yv = ps[:, 2 * t:2 * t + 2, :].rearrange("p a n -> p (a n)")
                if t < NT - 1:
                    dve.wait_ge(y_done, (NT - 1) * (q // NT) + t + 1)
                else:
                    dve.wait_ge(w_used, (B_MK, B_UP2, B_END)[q // NT])
                dve.wait_ge(x_in[t], 32 if q >= NT else 16)
                dve.wait_ge(g_in, 32 * (q // NT + 1))
                wait(dve, lnc, 6 * q)
                nc.vector.scalar_tensor_tensor(r, X[:, t, :], ALPHA, yv, ALU.mult, ALU.add).then_inc(lnc, 1)
                dve.wait_ge(lnc, 6 * q + 1)
                nc.vector.bn_stats(stats[:, 0, :], r[:, 0:512])
                nc.vector.bn_stats(stats[:, 1, :], r[:, 512:1024]).then_inc(lnc, 1)
                dve.wait_ge(lnc, 6 * q + 2)
                nc.vector.bn_aggr(mvar, moments[:, 0:12]).then_inc(lnc, 1)
                dve.wait_ge(ln_sd, q + 1)
                nc.vector.reciprocal(rstd[:, q % 2:q % 2 + 1], rstd[:, q % 2:q % 2 + 1]).then_inc(lnc, 1)
                nc.vector.scalar_tensor_tensor(r, r, mvar[:, 0:1], lng[:], ALU.subtract, ALU.mult).then_inc(lnc, 1)
                dve.wait_ge(lnc, 6 * q + 5)
                nc.vector.scalar_tensor_tensor(X[:, t, :], r, rstd[:, q % 2:q % 2 + 1], lnb[:], ALU.mult,
                                               ALU.add).then_inc(lnc, 1)

            def up(b0, h0):
                def body(i):
                    for p in range(2):
                        nb, _, _ = block(b0 + 2 * p + 1, i)
                        f = i * 2 + p
                        dve.wait_ge(sl_done, f + h0 + 1)
                        dve.wait_ge(w_used, nb + 1)
                        nc.vector.scalar_tensor_tensor(row(h, f), stmp[:, p, :], 0.5, ps[:, 2 * p + 1, :],
                                                       ALU.mult, ALU.mult).then_inc(h_done, 1)
                return body

            def hidden_lo(f, slot, h0):
                dve.wait_ge(hs_hi, f + h0 + 1)
                nc.vector.tensor_tensor(hlo[:, slot, :], row(h, f), hhi[:, slot, :].bitcast(F32),
                                        ALU.subtract).then_inc(hs_lo, 1)

            def ffn(b0, b1, h0, start):
                body = up(b0, h0)
                with dve.Fori(start, NF // 2 - 1) as i:
                    body(i)
                for f in range(RING):
                    hidden_lo(f, f, h0)
                body(NF // 2 - 1)
                with dve.Fori(0, 4) as i:
                    for j in range(RING):
                        hidden_lo(i * RING + (j + RING), j, h0)
                for f in range(20, NF):
                    hidden_lo(f, f % RING, h0)

            for t in range(NT):
                turned_lo(t, t)
            up(B_UP1, 0)(0)
            for kb in range(2):
                dve.wait_ge(t_hi, NT + kb + 1)
                nc.vector.tensor_tensor(mTlo[:, :, kb * P:(kb + 1) * P],
                                        ps[:, 4 + 2 * kb:6 + 2 * kb, :].rearrange("p a (k m) -> p (a k) m", m=P),
                                        mThi[:, :, kb * P:(kb + 1) * P].bitcast(F32), ALU.subtract).then_inc(t_lo, 1)
            ffn(B_UP1, B_DN1, 0, 1)
            TG1 = NT + 2
            def layer_norm(L, g):
                norm(NT * L); norm(NT * L + 1); turned_lo(g, 0); turned_lo(g + 1, 1)
                norm(NT * L + 2); norm(NT * L + 3); turned_lo(g + 2, 2); turned_lo(g + 3, 3)

            layer_norm(0, TG1)
            dve.wait_ge(sp_out, 16 * NT)
            dve.wait_ge(k_in, 16 * 5)
            R = slice(64, 96)
            two_pi = 2.0 * np.pi
            parts, rest = [], two_pi
            for bits in (5, 13, 21):
                c = float(np.round(rest * 2.0 ** bits) / 2.0 ** bits)
                parts.append(c)
                rest -= c
            parts.append(float(np.float32(rest)))
            magic = float(1.5 * 2 ** 23)
            nc.vector.tensor_scalar(tabs[R, 0, :], pos[R, :], cst[R, 0:1], None, ALU.mult).then_inc(tb_v, 1)
            dve.wait_ge(tb_v, 1)
            nc.vector.tensor_scalar(tabs[R, 1, :], tabs[R, 0, :], 1.0 / two_pi, magic, ALU.mult, ALU.add).then_inc(tb_v, 1)
            dve.wait_ge(tb_v, 2)
            nc.vector.tensor_scalar(tabs[R, 1, :], tabs[R, 1, :], magic, None, ALU.subtract).then_inc(tb_v, 1)
            for n, c in enumerate(parts):
                dve.wait_ge(tb_v, 3 + n)
                nc.vector.scalar_tensor_tensor(tabs[R, 0, :], tabs[R, 1, :], -c, tabs[R, 0, :], ALU.mult,
                                               ALU.add).then_inc(tb_v, 1)
            dve.wait_ge(tb_v, 7)
            nc.vector.tensor_scalar(tabs[R, 0, :], tabs[R, 0, :], 3.1415925, -3.1415925, ALU.min, ALU.max).then_inc(tb_v, 1)
            dve.wait_ge(h_done, NF)
            for c in range(KQ + KKV):
                dve.wait_ge(ev, E_C + c + 1)
                nc.vector.tensor_tensor(csq[:, c, :], craw[:, c, :], craw[:, c, :], ALU.mult).then_inc(sq_done, 1)
            for n, (a, b) in enumerate(((0, 1), (3, 4), (0, 2))):
                dve.wait_ge(sq_done, KQ + KKV + (n if n == 2 else 0))
                nc.vector.tensor_tensor(csq[:, a, :], csq[:, a, :], csq[:, b, :], ALU.add).then_inc(sq_done, 1)
            swap = [(k + ROPE // 2) % ROPE for k in range(ROPE)]

            def rotate(v, t, sin, cos, before):
                wait(dve, rp, before)
                nc.vector.stream_shuffle(t, v, swap).then_inc(rp, 1)
                dve.wait_ge(rp, before + 1)
                nc.vector.tensor_tensor(t, t, sin, ALU.mult).then_inc(rp, 1)
                nc.vector.tensor_tensor(v, v, cos, ALU.mult).then_inc(rp, 1)
                dve.wait_ge(rp, before + 3)
                nc.vector.tensor_tensor(v, v, t, ALU.add).then_inc(rp, 1)

            dve.wait_ge(tb_s, 3)
            dve.wait_ge(ev, E_KF + 2)
            rotate(kf[R, :], rtmp[R, :], tabs[R, 2, :], tabs[R, 3, :], 0)
            H8 = slice(0, HEADS)
            nc.vector.memset(tabs[H8, 4, :], 0.0).then_inc(fg_v, 1)
            dve.wait_ge(fg_s, 3)
            nc.vector.scalar_tensor_tensor(tabs[H8, 3, :], kf[H8, :], 0.0, tabs[H8, 2, :], ALU.min,
                                           ALU.subtract).then_inc(fg_v, 1)
            dve.wait_ge(fg_v, 2)
            nc.vector.tensor_tensor_scan(tabs[H8, 0, :], tabs[H8, 4, :], tabs[H8, 3, :], 0.0, ALU.add,
                                         ALU.add).then_inc(fg_v, 1)
            dve.wait_ge(fg_v, 3)
            nc.vector.tensor_copy(tabs[H8, 1, :].bitcast(F32R), tabs[H8, 0, :]).then_inc(fg_v, 1)
            dve.wait_ge(fg_v, 4)
            nc.vector.tensor_tensor(tabs[H8, 2, :], tabs[H8, 0, :], tabs[H8, 1, :], ALU.subtract).then_inc(fg_v, 1)
            nc.vector.tensor_scalar(tabs[H8, 3, :], tabs[H8, 1, :], -1.0, None, ALU.mult)
            dve.wait_ge(fg_v, 5)
            nc.vector.tensor_scalar(tabs[H8, 4, :], tabs[H8, 2, :], -1.0, None, ALU.mult).then_inc(fg_v, 1)
            nc.vector.memset(tabs[H8, 0, :], 1.0).then_inc(fg_v, 1)

            def stage(kind, j, hd, c, p):
                dve.wait_ge(st_hi, j + 1)

                def low(dst, src, hi, scale=None):
                    if scale is None:
                        return nc.vector.tensor_tensor(dst, src, hi.bitcast(F32), ALU.subtract)
                    return nc.vector.scalar_tensor_tensor(dst, src, scale, hi.bitcast(F32), ALU.mult, ALU.subtract)
                if kind == "mem":
                    low(ql[:], MQ[:, hd, :], qh[:], 128.0 ** -0.5)
                    low(kl[:, 0:M], mk[:, hd, :], kh[:, 0:M]).then_inc(st_lo, 1)
                elif kind == "mla":
                    low(ql[0:QK_MLA, :], rows(Q, 0, QK_MLA, hd), qh[0:QK_MLA, :], float(QK_MLA) ** -0.5)
                    low(kl[0:NOPE, :], rows(Kt, 0, NOPE, hd), kh[0:NOPE, :]).then_inc(st_lo, 1)
                else:
                    low(ql[0:64, :], rows(FQK, 64 * p, 64 * p + 64, c), qh[0:64, :], 0.125)
                    low(kl[0:64, :], rows(FQK, 64 * p, 64 * p + 64, c + 4), kh[0:64, :]).then_inc(st_lo, 1)

            def v_source(kind, hd):
                if kind == "mem":
                    return mv[:, :, hd * P:(hd + 1) * P], 2
                t = V if kind == "mla" else FV
                if isinstance(hd, int):
                    return t[:, :, hd * DV:(hd + 1) * DV], 4
                return t[:, :, bass.ds(hd * DV, DV)], 4

            def row_max(kind, j, p, qt):
                nk = M if kind == "mem" else P * (qt + 1)
                dve.wait_ge(s_done, j * 4 + qt + 1)
                nc.vector.tensor_reduce(nmax[:, 4 * p + qt:4 * p + qt + 1], ps[:, qt % 2, 0:nk], AX.X, ALU.max,
                                        negate=True).then_inc(mx_done, 1)

            def normalise(kind, j, p, qt):
                nk = M if kind == "mem" else P * (qt + 1)
                off = M * qt if kind == "mem" else P * qt * (qt + 1) // 2
                col = slice(4 * p + qt, 4 * p + qt + 1)
                dve.wait_ge(ex_done, j * 4 + qt + 1)
                nc.vector.reciprocal(rinv[:, col], rsum[:, col]).then_inc(rc_done, 1)
                dve.wait_ge(rc_done, j * 4 + qt + 1)
                nc.vector.tensor_scalar(prob[p][:, off:off + nk], prob[p][:, off:off + nk], rinv[:, col], None,
                                        ALU.mult).then_inc(pn_done, 1)

            def first_softmax(kind, j):
                for qt in range(NT):
                    row_max(kind, j, 0, qt)
                    if qt:
                        normalise(kind, j, 0, qt - 1)
                normalise(kind, j, 0, NT - 1)

            def head(kind, J, hd, p, more, nxt, fill, between=None):
                j = J(0)
                src, nb = v_source(kind, hd)
                dve.wait_ge(sv_hi, j + 1)
                nc.vector.tensor_tensor(vl[:].rearrange("p (k m) -> p k m", k=nb), src,
                                        vh[:].bitcast(F32).rearrange("p (k m) -> p k m", k=nb),
                                        ALU.subtract).then_inc(sv_lo, 1)
                kbs = 2 if kind == "mem" else 4
                for kb in range(NT):
                    if kb < kbs:
                        w = S if kind == "mem" else S - P * kb
                        off = PT_OFF[kind != "mem"][kb]
                        dve.wait_ge(ph_done, pt_first(j) + kb + 1)
                        nc.vector.tensor_tensor(ptlo[:, off:off + w], ps[:, 2 + kb % 2, 0:w],
                                                pthi[:, off:off + w].bitcast(F32), ALU.subtract).then_inc(pl_done, 1)
                    if more:
                        row_max(kind, J(1), 1 - p, kb)
                        if kb:
                            normalise(kind, J(1), 1 - p, kb - 1)
                    if between is not None:
                        between(kb)
                if more:
                    normalise(kind, J(1), 1 - p, NT - 1)
                if nxt is not None:
                    stage(*nxt)
                fill()

            dve.wait_ge(ev, E_MQ + 1)
            stage("mem", 0, 0, 0, 0)
            first_softmax("mem", 0)
            stage("mem", 1, 1, 0, 1)
            for hd in range(MEM_HEADS):
                def reciprocal_rms(part):
                    cols = slice(part * P, (part + 1) * P)
                    dve.wait_ge(rm_sd, hd + 1)
                    nc.vector.reciprocal(rms[:, hd, cols], rms[:, hd, cols]).then_inc(rm_r, 1)

                def fill():
                    if hd in (1, 2):
                        cs = range(KQ) if hd == 1 else range(KQ, KQ + KKV)
                        dve.wait_ge(rm_r, NT * hd)
                        for c in cs:
                            nc.vector.scalar_tensor_tensor(craw[:, c, :], craw[:, c, :], gq[:, c:c + 1],
                                                           rms[:, 0 if c < KQ else 1, :], ALU.mult,
                                                           ALU.mult).then_inc(cn, 1)
                        for c in cs:
                            hi, lo = (cqhi[:, c, :], cqlo[:, c, :]) if c < KQ else (ckhi[:, c - KQ, :], cklo[:, c - KQ, :])
                            dve.wait_ge(cn_hi, c + 1)
                            nc.vector.tensor_tensor(lo, craw[:, c, :], hi.bitcast(F32), ALU.subtract).then_inc(cn_lo, 1)
                nxt = ("mem", hd + 2, hd + 2, 0, hd % 2) if hd + 2 < MEM_HEADS else None
                head("mem", lambda d: hd + d, hd, hd % 2, hd + 1 < MEM_HEADS, nxt, fill,
                     reciprocal_rms if hd < 2 else None)

            def split_lo(src, br, c):
                dve.wait_ge(os_hi, 4 * br + c + 1)
                nc.vector.tensor_tensor(olo[:, c, :], src[:, c, :], ohi[:, c, :].bitcast(F32),
                                        ALU.subtract).then_inc(os_lo, 1)

            dve.wait_ge(w_used, B_UQ + KQ)
            for half in range(2):
                hs = slice(4 * half, 4 * half + 4)
                dve.wait_ge(ev, E_UQ + 4 * half + 4)
                rotate(Q[R, hs, :], Kt[R, hs, :], tabs[R, 2:3, :].to_broadcast([ROPE, 4, S]),
                       tabs[R, 3:4, :].to_broadcast([ROPE, 4, S]), 4 + 4 * half)
            dve.wait_ge(kr, 1)
            nc.vector.tensor_tensor(kl[64:96, :], kf[64:96, :], kh[64:96, :].bitcast(F32), ALU.subtract).then_inc(kr, 1)
            for c in range(4):
                split_lo(MQ, 0, c)
            stage("mla", J_MLA, 0, 0, 0)
            first_softmax("mla", J_MLA)
            stage("mla", J_MLA + 1, 1, 0, 1)
            dve.wait_ge(f_rows, 16 * 8)

            def merge(br, n, d, g, ybank):
                dve.wait_ge(sg_done, g + 1)
                dve.wait_ge(w_used, n + 1)
                if br == 0:
                    nc.vector.scalar_tensor_tensor(row(merged, d), sig[:], 1.0, ps[:, ybank, :], ALU.add,
                                                   ALU.mult).then_inc(mg_done, 1)
                else:
                    nc.vector.scalar_tensor_tensor(sig[:], sig[:], 1.0, ps[:, ybank, :], ALU.add, ALU.mult).then_inc(mt_done, 1)
                    dve.wait_ge(mt_done, g - 8 + 1)
                    nc.vector.tensor_tensor(row(merged, d), row(merged, d), sig[:], ALU.add).then_inc(mg_done, 1)

            def split_mla(kb):
                for c in ((0,), (1,), (2, 3), ())[kb]:
                    split_lo(Q, 1, c)

            def branch_heads(kind, br, j0):
                def body(i, last=False):
                    for p in range(2):
                        hd = i * 2 + p
                        n, _, _ = block(B_MG + 16 * br + 2 * p + 1, i)
                        if not last:
                            nxt = (kind, i * 2 + (j0 + p + 2), i * 2 + (p + 2), i + 1, p)
                        else:
                            nxt = ("fox", J_FOX + p, p, 0, p) if kind == "mla" else None
                        head(kind, lambda d: i * 2 + (j0 + p + d), hd, p, kind == "mla" or not (last and p == 1),
                             nxt, lambda: merge(br, n, hd, i * 2 + (8 * br + p), 7),
                             split_mla if br == 1 and p == 0 and isinstance(i, int) and i == 0
                             else None)
                if br == 1:
                    body(0)
                with dve.Fori(br, 3) as i:
                    body(i)
                body(3, True)

            branch_heads("mla", 0, J_MLA)
            branch_heads("fox", 1, J_FOX)
            for c in range(4):
                split_lo(FQK, 2, c)
            with dve.Fori(0, 4) as i:
                for p in range(2):
                    n, _, _ = block(B_MG + 32 + 2 * p + 1, i)
                    d = i * 2 + p
                    merge(2, n, d, i * 2 + (16 + p), (7, 5)[p])
                    dve.wait_ge(ms_hi, d + 1)
                    nc.vector.scalar_tensor_tensor(row(mlo, d), row(merged, d), 0.5, row(mhi, d).bitcast(F32),
                                                   ALU.mult, ALU.subtract).then_inc(ms_lo, 1)
            TG2 = TG1 + NT
            layer_norm(1, TG2)
            ffn(B_UP2, B_DN2, NF, 0)
            for t in range(NT):
                norm(2 * NT + t)

        @blk.tensor
        def _(pe):
            mm = nc.tensor.matmul

            def wv(t, like, m=P):
                return t[:, like % RING, :].rearrange("p (k m) -> p k m", m=m)

            def three(k):
                return ((0, 0), (0, 1), (1, 0))[k]

            def product(m, like, out_ap, rh, rl, last, cols=slice(0, P)):
                k, (a, b) = m // 3, three(m % 3)
                return mm(out_ap, wv((whi, wlo)[a], like)[:, k, cols], (rh, rl)[b](k), start=m == 0, stop=m == last)

            def feature_block(b, bank, cols=slice(0, P), rh=None, rl=None, width=S):
                n, like, _ = b
                pe.wait_ge(w_lo, n + 1)
                rh = rh or (lambda k: xhi[:, k, :])
                rl = rl or (lambda k: xlo[:, k, :])
                rows_out = cols.stop - cols.start
                for m in range(3 * KD):
                    ins = product(m, like, ps[0:rows_out, bank, 0:width], rh, rl, 3 * KD - 1, cols)
                ins.then_inc(w_used, 1)

            def turn(g, src, bank, ready=None):
                for k in range(KD):
                    ins = nc.tensor.transpose(ps[:, bank + k // 4, (k % 4) * P:(k % 4 + 1) * P],
                                              src[:, k * P:(k + 1) * P], ident[:])
                ins.then_inc(t_done, 1)

            def token_block(like, t, sh, sl, start, stop):
                for a, b in ((sh, whi), (sh, wlo), (sl, whi)):
                    for half in range(2):
                        ins = mm(ps[:, 2 * t + half, :], a(t), b[:, like % RING, half * 512:(half + 1) * 512],
                                 start=start and a is sh and b is whi, stop=stop and a is sl)
                return ins

            def up(b0, h0):
                def body(i):
                    for p in range(2):
                        f = i * 2 + p
                        wait(pe, h_done, f + h0 - 1)
                        feature_block(block(b0 + 2 * p, i), 2 * p)
                        feature_block(block(b0 + 2 * p + 1, i), 2 * p + 1)
                return body

            def first_up(b0, g, between=()):
                for half in range(2):
                    cols = slice(half * (S // 2), (half + 1) * (S // 2))
                    pe.wait_ge(t_lo, g + 2 * half + 2)
                    for j in range(RING):
                        if half == 0:
                            pe.wait_ge(w_lo, b0 + j + 1)
                        for m in range(3 * KD):
                            ins = product(m, b0 + j, ps[:, j, cols], lambda k: xhi[:, k, cols],
                                          lambda k: xlo[:, k, cols], 3 * KD - 1)
                        if half == 1:
                            ins.then_inc(w_used, 1)
                        if half == 0 and j % 2 == 1 and between:
                            turn_tile(1, between[j // 2])

            def hidden(slot):
                return (lambda t: hhi[:, slot, t * P:(t + 1) * P]), (lambda t: hlo[:, slot, t * P:(t + 1) * P])

            def turn_tile(L, t):
                pe.wait_ge(lnc, 6 * (L * NT + t + 1))
                turn(NT + 2 + L * NT + t, X[:, t, :], 2 * t)

            def finish(b0, sources, L):
                for t in range(NT):
                    for c, (sh, sl, ready, count) in enumerate(sources):
                        if t == 0:
                            pe.wait_ge(ready, count)
                            pe.wait_ge(w_lo, b0 + c + 1)
                        ins = token_block(b0 + c, t, sh, sl, False, c == RING - 1)
                        if t == NT - 1:
                            ins.then_inc(w_used, 1)
                        if t < NT - 1 and c == RING - 1:
                            ins.then_inc(y_done, 1)
                        if t + c == 3 and t >= 2 and L < 2:
                            turn_tile(L, t - 2)

            def down(b1, h0, L):
                def one(b, f, slot, first):
                    n, like, _ = b
                    pe.wait_ge(hs_lo, f + h0 + 1)
                    pe.wait_ge(w_lo, n + 1)
                    sh, sl = hidden(slot)
                    order = (2, 3, 0, 1) if first else range(NT)
                    for t in order:
                        if first and t == 0:
                            pe.wait_ge(h_done, h0 + NF)
                        ins = token_block(like, t, sh, sl, first, False)
                    ins.then_inc(w_used, 1)
                for f in range(RING):
                    one(block(b1 + f), f, f, f == 0)
                with pe.Fori(1, 4) as i:
                    for j in range(RING):
                        one(block(b1 + j, i), i * RING + j, j, False)
                for f in (16, 17):
                    one(block(b1 + f), f, f % RING, False)
                finish(b1 + 18, [(*hidden(f % RING), hs_lo, f + h0 + 1) for f in range(18, NF)], L)

            pe.wait_ge(act_c, 2)
            for t in range(NT):
                pe.wait_ge(x_in[t], 16)
                turn(t, X[:, t, :], 2 * t)
            first_up(B_UP1, 0)
            pe.wait_ge(m_in, 16)
            for kb in range(2):
                turn(NT + kb, res[:, kb, :], 4 + 2 * kb)
            with pe.Fori(1, NF // 2) as i:
                up(B_UP1, 0)(i)
            pe.wait_ge(t_lo, NT + 2)
            TG1 = NT + 2
            down(B_DN1, 0, 0)
            for j in range(4):
                if j % 2 == 0:
                    pe.wait_ge(t_lo, TG1 + j // 2 + 1)
                feature_block(block(B_MK + j), j, rh=lambda k: mThi[:, k, :], rl=lambda k: mTlo[:, k, :], width=M)
                if j == 1:
                    turn_tile(0, 2)
            pe.wait_ge(ev, E_MK + 2)
            for j in range(4):
                n, like, _ = block(B_MV + j)
                pe.wait_ge(w_lo, n + 1)
                for k in range(2):
                    for kb in range(2):
                        for a, b in ((0, 0), (0, 1), (1, 0)):
                            ins = mm(ps[:, kb, :], (mThi, mTlo)[a][:, 2 * j + k, kb * P:(kb + 1) * P],
                                     wv((whi, wlo)[b], like, 512)[:, k, :], start=j == 0 and k == 0 and a + b == 0,
                                     stop=j == 3 and k == 1 and a == 1)
                ins.then_inc(w_used, 1)
                if j == 1:
                    turn_tile(0, 3)
            pe.wait_ge(t_lo, TG1 + 4)
            for j in range(KQ + KKV):
                pe.wait_ge(ev, E_MK + min(j + 3, 4))
                feature_block(block(B_C + j), j + 2)
            feature_block(block(B_KF), 7, cols=slice(64, 104))

            def memory_query(j):
                pe.wait_ge(ev, (E_C + 3, E_C + 4, E_C + 5, E_KF + 2)[j])
                feature_block(block(B_MQ + j), 4 + j)
            memory_query(0)
            pe.wait_ge(ev, E_C + 2)
            pe.wait_ge(sq_done, KQ + KKV + 3)
            for c, k in enumerate((0, KQ)):
                mm(ps[:, 2 + c, :], ones[:], csq[:, k, :], start=True, stop=True).then_inc(ss_done, 1)
            memory_query(1)

            def logits(kind, j, qt):
                kq = {"mem": P, "mla": QK_MLA, "fox": 68}[kind]
                kq_lo = {"mem": P, "mla": QK_MLA, "fox": 64}[kind]
                causal = kind != "mem"
                nk = P * (qt + 1) if causal else M
                if qt == 0:
                    pe.wait_ge(st_lo, j + 1)
                wait(pe, ex_done, j * 4 + (qt - 1))
                o = ps[:, qt % 2, 0:nk]
                q_cols = slice(qt * P, (qt + 1) * P)
                mm(o, qh[0:kq, q_cols], kh[0:kq, 0:nk], start=True, stop=False)
                mm(o, qh[0:kq_lo, q_cols], kl[0:kq_lo, 0:nk], start=False, stop=False)
                ins = mm(o, ql[0:kq_lo, q_cols], kh[0:kq_lo, 0:nk], start=False, stop=not causal)
                if causal:
                    ins = mm(ps[:, qt % 2, nk - P:nk], identR[:], maskR[:], start=False, stop=True)
                ins.then_inc(s_done, 1)

            def head(kind, J, p, nxt, fill, cuts):
                j = J(0)
                causal = kind != "mem"
                step = [0]

                def filler():
                    fill(cuts[step[0]], cuts[step[0] + 1])
                    step[0] += 1

                def next_logits(qt):
                    if nxt is not None:
                        logits(nxt, J(1), qt)

                def turn_probs(kb):
                    wait(pe, pl_done, pt_first(j) + kb - 1)
                    pe.wait_ge(pn_done, j * 4 + NT)
                    first = kb if causal else 0
                    for qt in range(first, NT):
                        off = P * qt * (qt + 1) // 2 if causal else M * qt
                        ins = nc.tensor.transpose(ps[:, 2 + kb % 2, (qt - first) * P:(qt - first + 1) * P],
                                                  prob[p][:, off + kb * P:off + (kb + 1) * P], ident[:])
                    ins.then_inc(pt_done, 1)

                def values(kb):
                    w = S - P * kb if causal else S
                    off = PT_OFF[causal][kb]
                    dv = DV if causal else P
                    nb = 4 if causal else 2
                    pe.wait_ge(pl_done, pt_first(j) + kb + 1)
                    if kb == 0:
                        pe.wait_ge(sv_lo, j + 1)
                        wait(pe, o_done, j - 1)
                        if isinstance(j, int) and J_MLA <= j < J_MLA + 2:
                            pe.wait_ge(ev, E_FV + 2 * (j - J_MLA) + 2)
                    o = ps[0:dv, 4 + p, S - w:S]
                    for a, b in ((0, 0), (0, 1), (1, 0)):
                        ins = mm(o, (vh, vl)[a][:].rearrange("p (k m) -> p k m", k=nb)[:, kb, :],
                                 (pthi, ptlo)[b][:, off:off + w], start=kb == 0 and a + b == 0,
                                 stop=kb == nb - 1 and a == 1)
                    if kb == nb - 1:
                        ins.then_inc(pv_done, 1)

                if causal:
                    turn_probs(0)
                    next_logits(0)
                    filler()
                    turn_probs(1)
                    next_logits(1)
                    filler()
                    values(0)
                    turn_probs(2)
                    next_logits(2)
                    filler()
                    values(1)
                    turn_probs(3)
                    next_logits(3)
                    filler()
                    values(2)
                    filler()
                    values(3)
                    filler()
                else:
                    turn_probs(0)
                    next_logits(0)
                    filler()
                    turn_probs(1)
                    next_logits(1)
                    filler()
                    values(0)
                    next_logits(2)
                    filler()
                    next_logits(3)
                    filler()
                    values(1)
                    filler()

            pe.wait_ge(ev, E_MV + 2)
            logits("mem", 0, 0)
            logits("mem", 0, 1)
            memory_query(2)
            logits("mem", 0, 2)
            logits("mem", 0, 3)
            memory_query(3)
            pe.wait_ge(rm_sd, 2)
            for hd in range(MEM_HEADS):
                def fill(lo, hi):
                    for m in range(lo, hi):
                        k, m1 = m // 24, m % 24
                        n = B_FQK + 2 * hd + k
                        if m1 == 0:
                            pe.wait_ge(w_lo, n + 1)
                            pe.wait_ge(ev, (E_MQ + 3 + k) if hd == 0 else E_FQK + 2 * (hd - 1) + k + 1)
                        ins = product(m1, n, ps[:, 6 + k, :], lambda k: xhi[:, k, :], lambda k: xlo[:, k, :], 23)
                        if m1 == 23:
                            ins.then_inc(w_used, 1)
                head("mem", lambda d: hd + d, hd % 2, "mem" if hd + 1 < MEM_HEADS else None, fill,
                     [0, 9, 18, 27, 36, 48])
            pe.wait_ge(pl_done, 2 * MEM_HEADS)
            pe.wait_ge(ex_done, 4 * MEM_HEADS)
            pe.wait_ge(cn_lo, KQ)
            for k in range(KQ):
                pe.wait_ge(w_lo, B_UQ + k + 1)
            for hd in range(HEADS):
                if hd >= 4:
                    pe.wait_ge(ev, E_UQ + hd - 3)
                for k in range(KQ):
                    for a, b in ((0, 0), (0, 1), (1, 0)):
                        ins = mm(ps[0:QK_MLA, hd % 4, :],
                                 (whi, wlo)[a][:, (B_UQ + k) % RING, hd * QK_MLA:(hd + 1) * QK_MLA],
                                 (cqhi, cqlo)[b][:, k, :], start=k == 0 and a + b == 0, stop=k == KQ - 1 and a == 1)
                        if hd == HEADS - 1 and a == 1 and k < KQ - 1:
                            ins.then_inc(w_used, 1)
                if hd < HEADS - 1:
                    ins.then_inc(pj, 1)
            ins.then_inc(w_used, 1)

            def fox_values(j, tiles=range(NT)):
                n = B_FV + j if j < 2 else B_FV2 + j - 2
                pe.wait_ge(w_lo, n + 1)
                for t in tiles:
                    for k in range(2):
                        for a, b in ((0, 0), (0, 1), (1, 0)):
                            ins = mm(ps[:, 4 + t, :], (xhi, xlo)[a][:, 2 * j + k, t * P:(t + 1) * P],
                                     wv((whi, wlo)[b], n, 512)[:, k, :], start=j == 0 and k == 0 and a + b == 0,
                                     stop=j == 3 and k == 1 and a == 1)
                if tiles[-1] == NT - 1:
                    ins.then_inc(w_used, 1)

            pe.wait_ge(o_done, MEM_HEADS)
            pe.wait_ge(ev, E_FQK + 8)
            fox_values(0)
            fox_values(1)
            pe.wait_ge(cn_lo, KQ + KKV)
            for k in range(KKV):
                pe.wait_ge(w_lo, B_UKV + k + 1)
            for hd in range(HEADS):
                pe.wait_ge(ev, E_UQ + hd + 5)
                for k in range(KKV):
                    for a, b in ((0, 0), (0, 1), (1, 0)):
                        ins = mm(ps[0:NOPE, hd % 4, :],
                                 wv((whi, wlo)[a], B_UKV + k)[:, hd, 0:NOPE],
                                 (ckhi, cklo)[b][:, k, :], start=k == 0 and a + b == 0, stop=k == KKV - 1 and a == 1)
                ins.then_inc(pj, 1)
            for t in range(NT):
                pe.wait_ge(ev, E_K + 5 + t)
                for k in range(KKV):
                    for a, b in ((0, 0), (0, 1), (1, 0)):
                        ins = mm(ps[:, t, :], (ckhi, cklo)[a][:, k, t * P:(t + 1) * P],
                                 wv((whi, wlo)[b], B_UKV + k)[:, :, NOPE:P],
                                 start=k == 0 and a + b == 0, stop=k == KKV - 1 and a == 1)
                        if t == NT - 1 and k == 0 and a == 1:
                            ins.then_inc(w_used, 1)
                if t < NT - 1:
                    ins.then_inc(pj, 1)
            ins.then_inc(w_used, 1)
            fox_values(2)
            pe.wait_ge(ev, E_V + NT)
            pe.wait_ge(kr, 2)
            logits("mla", J_MLA, 0)
            logits("mla", J_MLA, 1)
            fox_values(3, (0,))
            logits("mla", J_MLA, 2)
            fox_values(3, (1,))
            logits("mla", J_MLA, 3)
            fox_values(3, (2, 3))

            def gate_and_branch(br, i, p, gbank, ybank, g):
                ng, lg, _ = block(B_MG + 16 * br + 2 * p, i)
                ny, ly, _ = block(B_MG + 16 * br + 2 * p + 1, i)

                def fill(lo, hi):
                    for m in range(lo, hi):
                        if m == 0:
                            pe.wait_ge(w_lo, ng + 1)
                            wait(pe, sg_done, g)
                            if isinstance(g, int) and g == 0:
                                pe.wait_ge(ev, E_FV + 1)
                        if m == 24:
                            pe.wait_ge(w_lo, ny + 1)
                            pe.wait_ge(os_lo, 4 * br + 4)
                            wait(pe, mg_done, g)
                            if isinstance(g, int) and g == 0:
                                pe.wait_ge(ev, E_FV + 3)
                        if m < 24:
                            ins = product(m, lg, ps[:, gbank, :], lambda k: xhi[:, k, :], lambda k: xlo[:, k, :], 23)
                        else:
                            ins = product(m - 24, ly, ps[:, ybank, :], lambda k: ohi[:, k, :],
                                          lambda k: olo[:, k, :], 11)
                        if m in (23, 35):
                            ins.then_inc(w_used, 1)
                return fill

            cuts = [0, 4, 9, 14, 22, 29, 36]
            for kind, br, j0 in (("mla", 0, J_MLA), ("fox", 1, J_FOX)):
                def two_heads(i, last=False):
                    for p in range(2):
                        nxt = kind if not (last and p == 1) else ("fox" if kind == "mla" else None)
                        head(kind, lambda d: i * 2 + (j0 + p + d), p, nxt,
                             gate_and_branch(br, i, p, 6, 7, i * 2 + (8 * br + p)), cuts)
                if br == 0:
                    two_heads(0)
                with pe.Fori(1 if br == 0 else 0, 3) as i:
                    two_heads(i)
                two_heads(3, True)
            pe.wait_ge(o_done, J_END)
            with pe.Fori(0, 4) as i:
                for p in range(2):
                    gate_and_branch(2, i, p, 6, (7, 5)[p], i * 2 + (16 + p))(0, 36)
            def chunk(k):
                return (lambda t: mhi[:, k, t * P:(t + 1) * P]), (lambda t: mlo[:, k, t * P:(t + 1) * P])
            for k in range(4):
                pe.wait_ge(ms_lo, k + 1)
                pe.wait_ge(w_lo, B_OUT + k + 1)
                for t in range(NT):
                    if k == 0 and t == 2:
                        pe.wait_ge(sg_done, 24)
                        pe.wait_ge(mg_done, 24)
                    ins = token_block(B_OUT + k, t, *chunk(k), k == 0, False)
                ins.then_inc(w_used, 1)
            TG2 = TG1 + NT
            finish(B_OUT + 4, [(*chunk(k), ms_lo, k + 1) for k in range(4, KD)], 1)
            first_up(B_UP2, TG2, between=(2, 3))
            with pe.Fori(1, NF // 2) as i:
                up(B_UP2, NF)(i)
            down(B_DN2, NF, 2)


_INS = ["x", "mem", "positions", "ln1_g", "ln1_b", "ffn1_w_in", "ffn1_w_down", "w_in", "b_gate", "mla_q_norm",
        "mla_w_uq", "mla_kv_norm", "mla_w_ukv", "fox_b_f", "mem_w_kv", "w_br_mla", "w_br_fox", "w_br_mem", "w_out",
        "ln2_g", "ln2_b", "ffn2_w_in", "ffn2_w_down", "ln3_g", "ln3_b"]


def kernel(**inputs):
    import numpy as _np
    import concourse.bacc as _bacc
    from concourse import mybir as _mybir
    from concourse.bass_utils import run_bass_kernel_spmd as _run

    nc = _bacc.Bacc("TRN2", target_bir_lowering=False, num_devices=1)
    arrays, args = {}, []
    for name in _INS:
        a = _np.ascontiguousarray(inputs[name])
        a = a.reshape(a.shape[1:])
        arrays[f"in_{name}_dram"] = a
        args.append(nc.dram_tensor(f"in_{name}_dram", a.shape, _mybir.dt.from_np(a.dtype), kind="ExternalInput").ap())
    arrays["in_consts_dram"] = shape_constants()
    args.append(nc.dram_tensor("in_consts_dram", (P, 8), _mybir.dt.float32, kind="ExternalInput").ap())
    args.append(nc.dram_tensor("out_0_dram", (S, D), _mybir.dt.float32, kind="ExternalOutput").ap())
    layer_program(nc, *args)
    r = _run(nc, [arrays], core_ids=[0])
    return r.results[0]["out_0_dram"].reshape(1, S, D)
```

```python
from contextlib import ExitStack

import numpy as np

import concourse.bass as bass
from concourse import mybir

F32 = mybir.dt.float32
F32R = mybir.dt.float32r
I32 = mybir.dt.int32
ALU = mybir.AluOpType
ACT = mybir.ActivationFunctionType
AX = mybir.AxisListType

P = 128
S, D, M = 512, 1024, 256
KD = D // P
NT = S // P
FF = 2816
NF = FF // P
HEADS, MEM_HEADS = 8, 4
NOPE, ROPE, DV = 64, 32, 64
QK_MLA = NOPE + ROPE
QL, KVL = 384, 256
KQ, KKV = QL // P, KVL // P
FOX_W = 512
ALPHA = 2.0 ** 0.25
LN_EPS, RMS_EPS = 1e-5, 1e-6
NEG = -1e30

C_CQ = 0
C_KPE = QL + KVL
C_FQ = C_KPE + ROPE
C_FK = C_FQ + FOX_W
C_FV = C_FK + FOX_W
C_FLOG = C_FV + FOX_W
C_MQ = C_FLOG + HEADS
C_GATE = C_MQ + 512

RING = 4
B_UP1 = 0
B_DN1 = B_UP1 + 2 * NF
B_MK = B_DN1 + NF
B_MV = B_MK + 4
B_C = B_MV + 4
B_KF = B_C + KQ + KKV
B_MQ = B_KF + 1
B_FQK = B_MQ + 4
B_UQ = B_FQK + 8
B_FV = B_UQ + KQ
B_UKV = B_FV + 2
B_FV2 = B_UKV + KKV
B_MG = B_FV2 + 2
B_OUT = B_MG + 3 * 16
B_UP2 = B_OUT + KD
B_DN2 = B_UP2 + 2 * NF
B_END = B_DN2 + NF

E_MK, E_MV, E_C, E_KF, E_MQ, E_FQK, E_UQ, E_K, E_V, E_FV, E_ALL = 0, 4, 6, 11, 13, 17, 25, 33, 41, 45, 49

J_MEM, J_MLA, J_FOX, J_END = 0, 4, 12, 20
PT_OFF = {False: (0, 512), True: (0, 512, 0, 512)}


def pt_first(j):
    return 2 * j if isinstance(j, int) and j <= J_MLA else j * 4 - 2 * J_MLA


def shape_constants():
    c = np.zeros((P, 8), np.float32)
    half = ROPE // 2
    inv = (10000.0 ** (-np.arange(half, dtype=np.float64) / half)).astype(np.float32)
    c[64:64 + half, 0] = inv
    c[64 + half:96, 0] = inv
    c[64:64 + half, 1] = -1.0
    c[64 + half:96, 1] = 1.0
    c[:, 2] = LN_EPS
    c[:, 3] = RMS_EPS
    c[:, 4] = np.pi / 2
    return c


def layer_program(nc, x, mem, positions, ln1_g, ln1_b, ffn1_w_in, ffn1_w_down, w_in, b_gate,
                  mla_q_norm, mla_w_uq, mla_kv_norm, mla_w_ukv, fox_b_f, mem_w_kv, w_br_mla, w_br_fox,
                  w_br_mem, w_out, ln2_g, ln2_b, ffn2_w_in, ffn2_w_down, ln3_g, ln3_b, consts, out):
    with ExitStack() as ctx:
        base = (nc.sbuf_base + 31) // 32 * 32
        ctx.enter_context(nc.sbuf_tensor("arena", [P, (nc.sbuf_usable_end - base - 64) // 4], F32))
        limit = nc.sbuf_usable_end

        def at(name, shape, dt, offset):
            size = 4
            for s in shape[1:]:
                size *= s
            assert base + offset + size <= limit, (name, base + offset + size, limit)
            return nc.alloc_sbuf_tensor_at(name, shape, dt, offset=base + offset)

        K1 = 1024
        whi = at("whi", [P, RING, 1024], F32R, 0)
        wlo = at("wlo", [P, RING, 1024], F32R, 16 * K1)
        raw = at("raw", [P, RING, 1024], F32, 32 * K1)
        xhi = at("xhi", [P, KD, S], F32R, 48 * K1)
        xlo = at("xlo", [P, KD, S], F32R, 64 * K1)
        X = at("X", [P, NT, D], F32, 80 * K1)
        merged = at("merged", [P, KD, S], F32, 80 * K1)
        A = 96 * K1
        h = at("h", [P, NF, S], F32, A)
        hhi = at("hhi", [P, RING, S], F32R, A + 44 * K1)
        hlo = at("hlo", [P, RING, S], F32R, A + 52 * K1)
        Q = at("Q", [P, HEADS, S], F32, A)
        craw = at("craw", [P, KQ + KKV, S], F32, A)
        csq = at("csq", [P, KQ + KKV, S], F32, A + 40 * K1)
        Kt = at("Kt", [P, HEADS, S], F32, A + 16 * K1)
        mk = at("mk", [P, MEM_HEADS, M], F32, A + 16 * K1)
        cqhi = at("cqhi", [P, KQ, S], F32R, A + 20 * K1)
        cqlo = at("cqlo", [P, KQ, S], F32R, A + 26 * K1)
        V = at("V", [P, NT, 512], F32, A + 32 * K1)
        mv = at("mv", [P, 2, 512], F32, A + 32 * K1)
        rms = at("rms", [P, 2, S], F32, A + 36 * K1)
        FQK = at("FQK", [P, 8, S], F32, A + 40 * K1)
        mhi = at("mhi", [P, KD, S], F32R, A)
        mlo = at("mlo", [P, KD, S], F32R, A + 16 * K1)
        FV = at("FV", [P, NT, 512], F32, A + 56 * K1)
        ckhi = at("ckhi", [P, KKV, S], F32R, A + 56 * K1)
        cklo = at("cklo", [P, KKV, S], F32R, A + 60 * K1)
        ohi = at("ohi", [P, 4, S], F32R, A + 64 * K1)
        olo = at("olo", [P, 4, S], F32R, A + 72 * K1)
        MQ = at("MQ", [P, MEM_HEADS, S], F32, A + 72 * K1)
        mThi = at("mThi", [P, KD, M], F32R, A + 64 * K1)
        mTlo = at("mTlo", [P, KD, M], F32R, A + 72 * K1)
        PB = A + 80 * K1
        stmp = at("stmp", [P, 2, S], F32, PB)
        T = PB + 5 * K1
        pthi = at("pthi", [P, 1024], F32R, T)
        ptlo = at("ptlo", [P, 1024], F32R, T + 4 * K1)
        res = at("res", [P, 2, D], F32, T)
        tabs = at("tabs", [P, 5, S], F32, 80 * K1)
        rtmp = at("rtmp", [P, S], F32, 90 * K1)
        G = T + 8 * K1
        qh = at("qh", [P, S], F32R, G)
        ql = at("ql", [P, S], F32R, G + 2 * K1)
        kh = at("kh", [P, S], F32R, G + 4 * K1)
        kl = at("kl", [P, S], F32R, G + 6 * K1)
        vhl = at("vhl", [P, 512], F32R, G + 8 * K1)
        lng = at("lng", [P, D], F32, G)
        lnb = at("lnb", [P, D], F32, G + 4 * K1)
        Z = G + 10 * K1
        identR = at("identR", [P, P], F32R, Z)
        maskR = at("maskR", [P, P], F32R, Z + 512)
        kf = at("kf", [P, S], F32, Z + 1024)
        sig = at("sig", [P, S], F32, Z + 1024)
        ones = at("ones", [P, P], F32, PB + 4 * K1)
        pos = at("pos", [P, S], I32, G + 8 * K1)
        maskF = at("maskF", [P, P], F32, A)
        ident = at("ident", [P, P], F32, Z + 3072)
        SM = Z + 3584
        cst = at("cst", [P, 8], F32, SM)
        bg = at("bg", [P, 24], F32, SM + 32)
        rms_gain = at("rms_gain_and_forget_bias", [P, 8], F32, SM + 128)
        gq, bf = rms_gain[:, 0:KQ + KKV], rms_gain[:, 5:6]
        moments = at("moments", [P, 16], F32, SM + 160)
        stats = moments[:, 0:12].rearrange("p (a b) -> p a b", b=6)
        mvar, rstd = moments[:, 12:14], moments[:, 14:16]
        nmax = at("nmax", [P, 8], F32, SM + 224)
        rsum = at("rsum", [P, 8], F32, SM + 256)
        rinv = at("rinv", [P, 8], F32, SM + 288)
        prob = [at("prob_even", [P, 1280], F32, PB), at("prob_odd", [P, 1280], F32, SM + 320)]

        ps = ctx.enter_context(nc.psum_tensor("ps", [P, 8, 512], F32))
        spill = nc.dram_tensor("spill_x1", (S, D), F32, kind="Internal").ap()

        def sem(name):
            return ctx.enter_context(nc.semaphore(name))

        w_raw = [sem(f"w_raw{i}") for i in range(RING)]
        w_hi, w_lo = sem("w_hi"), sem("w_lo")
        w_used = sem("w_used")
        c_in, k_in = sem("c_in"), sem("k_in")
        kf_in = sem("kf_in")
        x_in = [sem(f"x_in{t}") for t in range(NT)]
        m_in = sem("m_in")
        g_in = sem("g_in")
        sp_out = sem("sp_out")
        f_rows = sem("f_rows")
        y_out = sem("y_out")
        pool_c = sem("pool_c")
        act_c = sem("act_c")
        t_done = sem("t_done")
        t_hi, t_lo = sem("t_hi"), sem("t_lo")
        sl_done, h_done = sem("sl_done"), sem("h_done")
        hs_hi, hs_lo = sem("hs_hi"), sem("hs_lo")
        y_done = sem("y_done")
        x3_gain, x3_done = sem("x3_gain"), sem("x3_done")
        fin = sem("fin")
        lnc = sem("lnc")
        ln_sd = sem("ln_sd")
        ev = sem("ev")
        pj = sem("pj")
        sq_done, ss_done = sem("sq_done"), sem("ss_done")
        rm_sd, rm_r = sem("rm_sd"), sem("rm_r")
        cn, cn_hi, cn_lo = sem("cn"), sem("cn_hi"), sem("cn_lo")
        tb_v, tb_s = sem("tb_v"), sem("tb_s")
        fg_v, fg_s = sem("fg_v"), sem("fg_s")
        rp = sem("rp")
        kr = sem("kr")
        st_hi, st_lo = sem("st_hi"), sem("st_lo")
        st_f = sem("st_f")
        sv_hi = sem("sv_hi")
        s_done = sem("s_done")
        mx_done, ex_done = sem("mx_done"), sem("ex_done")
        rc_done, pn_done = sem("rc_done"), sem("pn_done")
        pt_done = sem("pt_done")
        ph_done, pl_done = sem("ph_done"), sem("pl_done")
        pv_done = sem("pv_done")
        oc_done, o_done = sem("oc_done"), sem("o_done")
        os_hi, os_lo = sem("os_hi"), sem("os_lo")
        sg_done, mt_done, mg_done = sem("sg_done"), sem("mt_done"), sem("mg_done")
        ms_hi, ms_lo = sem("ms_hi"), sem("ms_lo")

        def wait(eng, s, v):
            if not isinstance(v, int) or v > 0:
                eng.wait_ge(s, v)

        def apart(eng, *held):
            if any(not isinstance(v, int) for v in held):
                eng.wait_ge(c_in, 16)

        def row(t, i):
            if isinstance(i, int):
                return t[:, i, :]
            return t[:, bass.ds(i, 1), :].rearrange("p a n -> p (a n)")

        def rows(t, lo, hi, i):
            if isinstance(i, int):
                return t[lo:hi, i, :]
            return t[lo:hi, bass.ds(i, 1), :].rearrange("p a n -> p (a n)")

        def wcols(n):
            if n == B_KF:
                return lambda t: t[:, n % RING, :].rearrange("p (k m) -> p k m", m=P)[:, :, 64:104]
            if B_UQ <= n < B_UQ + KQ:
                return lambda t: t[:, n % RING, 0:768]
            if B_MG <= n < B_OUT and (n - B_MG) % 2:
                return lambda t: t[:, n % RING, 0:512]
            return lambda t: t[:, n % RING, :]

        def block(base_n, i=0, per=RING):
            if isinstance(i, int):
                n = base_n + per * i
                return n, n, n // RING
            return i * per + base_n, base_n, i * (per // RING) + base_n // RING

        def before(br, i, p):
            if isinstance(i, int) and i == 0 and p == 0:
                if br == 0:
                    return None
                n = B_MG + 16 * br - 2
                return n, n, br - 1, KD - 1, KD * br - 1
            n, like, _ = block(B_MG + 16 * br + 2 * p - 2, i)
            return n, like, br, i * 2 + (p - 1), i * 2 + (8 * br + p - 1)

        def v_parts(kind):
            if kind == "mem":
                return [vhl[:, 256 * c:256 * c + 256].rearrange("p (k m) -> p k m", k=2) for c in range(2)]
            v = vhl[:].rearrange("p (k m) -> p k m", k=4)
            return [v[:, :, DV * c:DV * c + DV] for c in range(2)]

        blk = ctx.enter_context(nc.Block())

        @blk.sync
        def _(sp):
            def load(b, src):
                n, like, lap = b
                apart(sp, n)
                wait(sp, w_lo, n - RING + 1)
                dst = wcols(like)(raw)
                if len(src.shape) == 3 and len(dst.shape) == 2:
                    dst = dst.rearrange("p (k m) -> p k m", k=src.shape[1])
                sp.dma_start(dst, src).then_inc(w_raw[like % RING], 16)

            def kcols(w, col, width=P):
                wv = w.rearrange("(k p) n -> p k n", p=P)
                return wv[:, :, bass.ds(col, width)] if not isinstance(col, int) else wv[:, :, col:col + width]

            def up(b0, w):
                def body(i):
                    for j in range(4):
                        f_off = (j // 2) * P + (j % 2) * FF
                        load(block(b0 + j, i), kcols(w, i * (2 * P) + f_off))
                return body

            def down_rows(w, r):
                if isinstance(r, int):
                    return w[r:r + P, :]
                return w[bass.ds(r, P), :]

            def down(b0, w):
                def body(i):
                    for j in range(4):
                        load(block(b0 + j, i), down_rows(w, i * (4 * P) + j * P))
                return body

            def ln_params(g, b):
                sp.dma_start(lng[:], g.partition_broadcast(P)).then_inc(g_in, 16)
                sp.dma_start(lnb[:], b.partition_broadcast(P)).then_inc(g_in, 16)

            xv = x.rearrange("(t p) d -> t p d", p=P)
            sp.dma_start(cst[:], consts).then_inc(c_in, 16)
            first = up(B_UP1, ffn1_w_in)
            for t in range(2):
                sp.dma_start(X[:, t, :], xv[t]).then_inc(x_in[t], 16)
            load(block(B_UP1), kcols(ffn1_w_in, 0))
            for t in range(2, NT):
                sp.dma_start(X[:, t, :], xv[t]).then_inc(x_in[t], 16)
            for j in range(1, 4):
                load(block(B_UP1 + j), kcols(ffn1_w_in, (j // 2) * P + (j % 2) * FF))
            memv = mem.rearrange("(t p) d -> p t d", p=P)
            sp.dma_start(res[:, :, :], memv).then_inc(m_in, 16)
            with nc.allow_non_contiguous_dma(reason="small per-feature parameters"):
                sp.dma_start(bg[:], b_gate.rearrange("(c p) -> p c", p=P)).then_inc(k_in, 16)
                sp.dma_start(gq[:, 0:KQ], mla_q_norm.rearrange("(c p) -> p c", p=P)).then_inc(k_in, 16)
                sp.dma_start(gq[:, KQ:KQ + KKV], mla_kv_norm.rearrange("(c p) -> p c", p=P)).then_inc(k_in, 16)
                sp.dma_start(bf[0:HEADS, :], fox_b_f.rearrange("(p a) -> p a", a=1)).then_inc(k_in, 16)
            sp.dma_start(pos[64:96, :], positions.partition_broadcast(ROPE)).then_inc(k_in, 16)
            ln_params(ln1_g, ln1_b)
            with sp.Fori(1, NF // 2) as i:
                first(i)
            dn1 = down(B_DN1, ffn1_w_down)
            with sp.Fori(0, NF // 4) as i:
                dn1(i)
            for f in range(NF // 4 * 4, NF):
                load(block(B_DN1 + f), down_rows(ffn1_w_down, f * P))
            for j in range(4):
                load(block(B_MK + j), kcols(mem_w_kv, j * P))
            mkv = mem_w_kv.rearrange("(k p) n -> p k n", p=P)
            for j in range(4):
                load(block(B_MV + j), mkv[:, 2 * j:2 * j + 2, 512:1024])
            for t in range(NT):
                wait(sp, lnc, 6 * (t + 1))
                sp.dma_start(spill[t * P:(t + 1) * P, :], X[:, t, :]).then_inc(sp_out, 16)
                if t < 3:
                    load(block(B_C + t), kcols(w_in, C_CQ + t * P))
            for j in range(3, KQ + KKV):
                load(block(B_C + j), kcols(w_in, C_CQ + j * P))
            n, like, lap = block(B_KF)
            wait(sp, w_lo, n - RING + 1)
            kfv = raw[:, n % RING, :].rearrange("p (k m) -> p k m", m=P)
            sp.dma_start(kfv[:, :, 64:96], kcols(w_in, C_KPE, ROPE)).then_inc(w_raw[n % RING], 16)
            with nc.allow_non_contiguous_dma(reason="eight columns"):
                sp.dma_start(kfv[:, :, 96:104], kcols(w_in, C_FLOG, HEADS)).then_inc(kf_in, 16)
            for j in range(4):
                load(block(B_MQ + j), kcols(w_in, C_MQ + j * P))
            for j in range(8):
                load(block(B_FQK + j), kcols(w_in, C_FQ + j * P))
            for k in range(KQ):
                load(block(B_UQ + k), mla_w_uq[k * P:(k + 1) * P, :])
            winv = w_in.rearrange("(k p) n -> p k n", p=P)
            for j in range(2):
                load(block(B_FV + j), winv[:, 2 * j:2 * j + 2, C_FV:C_FV + 512])
            for k in range(KKV):
                load(block(B_UKV + k), mla_w_ukv[k * P:(k + 1) * P, :])
            for j in range(2, 4):
                load(block(B_FV2 + j - 2), winv[:, 2 * j:2 * j + 2, C_FV:C_FV + 512])
            wait(sp, fg_v, 7)
            wait(sp, rp, 12)
            for r0, s0 in ((64, 1), (65, 2), (66, 0), (67, 0), (96, 0), (97, 0), (98, 3), (99, 4)):
                sp.dma_start(Kt[r0:r0 + 1, :, :], tabs[0:HEADS, s0, :]).then_inc(f_rows, 16)
            for b, (w_br, gate) in enumerate(((w_br_mem, 2), (w_br_mla, 0), (w_br_fox, 1))):
                for d in range(KD):
                    load(block(B_MG + 16 * b + 2 * d), kcols(w_in, C_GATE + gate * D + d * P))
                    load(block(B_MG + 16 * b + 2 * d + 1), kcols(w_br, d * P))
            for k in range(KD):
                load(block(B_OUT + k), w_out[k * P:(k + 1) * P, :])
            wait(sp, ms_lo, KD)
            wait(sp, sp_out, 16 * NT)
            for t in range(NT):
                sp.dma_start(X[:, t, :], spill[t * P:(t + 1) * P, :]).then_inc(x_in[t], 16)
            ln_params(ln2_g, ln2_b)
            second = up(B_UP2, ffn2_w_in)
            for i in range(2):
                second(i)
            wait(sp, lnc, 6 * 2 * NT)
            ln_params(ln3_g, ln3_b)
            with sp.Fori(2, NF // 2) as i:
                second(i)
            dn2 = down(B_DN2, ffn2_w_down)
            with sp.Fori(0, NF // 4) as i:
                dn2(i)
            for f in range(NF // 4 * 4, NF):
                load(block(B_DN2 + f), down_rows(ffn2_w_down, f * P))
            for t in range(NT - 1):
                sp.wait_ge(x3_done, t + 1)
                sp.dma_start(out[t * P:(t + 1) * P, :], X[:, t, :]).then_inc(y_out, 16)
            for half in range(2):
                sp.wait_ge(fin, 6 + 2 * half)
                cols = slice(512 * half, 512 * (half + 1))
                sp.dma_start(out[3 * P:4 * P, cols], X[:, 3, cols]).then_inc(y_out, 16)
            sp.wait_ge(y_out, 16 * (NT + 1))

        @blk.gpsimd
        def _(pool):
            nc.gpsimd.memset(ident[:], 0.0).then_inc(pool_c, 1)
            nc.gpsimd.memset(maskF[:], 0.0).then_inc(pool_c, 1)
            nc.gpsimd.memset(ones[:], 1.0).then_inc(pool_c, 1)
            pool.wait_ge(pool_c, 3)
            nc.gpsimd.affine_select(out=ident[:], in_=ident[:], compare_op=ALU.not_equal, fill=1.0, base=0,
                                    pattern=[[-1, P]], channel_multiplier=1).then_inc(pool_c, 1)
            nc.gpsimd.affine_select(out=maskF[:], in_=maskF[:], compare_op=ALU.is_ge, fill=NEG, base=0,
                                    pattern=[[-1, P]], channel_multiplier=1).then_inc(pool_c, 1)

            def low(b):
                n, like, lap = b
                v = wcols(like)
                pool.wait_ge(w_hi, n + 1)
                nc.gpsimd.tensor_tensor(v(wlo), v(raw), v(whi).bitcast(F32), ALU.subtract).then_inc(w_lo, 1)

            for n in range(RING):
                low(block(n))
            with pool.Fori(1, B_MV // RING + 1) as i:
                for j in range(RING):
                    low(block(j, i))
            for n in range((B_MV // RING + 1) * RING, B_MG + 3):
                low(block(n))
            with pool.Fori(0, 11) as i:
                for j in range(RING):
                    low(block(B_MG + 3 + j, i))
            for n in range(B_MG + 47, B_OUT + 3):
                low(block(n))
            with pool.Fori(0, (B_END - B_OUT - 3) // RING) as i:
                for j in range(RING):
                    low(block(B_OUT + 3 + j, i))
            for n in range(B_OUT + 3 + (B_END - B_OUT - 3) // RING * RING, B_END):
                low(block(n))
            for t in range(NT - 1):
                pool.wait_ge(lnc, 6 * (2 * NT + t) + 6)
                r = res[:, t % 2, :]
                nc.gpsimd.tensor_tensor(r, r, lng[:], ALU.mult).then_inc(x3_gain, 1)
                pool.wait_ge(x3_gain, t + 1)
                nc.gpsimd.tensor_tensor(X[:, t, :], r, lnb[:], ALU.add).then_inc(x3_done, 1)

        @blk.scalar
        def _(act):
            def high(b):
                n, like, lap = b
                v = wcols(like)
                act.wait_ge(w_raw[like % RING], lap * 16 + 16)
                if like == B_KF:
                    act.wait_ge(kf_in, 16)
                wait(act, w_used, n - RING + 1)
                nc.scalar.activation(v(whi), v(raw), ACT.Copy).then_inc(w_hi, 1)

            def turned_hi(g, t):
                act.wait_ge(t_done, g + 1)
                nc.scalar.activation(xhi[:, :, t * P:(t + 1) * P],
                                     ps[:, 2 * t:2 * t + 2, :].rearrange("p a (k m) -> p (a k) m", m=P),
                                     ACT.Copy).then_inc(t_hi, 1)

            def sd(q):
                act.wait_ge(lnc, 6 * q + 3)
                nc.scalar.activation(rstd[:, q % 2:q % 2 + 1], mvar[:, 1:2], ACT.Sqrt,
                                     bias=cst[:, 2:3]).then_inc(ln_sd, 1)

            def up(b0, h0):
                def body(i):
                    for p in range(2):
                        na, la, _ = block(b0 + 2 * p, i)
                        f = i * 2 + p
                        act.wait_ge(w_used, na + 1)
                        wait(act, h_done, f + h0 - 1)
                        nc.scalar.activation(stmp[:, p, :], ps[:, 2 * p, :], ACT.Silu).then_inc(sl_done, 1)
                        high(block(b0 + 2 * p + 4, i))
                        high(block(b0 + 2 * p + 5, i))
                return body

            def hidden_hi(f, slot, h0, after=None):
                apart(act, f)
                act.wait_ge(h_done, f + h0 + 1)
                if after is not None:
                    act.wait_ge(w_used, after)
                nc.scalar.activation(hhi[:, slot, :], row(h, f), ACT.Copy).then_inc(hs_hi, 1)

            def ffn(b0, b1, h0, start):
                body = up(b0, h0)
                with act.Fori(start, NF // 2 - 1) as i:
                    body(i)
                for f in range(RING):
                    hidden_hi(f, f, h0)
                body(NF // 2 - 1)
                with act.Fori(0, 4) as i:
                    for j in range(RING):
                        n, _, _ = block(b1 + j, i)
                        hidden_hi(i * RING + (j + RING), j, h0, after=n + 1)
                        high(block(b1 + j + RING, i))
                for f in range(16, 18):
                    hidden_hi(f + RING, f % RING, h0, after=b1 + f + 1)
                    high(block(b1 + f + RING))

            def evac(dst, src, done_sem, done, **kw):
                act.wait_ge(done_sem, done)
                nc.scalar.activation(dst, src, ACT.Identity if kw else ACT.Copy, **kw).then_inc(ev, 1)

            act.wait_ge(pool_c, 5)
            nc.scalar.activation(identR[:], ident[:], ACT.Copy).then_inc(act_c, 1)
            nc.scalar.activation(maskR[:], maskF[:], ACT.Copy).then_inc(act_c, 1)
            act.wait_ge(c_in, 16)
            turned_hi(0, 0); turned_hi(1, 1)
            high(block(0))
            turned_hi(2, 2); turned_hi(3, 3)
            for n in range(1, RING):
                high(block(n))
            up(B_UP1, 0)(0)
            for kb in range(2):
                act.wait_ge(t_done, NT + kb + 1)
                nc.scalar.activation(mThi[:, :, kb * P:(kb + 1) * P],
                                     ps[:, 4 + 2 * kb:6 + 2 * kb, :].rearrange("p a (k m) -> p (a k) m", m=P),
                                     ACT.Copy).then_inc(t_hi, 1)
            ffn(B_UP1, B_DN1, 0, 1)
            TG1 = NT + 2
            def two_tiles(L, g, b0):
                sd(NT * L); sd(NT * L + 1)
                turned_hi(g, 0)
                high(block(b0))
                turned_hi(g + 1, 1)
                for n in range(b0 + 1, b0 + 4):
                    high(block(n))
                sd(NT * L + 2)

            two_tiles(0, TG1, B_MK)
            for j in range(4):
                evac(mk[:, j, :], ps[:, j, 0:M], w_used, B_MK + j + 1)
                high(block(B_MK + j + 4))
                if j == 1:
                    turned_hi(TG1 + 2, 2)
                    sd(3)
            for j in range(4):
                high(block(B_MV + j + 4))
                if j == 1:
                    turned_hi(TG1 + 3, 3)
            for kb in range(2):
                evac(mv[:, kb, :], ps[:, kb, :], w_used, B_MV + 4)
            act.wait_ge(k_in, 16 * 5)
            nc.scalar.activation(bg[:], bg[:], ACT.Copy, scale=0.5)
            for j in range(KQ + KKV):
                evac(craw[:, j, :], ps[:, j + 2, :], w_used, B_C + j + 1)
                high(block(B_C + j + 4))
                if j == 3:
                    act.wait_ge(tb_v, 8)
                    nc.scalar.activation(tabs[64:96, 2, :], tabs[64:96, 0, :], ACT.Sin,
                                         scale=cst[64:96, 1:2]).then_inc(tb_s, 1)
                    nc.scalar.activation(tabs[64:96, 1, :], tabs[64:96, 0, :], ACT.Abs).then_inc(tb_s, 1)
                    act.wait_ge(tb_s, 2)
                    nc.scalar.activation(tabs[64:96, 3, :], tabs[64:96, 1, :], ACT.Sin, scale=-1.0,
                                         bias=cst[64:96, 4:5]).then_inc(tb_s, 1)
            evac(kf[64:96, :], ps[0:ROPE, 7, :], w_used, B_KF + 1)
            evac(kf[0:HEADS, :], ps[32:32 + HEADS, 7, :], w_used, B_KF + 1, bias=bf[0:HEADS, :])
            high(block(B_KF + 4))
            act.wait_ge(ev, E_KF + 2)
            nc.scalar.activation(tabs[0:HEADS, 0, :], kf[0:HEADS, :], ACT.Abs).then_inc(fg_s, 1)
            act.wait_ge(fg_s, 1)
            nc.scalar.activation(tabs[0:HEADS, 1, :], tabs[0:HEADS, 0, :], ACT.Exp, scale=-1.0).then_inc(fg_s, 1)
            act.wait_ge(fg_s, 2)
            nc.scalar.activation(tabs[0:HEADS, 2, :], tabs[0:HEADS, 1, :], ACT.Ln, bias=1.0).then_inc(fg_s, 1)

            def memory_query(j):
                evac(MQ[:, j, :], ps[:, 4 + j, :], w_used, B_MQ + j + 1)
                high(block(B_MQ + j + 4))

            def stage(kind, j, hd, c, p):
                apart(act, j)
                wait(act, s_done, j * 4)
                if kind == "mem":
                    act.wait_ge(ev, E_MQ + hd + 1)
                    nc.scalar.activation(qh[:], MQ[:, hd, :], ACT.Copy, scale=128.0 ** -0.5)
                    nc.scalar.activation(kh[:, 0:M], mk[:, hd, :], ACT.Copy).then_inc(st_hi, 1)
                elif kind == "mla":
                    nc.scalar.activation(qh[0:QK_MLA, :], rows(Q, 0, QK_MLA, hd), ACT.Copy,
                                         scale=float(QK_MLA) ** -0.5)
                    nc.scalar.activation(kh[0:NOPE, :], rows(Kt, 0, NOPE, hd), ACT.Copy).then_inc(st_hi, 1)
                else:
                    q, k = rows(FQK, 64 * p, 64 * p + 64, c), rows(FQK, 64 * p, 64 * p + 64, c + 4)
                    nc.scalar.activation(qh[0:64, :], q, ACT.Copy, scale=0.125)
                    nc.scalar.activation(kh[64 * p:64 * p + 64, :], k, ACT.Copy).then_inc(st_hi, 1)

            def stage_rest(kind, j, hd, c, p):
                if kind == "fox":
                    if isinstance(j, int) and j == J_FOX:
                        act.wait_ge(f_rows, 16 * 8)
                    q, k = rows(FQK, 64 * p, 64 * p + 64, c), rows(FQK, 64 * p, 64 * p + 64, c + 4)
                    nc.scalar.activation(kh[64 * (1 - p):64 * (1 - p) + 64, :], k, ACT.Copy)
                    nc.scalar.activation(ql[0:64, :], q, ACT.Copy, scale=0.125)
                    nc.scalar.activation(qh[64:68, :], rows(Kt, 64, 68, hd), ACT.Copy)
                    nc.scalar.activation(kl[64:68, :], rows(Kt, 96, 100, hd), ACT.Copy).then_inc(st_f, 1)

            def v_source(kind, hd):
                if kind == "mem":
                    return mv[:, :, hd * P:(hd + 1) * P]
                t = V if kind == "mla" else FV
                if isinstance(hd, int):
                    return t[:, :, hd * DV:(hd + 1) * DV]
                return t[:, :, bass.ds(hd * DV, DV)]

            def exponentials(kind, j, p, qt):
                nk = M if kind == "mem" else P * (qt + 1)
                off = M * qt if kind == "mem" else P * qt * (qt + 1) // 2
                act.wait_ge(mx_done, j * 4 + qt + 1)
                nc.scalar.activation(prob[p][:, off:off + nk], ps[:, qt % 2, 0:nk], ACT.Exp,
                                     bias=nmax[:, 4 * p + qt:4 * p + qt + 1],
                                     accum_out=rsum[:, 4 * p + qt:4 * p + qt + 1]).then_inc(ex_done, 1)

            def head(kind, J, hd, pair, p, more, nxt, fill, after):
                j = J(0)
                src = v_source(kind, hd)
                nc.scalar.activation(v_parts(kind)[0], src, ACT.Copy).then_inc(sv_hi, 1)

                def probs_hi(kb):
                    w = S if kind == "mem" else S - P * kb
                    off = PT_OFF[kind != "mem"][kb]
                    act.wait_ge(pt_done, pt_first(j) + kb + 1)
                    nc.scalar.activation(pthi[:, off:off + w], ps[:, 2 + kb % 2, 0:w],
                                         ACT.Copy).then_inc(ph_done, 1)

                probs_hi(0)
                probs_hi(1)
                after(-1)
                for qt in range(NT):
                    if qt >= 2 and kind != "mem":
                        probs_hi(qt)
                    if qt == NT - 1 and nxt is not None:
                        stage(*nxt)
                    if more:
                        exponentials(kind, J(1), 1 - p, qt)
                    after(qt)
                if nxt is not None:
                    stage_rest(*nxt)
                fill()
                apart(act, j)
                act.wait_ge(pv_done, j + 1)
                if kind == "mem":
                    nc.scalar.activation(MQ[:, hd, :], ps[:, 4 + p, :], ACT.Copy).then_inc(o_done, 1)
                else:
                    t = Q if kind == "mla" else FQK
                    nc.scalar.activation(rows(t, 64 * p, 64 * p + 64, pair), ps[64:128, 4 + p, :],
                                         ACT.Copy).then_inc(oc_done, 1)

            memory_query(0)
            stage("mem", 0, 0, 0, 0)
            for c, width in enumerate((QL, KVL)):
                act.wait_ge(ss_done, c + 1)
                nc.scalar.activation(rms[:, c, :], ps[:, 2 + c, :], ACT.Sqrt, scale=1.0 / width,
                                     bias=cst[:, 3:4]).then_inc(rm_sd, 1)
            memory_query(1)
            for qt in range(2):
                exponentials("mem", 0, 0, qt)
            memory_query(2)
            for qt in range(2, NT):
                exponentials("mem", 0, 0, qt)
            stage("mem", 1, 1, 0, 1)
            memory_query(3)

            def second_chunk(hd):
                n = B_FQK + 2 * hd + 1
                evac(FQK[:, 2 * hd + 1, :], ps[:, 7, :], w_used, n + 1)
                high(block(n + 4))

            for hd in range(MEM_HEADS):
                n = B_FQK + 2 * hd

                def fill_a():
                    evac(FQK[:, 2 * hd, :], ps[:, 6, :], w_used, n + 1)
                    high(block(n + 4))

                def after(qt):
                    if hd and qt == -1:
                        second_chunk(hd - 1)
                    for c in {2: ((0, 1), (2,), (3,), (4,))}.get(hd, ((),) * NT)[qt] if qt >= 0 else ():
                        act.wait_ge(cn, c + 1)
                        dst = cqhi[:, c, :] if c < KQ else ckhi[:, c - KQ, :]
                        nc.scalar.activation(dst, craw[:, c, :], ACT.Copy).then_inc(cn_hi, 1)
                nxt = ("mem", hd + 2, hd + 2, 0, hd % 2) if hd + 2 < MEM_HEADS else None
                head("mem", lambda d: hd + d, hd, None, hd % 2, hd + 1 < MEM_HEADS, nxt, fill_a, after)
            second_chunk(MEM_HEADS - 1)

            def split_hi(src, br, c):
                act.wait_ge(o_done, (MEM_HEADS, J_FOX, J_END)[br])
                if br:
                    act.wait_ge(w_used, B_MG + 16 * br)
                nc.scalar.activation(ohi[:, c, :], src[:, c, :], ACT.Copy).then_inc(os_hi, 1)

            act.wait_ge(cn_lo, KQ + KKV)
            for hd in range(HEADS):
                evac(Q[0:QK_MLA, hd, :], ps[0:QK_MLA, hd % 4, :],
                     *((pj, hd + 1) if hd < 7 else (w_used, B_UQ + KQ)))
            for n in range(B_UQ, B_UQ + KQ):
                high(block(n + 4))
            nc.scalar.activation(kh[64:96, :], kf[64:96, :], ACT.Copy).then_inc(kr, 1)
            for n in (B_FV, B_FV + 1):
                high(block(n + 4))
            for c in range(4):
                split_hi(MQ, 0, c)
            for hd in range(HEADS):
                evac(Kt[0:NOPE, hd, :], ps[0:NOPE, hd % 4, :], pj, HEADS + hd)
            for t in range(NT):
                evac(V[:, t, :], ps[:, t, :], *((pj, 2 * HEADS + t) if t < 3 else (w_used, B_UKV + KKV)))
            act.wait_ge(rp, 12)
            act.wait_ge(ev, E_V + NT)
            stage("mla", J_MLA, 0, 0, 0)
            for n in (B_UKV, B_UKV + 1, B_FV2):
                high(block(n + 4))
            for qt in range(NT):
                exponentials("mla", J_MLA, 0, qt)
            stage("mla", J_MLA + 1, 1, 0, 1)

            def fox_values(t):
                evac(FV[:, t, :], ps[:, 4 + t, :], w_used, B_FV2 + 2)
            fox_values(2)
            fox_values(0)
            high(block(B_FV2 + 5))
            act.wait_ge(kr, 2)

            def gate(br, n, d, g):
                apart(act, g)
                act.wait_ge(w_used, n + 1)
                wait(act, mg_done, g)
                bank = 6
                bcol = (2, 0, 1)[br] * 8
                b_ap = bg[:, bcol + d:bcol + d + 1] if isinstance(d, int) else bg[:, bass.ds(d + bcol, 1)]
                nc.scalar.activation(sig[:], ps[:, bank, :], ACT.Tanh, scale=0.5, bias=b_ap).then_inc(sg_done, 1)

            def branch_heads(kind, br, j0):
                def body(i, last=False):
                    for p in range(2):
                        hd = i * 2 + p
                        prev = before(br, i, p)

                        def after(qt):
                            if prev is not None and qt == -1:
                                n, _, b, d, g = prev
                                gate(b, n, d, g)
                            if prev is not None and qt == 1:
                                high(block(B_MG + 16 * br + 2 * p + 2, i))
                            if isinstance(i, int) and i == p == 0 and br == 1 and qt >= 2:
                                for c in (2 * qt - 4, 2 * qt - 3):
                                    split_hi(Q, 1, c)
                            if isinstance(i, int) and i == p == br == 0 and qt in (0, 1):
                                fox_values(3 - 2 * qt)

                        def a():
                            if prev is not None:
                                high(block(B_MG + 16 * br + 2 * p + 3, i))
                            elif br == 0:
                                act.wait_ge(ev, E_ALL)
                        if not last:
                            nxt = (kind, i * 2 + (j0 + p + 2), i * 2 + (p + 2), i + 1, p)
                        else:
                            nxt = ("fox", J_FOX + p, p, 0, p) if kind == "mla" else None
                        head(kind, lambda d: i * 2 + (j0 + p + d), hd, i, p, kind == "mla" or not (last and p == 1),
                             nxt, a, after)
                body(0)
                with act.Fori(1, 3) as i:
                    body(i)
                body(3, True)

            branch_heads("mla", 0, J_MLA)
            branch_heads("fox", 1, J_FOX)
            n, _, b, d, g = before(2, 0, 0)
            gate(b, n, d, g)
            high(block(n + 4))
            for c in range(4):
                split_hi(FQK, 2, c)
            high(block(n + 5))

            def merge(i):
                for p in range(2):
                    n, _, _ = block(B_MG + 32 + 2 * p, i)
                    d, g = i * 2 + p, i * 2 + (16 + p)
                    gate(2, n, d, g)
                    high(block(B_MG + 32 + 2 * p + 4, i))
                    high(block(B_MG + 32 + 2 * p + 5, i))
                    apart(act, d)
                    act.wait_ge(mg_done, g + 1)
                    nc.scalar.activation(row(mhi, d), row(merged, d), ACT.Copy, scale=0.5).then_inc(ms_hi, 1)
            with act.Fori(0, 3) as i:
                merge(i)
            merge(3)
            for k in range(4):
                high(block(B_OUT + k + 4))
            TG2 = TG1 + NT
            two_tiles(1, TG2, B_UP2)
            turned_hi(TG2 + 2, 2)
            sd(7)
            turned_hi(TG2 + 3, 3)
            body = up(B_UP2, NF)
            with act.Fori(0, NF // 2 - 1) as i:
                body(i)
            for f in range(RING):
                hidden_hi(f, f, NF)
            body(NF // 2 - 1)
            with act.Fori(0, 4) as i:
                for j in range(RING):
                    n, _, _ = block(B_DN2 + j, i)
                    hidden_hi(i * RING + (j + RING), j, NF, after=n + 1)
                    high(block(B_DN2 + j + RING, i))
            for f in range(16, 18):
                hidden_hi(f + RING, f % RING, NF, after=B_DN2 + f + 1)
                high(block(B_DN2 + f + RING))
            for q in range(2 * NT, 3 * NT):
                sd(q)

        @blk.vector
        def _(dve):
            def turned_lo(g, t):
                dve.wait_ge(t_hi, g + 1)
                nc.vector.tensor_tensor(xlo[:, :, t * P:(t + 1) * P],
                                        ps[:, 2 * t:2 * t + 2, :].rearrange("p a (k m) -> p (a k) m", m=P),
                                        xhi[:, :, t * P:(t + 1) * P].bitcast(F32), ALU.subtract).then_inc(t_lo, 1)

            def norm(q):
                t = q % NT
                r = res[:, q % 2, :]
                yv = ps[:, 2 * t:2 * t + 2, :].rearrange("p a n -> p (a n)")
                if t < NT - 1:
                    dve.wait_ge(y_done, (NT - 1) * (q // NT) + t + 1)
                else:
                    dve.wait_ge(w_used, (B_MK, B_UP2, B_END)[q // NT])
                dve.wait_ge(x_in[t], 32 if q >= NT else 16)
                dve.wait_ge(g_in, 32 * (q // NT + 1))
                wait(dve, lnc, 6 * q)
                wait(dve, x3_done, q - 2 * NT - 1)
                nc.vector.scalar_tensor_tensor(r, X[:, t, :], ALPHA, yv, ALU.mult, ALU.add).then_inc(lnc, 1)
                dve.wait_ge(lnc, 6 * q + 1)
                nc.vector.bn_stats(stats[:, 0, :], r[:, 0:512])
                nc.vector.bn_stats(stats[:, 1, :], r[:, 512:1024]).then_inc(lnc, 1)
                dve.wait_ge(lnc, 6 * q + 2)
                nc.vector.bn_aggr(mvar, moments[:, 0:12]).then_inc(lnc, 1)
                dve.wait_ge(ln_sd, q + 1)
                nc.vector.reciprocal(rstd[:, q % 2:q % 2 + 1], rstd[:, q % 2:q % 2 + 1]).then_inc(lnc, 1)
                if q >= 2 * NT:
                    dve.wait_ge(lnc, 6 * q + 4)
                    nc.vector.tensor_scalar(r, r, mvar[:, 0:1], rstd[:, q % 2:q % 2 + 1], ALU.subtract,
                                            ALU.mult).then_inc(lnc, 2)
                    return
                nc.vector.scalar_tensor_tensor(r, r, mvar[:, 0:1], lng[:], ALU.subtract, ALU.mult).then_inc(lnc, 1)
                dve.wait_ge(lnc, 6 * q + 5)
                nc.vector.scalar_tensor_tensor(X[:, t, :], r, rstd[:, q % 2:q % 2 + 1], lnb[:], ALU.mult,
                                               ALU.add).then_inc(lnc, 1)

            def up(b0, h0):
                def body(i):
                    for p in range(2):
                        nb, _, _ = block(b0 + 2 * p + 1, i)
                        f = i * 2 + p
                        dve.wait_ge(sl_done, f + h0 + 1)
                        dve.wait_ge(w_used, nb + 1)
                        nc.vector.scalar_tensor_tensor(row(h, f), stmp[:, p, :], 0.5, ps[:, 2 * p + 1, :],
                                                       ALU.mult, ALU.mult).then_inc(h_done, 1)
                return body

            def hidden_lo(f, slot, h0):
                dve.wait_ge(hs_hi, f + h0 + 1)
                nc.vector.tensor_tensor(hlo[:, slot, :], row(h, f), hhi[:, slot, :].bitcast(F32),
                                        ALU.subtract).then_inc(hs_lo, 1)

            def ffn(b0, b1, h0, start):
                body = up(b0, h0)
                with dve.Fori(start, NF // 2 - 1) as i:
                    body(i)
                for f in range(RING):
                    hidden_lo(f, f, h0)
                body(NF // 2 - 1)
                with dve.Fori(0, 4) as i:
                    for j in range(RING):
                        hidden_lo(i * RING + (j + RING), j, h0)
                for f in range(20, NF):
                    hidden_lo(f, f % RING, h0)

            for t in range(NT):
                turned_lo(t, t)
            up(B_UP1, 0)(0)
            for kb in range(2):
                dve.wait_ge(t_hi, NT + kb + 1)
                nc.vector.tensor_tensor(mTlo[:, :, kb * P:(kb + 1) * P],
                                        ps[:, 4 + 2 * kb:6 + 2 * kb, :].rearrange("p a (k m) -> p (a k) m", m=P),
                                        mThi[:, :, kb * P:(kb + 1) * P].bitcast(F32), ALU.subtract).then_inc(t_lo, 1)
            ffn(B_UP1, B_DN1, 0, 1)
            TG1 = NT + 2
            def layer_norm(L, g):
                norm(NT * L); norm(NT * L + 1); turned_lo(g, 0); turned_lo(g + 1, 1)
                norm(NT * L + 2); norm(NT * L + 3); turned_lo(g + 2, 2); turned_lo(g + 3, 3)

            layer_norm(0, TG1)
            dve.wait_ge(sp_out, 16 * NT)
            dve.wait_ge(k_in, 16 * 5)
            R = slice(64, 96)
            two_pi = 2.0 * np.pi
            parts, rest = [], two_pi
            for bits in (5, 13, 21):
                c = float(np.round(rest * 2.0 ** bits) / 2.0 ** bits)
                parts.append(c)
                rest -= c
            parts.append(float(np.float32(rest)))
            magic = float(1.5 * 2 ** 23)
            nc.vector.tensor_scalar(tabs[R, 0, :], pos[R, :], cst[R, 0:1], None, ALU.mult).then_inc(tb_v, 1)
            dve.wait_ge(tb_v, 1)
            nc.vector.tensor_scalar(tabs[R, 1, :], tabs[R, 0, :], 1.0 / two_pi, magic, ALU.mult, ALU.add).then_inc(tb_v, 1)
            dve.wait_ge(tb_v, 2)
            nc.vector.tensor_scalar(tabs[R, 1, :], tabs[R, 1, :], magic, None, ALU.subtract).then_inc(tb_v, 1)
            for n, c in enumerate(parts):
                dve.wait_ge(tb_v, 3 + n)
                nc.vector.scalar_tensor_tensor(tabs[R, 0, :], tabs[R, 1, :], -c, tabs[R, 0, :], ALU.mult,
                                               ALU.add).then_inc(tb_v, 1)
            dve.wait_ge(tb_v, 7)
            nc.vector.tensor_scalar(tabs[R, 0, :], tabs[R, 0, :], 3.1415925, -3.1415925, ALU.min, ALU.max).then_inc(tb_v, 1)
            dve.wait_ge(h_done, NF)
            for c in range(KQ + KKV):
                dve.wait_ge(ev, E_C + c + 1)
                nc.vector.tensor_tensor(csq[:, c, :], craw[:, c, :], craw[:, c, :], ALU.mult).then_inc(sq_done, 1)
            for n, (a, b) in enumerate(((0, 1), (3, 4), (0, 2))):
                dve.wait_ge(sq_done, KQ + KKV + (n if n == 2 else 0))
                nc.vector.tensor_tensor(csq[:, a, :], csq[:, a, :], csq[:, b, :], ALU.add).then_inc(sq_done, 1)
            swap = [(k + ROPE // 2) % ROPE for k in range(ROPE)]

            def rotate(v, t, sin, cos, before):
                wait(dve, rp, before)
                nc.vector.stream_shuffle(t, v, swap).then_inc(rp, 1)
                dve.wait_ge(rp, before + 1)
                nc.vector.tensor_tensor(t, t, sin, ALU.mult).then_inc(rp, 1)
                nc.vector.tensor_tensor(v, v, cos, ALU.mult).then_inc(rp, 1)
                dve.wait_ge(rp, before + 3)
                nc.vector.tensor_tensor(v, v, t, ALU.add).then_inc(rp, 1)

            dve.wait_ge(tb_s, 3)
            dve.wait_ge(ev, E_KF + 2)
            rotate(kf[R, :], rtmp[R, :], tabs[R, 2, :], tabs[R, 3, :], 0)
            H8 = slice(0, HEADS)
            nc.vector.memset(tabs[H8, 4, :], 0.0).then_inc(fg_v, 1)
            dve.wait_ge(fg_s, 3)
            nc.vector.scalar_tensor_tensor(tabs[H8, 3, :], kf[H8, :], 0.0, tabs[H8, 2, :], ALU.min,
                                           ALU.subtract).then_inc(fg_v, 1)
            dve.wait_ge(fg_v, 2)
            nc.vector.tensor_tensor_scan(tabs[H8, 0, :], tabs[H8, 4, :], tabs[H8, 3, :], 0.0, ALU.add,
                                         ALU.add).then_inc(fg_v, 1)
            dve.wait_ge(fg_v, 3)
            nc.vector.tensor_copy(tabs[H8, 1, :].bitcast(F32R), tabs[H8, 0, :]).then_inc(fg_v, 1)
            dve.wait_ge(fg_v, 4)
            nc.vector.tensor_tensor(tabs[H8, 2, :], tabs[H8, 0, :], tabs[H8, 1, :], ALU.subtract).then_inc(fg_v, 1)
            nc.vector.tensor_scalar(tabs[H8, 3, :], tabs[H8, 1, :], -1.0, None, ALU.mult)
            dve.wait_ge(fg_v, 5)
            nc.vector.tensor_scalar(tabs[H8, 4, :], tabs[H8, 2, :], -1.0, None, ALU.mult).then_inc(fg_v, 1)
            nc.vector.memset(tabs[H8, 0, :], 1.0).then_inc(fg_v, 1)

            def stage(kind, j, hd, c, p):
                dve.wait_ge(st_hi, j + 1)

                def low(dst, src, hi, scale=None):
                    if scale is None:
                        return nc.vector.tensor_tensor(dst, src, hi.bitcast(F32), ALU.subtract)
                    return nc.vector.scalar_tensor_tensor(dst, src, scale, hi.bitcast(F32), ALU.mult, ALU.subtract)
                if kind == "mem":
                    low(ql[:], MQ[:, hd, :], qh[:], 128.0 ** -0.5)
                    low(kl[:, 0:M], mk[:, hd, :], kh[:, 0:M]).then_inc(st_lo, 1)
                elif kind == "mla":
                    low(ql[0:QK_MLA, :], rows(Q, 0, QK_MLA, hd), qh[0:QK_MLA, :], float(QK_MLA) ** -0.5)
                    low(kl[0:NOPE, :], rows(Kt, 0, NOPE, hd), kh[0:NOPE, :]).then_inc(st_lo, 1)
                else:
                    low(ql[64:128, :], rows(FQK, 64 * p, 64 * p + 64, c), qh[0:64, :], 0.125)
                    low(kl[0:64, :], rows(FQK, 64 * p, 64 * p + 64, c + 4),
                        kh[64 * p:64 * p + 64, :]).then_inc(st_lo, 1)

            def v_source(kind, hd):
                if kind == "mem":
                    return mv[:, :, hd * P:(hd + 1) * P]
                t = V if kind == "mla" else FV
                if isinstance(hd, int):
                    return t[:, :, hd * DV:(hd + 1) * DV]
                return t[:, :, bass.ds(hd * DV, DV)]

            def row_max(kind, j, p, qt):
                nk = M if kind == "mem" else P * (qt + 1)
                dve.wait_ge(s_done, j * 4 + qt + 1)
                nc.vector.tensor_reduce(nmax[:, 4 * p + qt:4 * p + qt + 1], ps[:, qt % 2, 0:nk], AX.X, ALU.max,
                                        negate=True).then_inc(mx_done, 1)

            def normalise(kind, j, p, qt):
                nk = M if kind == "mem" else P * (qt + 1)
                off = M * qt if kind == "mem" else P * qt * (qt + 1) // 2
                col = slice(4 * p + qt, 4 * p + qt + 1)
                dve.wait_ge(ex_done, j * 4 + qt + 1)
                nc.vector.reciprocal(rinv[:, col], rsum[:, col]).then_inc(rc_done, 1)
                dve.wait_ge(rc_done, j * 4 + qt + 1)
                nc.vector.tensor_scalar(prob[p][:, off:off + nk], prob[p][:, off:off + nk], rinv[:, col], None,
                                        ALU.mult).then_inc(pn_done, 1)

            def first_softmax(kind, j):
                for qt in range(NT):
                    row_max(kind, j, 0, qt)
                    if qt:
                        normalise(kind, j, 0, qt - 1)
                normalise(kind, j, 0, NT - 1)

            def head(kind, J, hd, pair, p, more, nxt, fill=None, between=None):
                j = J(0)
                src = v_source(kind, hd)
                dve.wait_ge(sv_hi, j + 1)
                high, low = v_parts(kind)
                nc.vector.tensor_tensor(low, src, high.bitcast(F32), ALU.subtract)

                def probs_lo(kb):
                    w = S if kind == "mem" else S - P * kb
                    off = PT_OFF[kind != "mem"][kb]
                    dve.wait_ge(ph_done, pt_first(j) + kb + 1)
                    nc.vector.tensor_tensor(ptlo[:, off:off + w], ps[:, 2 + kb % 2, 0:w],
                                            pthi[:, off:off + w].bitcast(F32), ALU.subtract).then_inc(pl_done, 1)

                probs_lo(0)
                probs_lo(1)
                for qt in range(NT):
                    if qt >= 2 and kind != "mem":
                        probs_lo(qt)
                    if more:
                        row_max(kind, J(1), 1 - p, qt)
                        if qt:
                            normalise(kind, J(1), 1 - p, qt - 1)
                    if between is not None:
                        between(qt)
                if nxt is not None:
                    stage(*nxt)
                if more:
                    normalise(kind, J(1), 1 - p, NT - 1)
                if fill is not None:
                    fill()
                if kind != "mem":
                    o = rows(Q if kind == "mla" else FQK, 64 * p, 64 * p + 64, pair)
                    apart(dve, j)
                    dve.wait_ge(oc_done, J(1 - J_MLA))
                    nc.vector.tensor_tensor(o, ps[0:64, 4 + p, :], o, ALU.add).then_inc(o_done, 1)

            dve.wait_ge(ev, E_MQ + 1)
            stage("mem", 0, 0, 0, 0)
            first_softmax("mem", 0)
            stage("mem", 1, 1, 0, 1)
            for hd in range(MEM_HEADS):
                def between(qt):
                    if hd < 2:
                        cols = slice(qt * P, (qt + 1) * P)
                        dve.wait_ge(rm_sd, hd + 1)
                        nc.vector.reciprocal(rms[:, hd, cols], rms[:, hd, cols]).then_inc(rm_r, 1)
                    for c in (((), (), (), ()), ((0,), (1,), (2,), ()), ((3,), (4,), (), ()), ((), (), (), ()))[hd][qt]:
                        dve.wait_ge(rm_r, NT * hd)
                        nc.vector.scalar_tensor_tensor(craw[:, c, :], craw[:, c, :], gq[:, c:c + 1],
                                                       rms[:, 0 if c < KQ else 1, :], ALU.mult,
                                                       ALU.mult).then_inc(cn, 1)
                    for c in (((), (), (), ()), ((), (), (), ()), ((), (0,), (1,), (2,)), ((3,), (4,), (), ()))[hd][qt]:
                        hi, lo = (cqhi[:, c, :], cqlo[:, c, :]) if c < KQ else (ckhi[:, c - KQ, :], cklo[:, c - KQ, :])
                        dve.wait_ge(cn_hi, c + 1)
                        nc.vector.tensor_tensor(lo, craw[:, c, :], hi.bitcast(F32), ALU.subtract).then_inc(cn_lo, 1)
                nxt = ("mem", hd + 2, hd + 2, 0, hd % 2) if hd + 2 < MEM_HEADS else None
                head("mem", lambda d: hd + d, hd, None, hd % 2, hd + 1 < MEM_HEADS, nxt, between=between)

            def split_lo(src, br, c):
                dve.wait_ge(os_hi, 4 * br + c + 1)
                nc.vector.tensor_tensor(olo[:, c, :], src[:, c, :], ohi[:, c, :].bitcast(F32),
                                        ALU.subtract).then_inc(os_lo, 1)

            dve.wait_ge(w_used, B_UQ + KQ)
            for half in range(2):
                hs = slice(4 * half, 4 * half + 4)
                dve.wait_ge(ev, E_UQ + 4 * half + 4)
                rotate(Q[R, hs, :], Kt[R, hs, :], tabs[R, 2:3, :].to_broadcast([ROPE, 4, S]),
                       tabs[R, 3:4, :].to_broadcast([ROPE, 4, S]), 4 + 4 * half)
            dve.wait_ge(kr, 1)
            nc.vector.tensor_tensor(kl[64:96, :], kf[64:96, :], kh[64:96, :].bitcast(F32), ALU.subtract).then_inc(kr, 1)
            for c in range(4):
                split_lo(MQ, 0, c)
            stage("mla", J_MLA, 0, 0, 0)
            first_softmax("mla", J_MLA)
            stage("mla", J_MLA + 1, 1, 0, 1)
            dve.wait_ge(f_rows, 16 * 8)

            def merge(br, n, d, g, ybank):
                dve.wait_ge(sg_done, g + 1)
                dve.wait_ge(w_used, n + 1)
                if br == 0:
                    nc.vector.scalar_tensor_tensor(row(merged, d), sig[:], 1.0, ps[:, ybank, :], ALU.add,
                                                   ALU.mult).then_inc(mg_done, 1)
                else:
                    nc.vector.scalar_tensor_tensor(sig[:], sig[:], 1.0, ps[:, ybank, :], ALU.add, ALU.mult).then_inc(mt_done, 1)
                    dve.wait_ge(mt_done, g - 8 + 1)
                    nc.vector.tensor_tensor(row(merged, d), row(merged, d), sig[:], ALU.add).then_inc(mg_done, 1)

            def merge_before(br, i, p):
                prev = before(br, i, p)
                if prev is not None:
                    n, _, b, d, g = prev
                    merge(b, n + 1, d, g, 7)

            def branch_heads(kind, br, j0):
                def body(i, last=False):
                    for p in range(2):
                        hd = i * 2 + p

                        def fill():
                            merge_before(br, i, p)
                            if br == 1 and isinstance(i, int) and hd == 0:
                                for c in range(4):
                                    split_lo(Q, 1, c)
                        if not last:
                            nxt = (kind, i * 2 + (j0 + p + 2), i * 2 + (p + 2), i + 1, p)
                        else:
                            nxt = ("fox", J_FOX + p, p, 0, p) if kind == "mla" else None
                        head(kind, lambda d: i * 2 + (j0 + p + d), hd, i, p, kind == "mla" or not (last and p == 1),
                             nxt, fill)
                body(0)
                with dve.Fori(1, 3) as i:
                    body(i)
                body(3, True)

            branch_heads("mla", 0, J_MLA)
            branch_heads("fox", 1, J_FOX)
            for c in range(4):
                split_lo(FQK, 2, c)
            merge_before(2, 0, 0)
            with dve.Fori(0, 4) as i:
                for p in range(2):
                    n, _, _ = block(B_MG + 32 + 2 * p + 1, i)
                    d = i * 2 + p
                    merge(2, n, d, i * 2 + (16 + p), (7, 5)[p])
                    dve.wait_ge(ms_hi, d + 1)
                    nc.vector.scalar_tensor_tensor(row(mlo, d), row(merged, d), 0.5, row(mhi, d).bitcast(F32),
                                                   ALU.mult, ALU.subtract).then_inc(ms_lo, 1)
            TG2 = TG1 + NT
            layer_norm(1, TG2)
            ffn(B_UP2, B_DN2, NF, 0)
            for t in range(NT - 1):
                norm(2 * NT + t)
            q = 3 * NT - 1
            halves = [slice(0, 512), slice(512, 1024)]
            dve.wait_ge(x3_done, 2)
            dve.wait_ge(lnc, 6 * q)
            for h2 in range(2):
                if h2 == 0:
                    dve.wait_ge(y_done, 3 * (NT - 1) + 1)
                else:
                    dve.wait_ge(w_used, B_END)
                nc.vector.scalar_tensor_tensor(res[:, 1, halves[h2]], X[:, 3, halves[h2]], ALPHA, ps[:, 6 + h2, :],
                                               ALU.mult, ALU.add).then_inc(fin, 1)
                dve.wait_ge(fin, h2 * 2 + 1)
                nc.vector.bn_stats(stats[:, h2, :], res[:, 1, halves[h2]]).then_inc(fin, 1)
            dve.wait_ge(fin, 4)
            nc.vector.bn_aggr(mvar, moments[:, 0:12]).then_inc(lnc, 3)
            dve.wait_ge(ln_sd, q + 1)
            nc.vector.reciprocal(rstd[:, 1:2], rstd[:, 1:2]).then_inc(lnc, 1)
            for h2 in range(2):
                r = res[:, 1, halves[h2]]
                nc.vector.scalar_tensor_tensor(r, r, mvar[:, 0:1], lng[:, halves[h2]], ALU.subtract,
                                               ALU.mult).then_inc(fin, 1)
                dve.wait_ge(fin, 2 * h2 + 5)
                nc.vector.scalar_tensor_tensor(X[:, 3, halves[h2]], r, rstd[:, 1:2], lnb[:, halves[h2]], ALU.mult,
                                               ALU.add).then_inc(fin, 1)

        @blk.tensor
        def _(pe):
            mm = nc.tensor.matmul

            def wv(t, like, m=P):
                return t[:, like % RING, :].rearrange("p (k m) -> p k m", m=m)

            def three(k):
                return ((0, 0), (0, 1), (1, 0))[k]

            def product(m, like, out_ap, rh, rl, last, cols=slice(0, P)):
                k, (a, b) = m // 3, three(m % 3)
                return mm(out_ap, wv((whi, wlo)[a], like)[:, k, cols], (rh, rl)[b](k), start=m == 0, stop=m == last)

            def feature_block(b, bank, cols=slice(0, P), rh=None, rl=None, width=S):
                n, like, _ = b
                pe.wait_ge(w_lo, n + 1)
                rh = rh or (lambda k: xhi[:, k, :])
                rl = rl or (lambda k: xlo[:, k, :])
                rows_out = cols.stop - cols.start
                for m in range(3 * KD):
                    ins = product(m, like, ps[0:rows_out, bank, 0:width], rh, rl, 3 * KD - 1, cols)
                ins.then_inc(w_used, 1)

            def turn(g, src, bank):
                for k in range(KD):
                    ins = nc.tensor.transpose(ps[:, bank + k // 4, (k % 4) * P:(k % 4 + 1) * P],
                                              src[:, k * P:(k + 1) * P], ident[:])
                ins.then_inc(t_done, 1)

            def token_block(like, t, sh, sl, start, stop, halves=(0, 1)):
                for a, b in ((sh, whi), (sh, wlo), (sl, whi)):
                    for half in halves:
                        ins = mm(ps[:, 2 * t + half, :], a(t), b[:, like % RING, half * 512:(half + 1) * 512],
                                 start=start and a is sh and b is whi, stop=stop and a is sl)
                return ins

            def up(b0, h0):
                def body(i):
                    for p in range(2):
                        f = i * 2 + p
                        wait(pe, h_done, f + h0 - 1)
                        feature_block(block(b0 + 2 * p, i), 2 * p)
                        feature_block(block(b0 + 2 * p + 1, i), 2 * p + 1)
                return body

            def first_up(b0, g, between={}):
                for half in range(2):
                    cols = slice(half * (S // 2), (half + 1) * (S // 2))
                    pe.wait_ge(t_lo, g + 2 * half + 2)
                    for j in range(RING):
                        if half == 0:
                            pe.wait_ge(w_lo, b0 + j + 1)
                        for m in range(3 * KD):
                            ins = product(m, b0 + j, ps[:, j, cols], lambda k: xhi[:, k, cols],
                                          lambda k: xlo[:, k, cols], 3 * KD - 1)
                            if half == 0 and (j, m) in between:
                                turn_tile(1, between[j, m])
                        if half == 1:
                            ins.then_inc(w_used, 1)

            def hidden(slot):
                return (lambda t: hhi[:, slot, t * P:(t + 1) * P]), (lambda t: hlo[:, slot, t * P:(t + 1) * P])

            def turn_tile(L, t):
                pe.wait_ge(lnc, 6 * (L * NT + t + 1))
                turn(NT + 2 + L * NT + t, X[:, t, :], 2 * t)

            def finish(b0, sources, L):
                for t in range(NT):
                    if L == 2 and t == NT - 1:
                        for half in range(2):
                            for c, (sh, sl, _, _) in enumerate(sources):
                                ins = token_block(b0 + c, t, sh, sl, False, c == RING - 1, (half,))
                                if half == 1:
                                    ins.then_inc(w_used, 1)
                            if half == 0:
                                ins.then_inc(y_done, 1)
                        return
                    for c, (sh, sl, ready, count) in enumerate(sources):
                        if t == 0:
                            pe.wait_ge(ready, count)
                            pe.wait_ge(w_lo, b0 + c + 1)
                        ins = token_block(b0 + c, t, sh, sl, False, c == RING - 1)
                        if t == NT - 1:
                            ins.then_inc(w_used, 1)
                        if t < NT - 1 and c == RING - 1:
                            ins.then_inc(y_done, 1)
                        if t + c == 3 and t >= 2 and L < 2:
                            turn_tile(L, t - 2)

            def down(b1, h0, L):
                def one(b, f, slot, first):
                    n, like, _ = b
                    pe.wait_ge(hs_lo, f + h0 + 1)
                    pe.wait_ge(w_lo, n + 1)
                    sh, sl = hidden(slot)
                    order = (2, 3, 0, 1) if first else range(NT)
                    for t in order:
                        if first and t == 0:
                            pe.wait_ge(h_done, h0 + NF)
                        ins = token_block(like, t, sh, sl, first, False)
                    ins.then_inc(w_used, 1)
                for f in range(RING):
                    one(block(b1 + f), f, f, f == 0)
                with pe.Fori(1, 4) as i:
                    for j in range(RING):
                        one(block(b1 + j, i), i * RING + j, j, False)
                for f in (16, 17):
                    one(block(b1 + f), f, f % RING, False)
                finish(b1 + 18, [(*hidden(f % RING), hs_lo, f + h0 + 1) for f in range(18, NF)], L)

            pe.wait_ge(act_c, 2)
            for t in range(NT):
                pe.wait_ge(x_in[t], 16)
                turn(t, X[:, t, :], 2 * t)
            first_up(B_UP1, 0)
            pe.wait_ge(m_in, 16)
            for kb in range(2):
                turn(NT + kb, res[:, kb, :], 4 + 2 * kb)
            with pe.Fori(1, NF // 2) as i:
                up(B_UP1, 0)(i)
            pe.wait_ge(t_lo, NT + 2)
            TG1 = NT + 2
            down(B_DN1, 0, 0)
            for j in range(4):
                if j % 2 == 0:
                    pe.wait_ge(t_lo, TG1 + j // 2 + 1)
                feature_block(block(B_MK + j), j, rh=lambda k: mThi[:, k, :], rl=lambda k: mTlo[:, k, :], width=M)
                if j == 1:
                    turn_tile(0, 2)
            pe.wait_ge(ev, E_MK + 2)
            for j in range(4):
                n, like, _ = block(B_MV + j)
                pe.wait_ge(w_lo, n + 1)
                for k in range(2):
                    for kb in range(2):
                        for a, b in ((0, 0), (0, 1), (1, 0)):
                            ins = mm(ps[:, kb, :], (mThi, mTlo)[a][:, 2 * j + k, kb * P:(kb + 1) * P],
                                     wv((whi, wlo)[b], like, 512)[:, k, :], start=j == 0 and k == 0 and a + b == 0,
                                     stop=j == 3 and k == 1 and a == 1)
                ins.then_inc(w_used, 1)
                if j == 1:
                    turn_tile(0, 3)
            pe.wait_ge(t_lo, TG1 + 4)
            for j in range(KQ + KKV):
                pe.wait_ge(ev, E_MK + min(j + 3, 4))
                feature_block(block(B_C + j), j + 2)
            feature_block(block(B_KF), 7, cols=slice(64, 104))

            def memory_query(j):
                pe.wait_ge(ev, (E_C + 3, E_C + 4, E_C + 5, E_KF + 2)[j])
                feature_block(block(B_MQ + j), 4 + j)
            memory_query(0)
            pe.wait_ge(ev, E_C + 2)
            pe.wait_ge(sq_done, KQ + KKV + 3)
            for c, k in enumerate((0, KQ)):
                mm(ps[:, 2 + c, :], ones[:], csq[:, k, :], start=True, stop=True).then_inc(ss_done, 1)
            memory_query(1)

            def logits(kind, j, qt):
                kq = {"mem": P, "mla": QK_MLA, "fox": 68}[kind]
                causal = kind != "mem"
                nk = P * (qt + 1) if causal else M
                if qt == 0:
                    pe.wait_ge(st_lo, j + 1)
                    if kind == "fox":
                        pe.wait_ge(st_f, j - (J_FOX - 1))
                if qt >= 2:
                    pe.wait_ge(ex_done, j * 4 + (qt - 1))
                o = ps[:, qt % 2, 0:nk]
                q_cols = slice(qt * P, (qt + 1) * P)
                if kind == "fox":
                    mm(o, ql[:, q_cols], kh[:, 0:nk], start=True, stop=False)
                    mm(o, qh[0:kq, q_cols], kl[0:kq, 0:nk], start=False, stop=False)
                else:
                    mm(o, qh[0:kq, q_cols], kh[0:kq, 0:nk], start=True, stop=False)
                    mm(o, qh[0:kq, q_cols], kl[0:kq, 0:nk], start=False, stop=False)
                    ins = mm(o, ql[0:kq, q_cols], kh[0:kq, 0:nk], start=False, stop=not causal)
                if causal:
                    ins = mm(ps[:, qt % 2, nk - P:nk], identR[:], maskR[:], start=False, stop=True)
                ins.then_inc(s_done, 1)

            def head(kind, J, p, nxt, fill, cuts):
                j = J(0)
                causal = kind != "mem"
                step = [0]

                def filler():
                    fill(cuts[step[0]], cuts[step[0] + 1])
                    step[0] += 1

                def next_logits(qt):
                    if nxt is not None:
                        logits(nxt, J(1), qt)

                def turn_probs(kb):
                    if kb == 0:
                        pe.wait_ge(pn_done, j * 4 + NT)
                    first = kb if causal else 0
                    for qt in range(first, NT):
                        off = P * qt * (qt + 1) // 2 if causal else M * qt
                        ins = nc.tensor.transpose(ps[:, 2 + kb % 2, (qt - first) * P:(qt - first + 1) * P],
                                                  prob[p][:, off + kb * P:off + (kb + 1) * P], ident[:])
                    ins.then_inc(pt_done, 1)

                def values(kb):
                    w = S - P * kb if causal else S
                    off = PT_OFF[causal][kb]
                    nb = 4 if causal else 2
                    pe.wait_ge(pl_done, pt_first(j) + kb + 1)
                    if kb == 0:
                        if isinstance(j, int) and J_MLA <= j < J_MLA + 2:
                            pe.wait_ge(ev, E_FV + 2 * (j - J_MLA) + 2)
                    last = kb == nb - 1
                    hi, lo = pthi[:, off:off + w], ptlo[:, off:off + w]
                    if causal:
                        v = vhl[:].rearrange("p (k m) -> p k m", k=4)[:, kb, :]
                        if last:
                            mm(ps[0:DV, 4 + p, S - w:S], v[:, 0:DV], lo, start=False, stop=False)
                        ins = mm(ps[:, 4 + p, S - w:S], v, hi, start=kb == 0, stop=last)
                        if not last:
                            mm(ps[0:DV, 4 + p, S - w:S], v[:, 0:DV], lo, start=False, stop=False)
                    else:
                        vh, vl = (v[:, kb, :] for v in v_parts(kind))
                        mm(ps[:, 4 + p, :], vh, hi, start=kb == 0, stop=False)
                        mm(ps[:, 4 + p, :], vh, lo, start=False, stop=False)
                        ins = mm(ps[:, 4 + p, :], vl, hi, start=False, stop=last)
                    if kb == nb - 1:
                        ins.then_inc(pv_done, 1)

                turn_probs(0)
                turn_probs(1)
                filler()
                next_logits(0)
                next_logits(1)
                values(0)
                filler()
                if causal:
                    turn_probs(2)
                next_logits(2)
                values(1)
                if causal:
                    turn_probs(3)
                filler()
                next_logits(3)
                filler()
                if causal:
                    values(2)
                filler()
                if causal:
                    values(3)
                filler()

            pe.wait_ge(ev, E_MV + 2)
            logits("mem", 0, 0)
            logits("mem", 0, 1)
            memory_query(2)
            logits("mem", 0, 2)
            logits("mem", 0, 3)
            memory_query(3)
            pe.wait_ge(rm_sd, 2)
            for hd in range(MEM_HEADS):
                def fill(lo, hi):
                    for m in range(lo, hi):
                        k, m1 = m // 24, m % 24
                        n = B_FQK + 2 * hd + k
                        if m1 == 0:
                            pe.wait_ge(w_lo, n + 1)
                            pe.wait_ge(ev, (E_MQ + 3 + k) if hd == 0 else E_FQK + 2 * (hd - 1) + k + 1)
                        ins = product(m1, n, ps[:, 6 + k, :], lambda k: xhi[:, k, :], lambda k: xlo[:, k, :], 23)
                        if m1 == 23:
                            ins.then_inc(w_used, 1)
                head("mem", lambda d: hd + d, hd % 2, "mem" if hd + 1 < MEM_HEADS else None, fill,
                     [0, 8, 16, 24, 32, 40, 48])
            pe.wait_ge(pl_done, 2 * MEM_HEADS)
            pe.wait_ge(ex_done, 4 * MEM_HEADS)
            pe.wait_ge(cn_lo, KQ)
            for k in range(KQ):
                pe.wait_ge(w_lo, B_UQ + k + 1)
            for hd in range(HEADS):
                if hd >= 4:
                    pe.wait_ge(ev, E_UQ + hd - 3)
                for k in range(KQ):
                    for a, b in ((0, 0), (0, 1), (1, 0)):
                        ins = mm(ps[0:QK_MLA, hd % 4, :],
                                 (whi, wlo)[a][:, (B_UQ + k) % RING, hd * QK_MLA:(hd + 1) * QK_MLA],
                                 (cqhi, cqlo)[b][:, k, :], start=k == 0 and a + b == 0, stop=k == KQ - 1 and a == 1)
                        if hd == HEADS - 1 and a == 1 and k < KQ - 1:
                            ins.then_inc(w_used, 1)
                if hd < HEADS - 1:
                    ins.then_inc(pj, 1)
            ins.then_inc(w_used, 1)

            def fox_values(j, tiles=range(NT)):
                n = B_FV + j if j < 2 else B_FV2 + j - 2
                pe.wait_ge(w_lo, n + 1)
                for t in tiles:
                    for k in range(2):
                        for a, b in ((0, 0), (0, 1), (1, 0)):
                            ins = mm(ps[:, 4 + t, :], (xhi, xlo)[a][:, 2 * j + k, t * P:(t + 1) * P],
                                     wv((whi, wlo)[b], n, 512)[:, k, :], start=j == 0 and k == 0 and a + b == 0,
                                     stop=j == 3 and k == 1 and a == 1)
                if tiles[-1] == NT - 1:
                    ins.then_inc(w_used, 1)

            pe.wait_ge(o_done, MEM_HEADS)
            pe.wait_ge(ev, E_FQK + 8)
            fox_values(0)
            fox_values(1)
            pe.wait_ge(cn_lo, KQ + KKV)
            for k in range(KKV):
                pe.wait_ge(w_lo, B_UKV + k + 1)
            for hd in range(HEADS):
                pe.wait_ge(ev, E_UQ + hd + 5)
                for k in range(KKV):
                    for a, b in ((0, 0), (0, 1), (1, 0)):
                        ins = mm(ps[0:NOPE, hd % 4, :],
                                 wv((whi, wlo)[a], B_UKV + k)[:, hd, 0:NOPE],
                                 (ckhi, cklo)[b][:, k, :], start=k == 0 and a + b == 0, stop=k == KKV - 1 and a == 1)
                ins.then_inc(pj, 1)
            for t in range(NT):
                pe.wait_ge(ev, E_K + 5 + t)
                for k in range(KKV):
                    for a, b in ((0, 0), (0, 1), (1, 0)):
                        ins = mm(ps[:, t, :], (ckhi, cklo)[a][:, k, t * P:(t + 1) * P],
                                 wv((whi, wlo)[b], B_UKV + k)[:, :, NOPE:P],
                                 start=k == 0 and a + b == 0, stop=k == KKV - 1 and a == 1)
                        if t == NT - 1 and k == 0 and a == 1:
                            ins.then_inc(w_used, 1)
                if t < NT - 1:
                    ins.then_inc(pj, 1)
            ins.then_inc(w_used, 1)
            fox_values(2)
            pe.wait_ge(ev, E_V + NT)
            pe.wait_ge(kr, 2)
            logits("mla", J_MLA, 0)
            logits("mla", J_MLA, 1)
            fox_values(3, (0,))
            logits("mla", J_MLA, 2)
            fox_values(3, (1,))
            logits("mla", J_MLA, 3)
            fox_values(3, (2, 3))

            def gate_part(m, n, like, g):
                if m == 0:
                    pe.wait_ge(w_lo, n + 1)
                    wait(pe, sg_done, g)
                    if isinstance(g, int) and g == 0:
                        pe.wait_ge(ev, E_FV + 1)
                ins = product(m, like, ps[:, 6, :], lambda k: xhi[:, k, :], lambda k: xlo[:, k, :], 23)
                if m == 23:
                    ins.then_inc(w_used, 1)

            def branch_part(m, n, like, br, g, bank=7):
                if m == 0:
                    pe.wait_ge(w_lo, n + 1)
                    pe.wait_ge(os_lo, 4 * br + 4)
                    wait(pe, mg_done, g)
                    if isinstance(g, int) and g == 0:
                        pe.wait_ge(ev, E_FV + 3)
                ins = product(m, like, ps[:, bank, :], lambda k: ohi[:, k, :], lambda k: olo[:, k, :], 11)
                if m == 11:
                    ins.then_inc(w_used, 1)

            cuts = [0, 5, 10, 15, 22, 29, 36]
            for kind, br, j0 in (("mla", 0, J_MLA), ("fox", 1, J_FOX)):
                def two_heads(i, last=False):
                    for p in range(2):
                        prev = before(br, i, p)
                        ng, lg, _ = block(B_MG + 16 * br + 2 * p, i)

                        def fill(lo, hi):
                            for m in range(lo, hi):
                                if m >= 12:
                                    gate_part(m - 12, ng, lg, i * 2 + (8 * br + p))
                                elif prev is not None:
                                    n, like, b, _, g = prev
                                    branch_part(m, n + 1, like + 1, b, g)
                        nxt = kind if not (last and p == 1) else ("fox" if kind == "mla" else None)
                        head(kind, lambda d: i * 2 + (j0 + p + d), p, nxt, fill,
                             cuts if prev is not None else [12, 16, 20, 24, 28, 32, 36])
                two_heads(0)
                with pe.Fori(1, 3) as i:
                    two_heads(i)
                two_heads(3, True)
            n, like, b, _, g = before(2, 0, 0)
            for m in range(12):
                branch_part(m, n + 1, like + 1, b, g)
            with pe.Fori(0, 4) as i:
                for p in range(2):
                    ng, lg, _ = block(B_MG + 32 + 2 * p, i)
                    g = i * 2 + (16 + p)
                    for m in range(24):
                        gate_part(m, ng, lg, g)
                    for m in range(12):
                        branch_part(m, ng + 1, lg + 1, 2, g, (7, 5)[p])
            def chunk(k):
                return (lambda t: mhi[:, k, t * P:(t + 1) * P]), (lambda t: mlo[:, k, t * P:(t + 1) * P])
            for k in range(4):
                pe.wait_ge(ms_lo, k + 1)
                pe.wait_ge(w_lo, B_OUT + k + 1)
                for t in range(NT):
                    if k == 0 and t == 2:
                        pe.wait_ge(sg_done, 24)
                        pe.wait_ge(mg_done, 24)
                    ins = token_block(B_OUT + k, t, *chunk(k), k == 0, False)
                ins.then_inc(w_used, 1)
            TG2 = TG1 + NT
            finish(B_OUT + 4, [(*chunk(k), ms_lo, k + 1) for k in range(4, KD)], 1)
            first_up(B_UP2, TG2, between={(1, 23): 2, (3, 17): 3})
            with pe.Fori(1, NF // 2) as i:
                up(B_UP2, NF)(i)
            down(B_DN2, NF, 2)


_INS = ["x", "mem", "positions", "ln1_g", "ln1_b", "ffn1_w_in", "ffn1_w_down", "w_in", "b_gate", "mla_q_norm",
        "mla_w_uq", "mla_kv_norm", "mla_w_ukv", "fox_b_f", "mem_w_kv", "w_br_mla", "w_br_fox", "w_br_mem", "w_out",
        "ln2_g", "ln2_b", "ffn2_w_in", "ffn2_w_down", "ln3_g", "ln3_b"]


def kernel(**inputs):
    import numpy as _np
    import concourse.bacc as _bacc
    from concourse import mybir as _mybir
    from concourse.bass_utils import run_bass_kernel_spmd as _run

    nc = _bacc.Bacc("TRN2", target_bir_lowering=False, num_devices=1)
    arrays, args = {}, []
    for name in _INS:
        a = _np.ascontiguousarray(inputs[name])
        a = a.reshape(a.shape[1:])
        arrays[f"in_{name}_dram"] = a
        args.append(nc.dram_tensor(f"in_{name}_dram", a.shape, _mybir.dt.from_np(a.dtype), kind="ExternalInput").ap())
    arrays["in_consts_dram"] = shape_constants()
    args.append(nc.dram_tensor("in_consts_dram", (P, 8), _mybir.dt.float32, kind="ExternalInput").ap())
    args.append(nc.dram_tensor("out_0_dram", (S, D), _mybir.dt.float32, kind="ExternalOutput").ap())
    layer_program(nc, *args)
    r = _run(nc, [arrays], core_ids=[0])
    return r.results[0]["out_0_dram"].reshape(1, S, D)
```
